# Optimizing a Trainium2 kernel written in Bass

```python
import jax, jax.numpy as jnp
from jax import lax
import numpy as np

D_MODEL = 1024
BATCH = 1
SEQ = 1024
DEPTH = 1

MEM_LEN = 256
RW_HEADS = 8
RW_HEAD_DIM = 64
RW_WIDTH = RW_HEADS * RW_HEAD_DIM
DECAY_LORA = 64
AAA_LORA = 64
GATE_LORA = 128
RW_COLS = 3 * RW_WIDTH + DECAY_LORA + AAA_LORA + GATE_LORA
GN_EPS = 64e-5
ML_HEADS = 4
ML_HEAD_DIM = 128
ML_WIDTH = ML_HEADS * ML_HEAD_DIM
ML_CONV = 4
ML_CHUNK = 64
ML_COLS = 4 * ML_WIDTH + 2 * ML_HEADS
ML_NORM_EPS = 1e-6
IN_COLS = RW_COLS + ML_COLS + 2 * D_MODEL
D_FF = 2816
FFN_HALF = 0.5
XA_HEADS = 4
XA_HEAD_DIM = D_MODEL // XA_HEADS
NORM_EPS = 1e-5

kernel_name = "hybrid_rwkv7_mlstm_macaron_memxattn"

def _split(z, sizes):
    idx = np.cumsum(sizes)[:-1].tolist()
    return jnp.split(z, idx, axis=-1)

def _shift(u, j):
    if j == 0:
        return u
    return jnp.pad(u[:, :-j], ((0, 0), (j, 0), (0, 0)))

def _rmsnorm(x, g):
    xf = x.astype(jnp.float32)
    r = xf * lax.rsqrt(jnp.mean(xf * xf, axis=-1, keepdims=True) + NORM_EPS)
    return (r * g.astype(jnp.float32)).astype(x.dtype)

def _swiglu(h, w_gate, w_up, w_down):
    return (jax.nn.silu(h @ w_gate) * (h @ w_up)) @ w_down

def _causal_conv(u, w, b):
    out = b
    for j in range(ML_CONV):
        out = out + w[j] * _shift(u, j)
    return out

def _rwkv7_scan(r, decay, k, v, kk, kka):
    bsz, _, nh, n = r.shape

    def step(state, xs):
        r_t, w_t, k_t, v_t, kk_t, b_t = xs
        sa = jnp.einsum('bhvk,bhk->bhv', state, -kk_t)
        state = (state * w_t[:, :, None, :] + sa[..., None] * b_t[:, :, None, :]
                 + v_t[..., None] * k_t[:, :, None, :])
        return state, jnp.einsum('bhvk,bhk->bhv', state, r_t)

    xs = tuple(jnp.moveaxis(t, 1, 0) for t in (r, decay, k, v, kk, kka))
    init = jnp.zeros((bsz, nh, n, n), jnp.float32)
    _, y = lax.scan(step, init, xs)
    return jnp.moveaxis(y, 0, 1)

def _mlstm_chunkwise(q, k, v, i_pre, f_pre):
    bsz, seq, nh, dk = q.shape
    dv = v.shape[-1]
    nc, cl = seq // ML_CHUNK, ML_CHUNK

    def chunks(t):
        t = t.astype(jnp.float32).reshape((bsz, nc, cl, nh) + t.shape[3:])
        return jnp.moveaxis(t, 3, 1)

    q = chunks(q) * (dk ** -0.5)
    k, v = chunks(k), chunks(v)
    ig = chunks(i_pre)
    b = jnp.cumsum(jax.nn.log_sigmoid(chunks(f_pre)), axis=-1)
    b_end = b[..., -1]

    log_w_end = b_end[..., None] - b + ig
    m_chunk = jnp.max(log_w_end, axis=-1)
    w_end = jnp.exp(log_w_end - m_chunk[..., None])
    c_chunk = jnp.einsum('bhcl,bhclv,bhclk->bhcvk', w_end, v, k)
    n_chunk = jnp.einsum('bhcl,bhclk->bhck', w_end, k)

    def step(carry, xs):
        c, n, m = carry
        be, mc, cc, nck = xs
        m_new = jnp.maximum(be + m, mc)
        dec = jnp.exp(be + m - m_new)
        sc = jnp.exp(mc - m_new)
        c_new = dec[..., None, None] * c + sc[..., None, None] * cc
        n_new = dec[..., None] * n + sc[..., None] * nck
        return (c_new, n_new, m_new), (c, n, m)

    init = (jnp.zeros((bsz, nh, dv, dk), jnp.float32),
            jnp.zeros((bsz, nh, dk), jnp.float32),
            jnp.zeros((bsz, nh), jnp.float32))
    xs = tuple(jnp.moveaxis(t, 2, 0) for t in (b_end, m_chunk, c_chunk, n_chunk))
    _, (c_prev, n_prev, m_prev) = lax.scan(step, init, xs)
    c_prev = jnp.moveaxis(c_prev, 0, 2)
    n_prev = jnp.moveaxis(n_prev, 0, 2)
    m_prev = jnp.moveaxis(m_prev, 0, 2)

    causal = jnp.tril(jnp.ones((cl, cl), dtype=bool))
    log_d = jnp.where(causal, b[..., :, None] - b[..., None, :] + ig[..., None, :], -jnp.inf)
    log_inter = b + m_prev[..., None]
    m_row = jnp.maximum(log_inter, jnp.max(log_d, axis=-1))
    p = jnp.exp(log_d - m_row[..., None]) * jnp.einsum('bhcsk,bhcrk->bhcsr', q, k)
    w_inter = jnp.exp(log_inter - m_row)
    num = (jnp.einsum('bhcsr,bhcrv->bhcsv', p, v)
           + w_inter[..., None] * jnp.einsum('bhcvk,bhcsk->bhcsv', c_prev, q))
    den = jnp.sum(p, axis=-1) + w_inter * jnp.einsum('bhck,bhcsk->bhcs', n_prev, q)
    h = num / jnp.maximum(jnp.abs(den), jnp.exp(-m_row))[..., None]
    return jnp.moveaxis(h, 1, 3).reshape(bsz, seq, nh, dv)

def _token_mix(h, w_in, rw_mu, rw_w0, rw_w2, rw_a0, rw_a2, rw_g2, rw_k_k, rw_k_a, rw_r_k,
               rw_gn_w, rw_gn_b, ml_conv_w, ml_conv_b, ml_i_b, ml_f_b, ml_norm,
               w_up_rw, w_up_ml, w_out):
    bsz, seq, _ = h.shape
    f32 = jnp.float32
    z = h @ w_in
    z_rw, z_ml, z_gate = _split(z, [RW_COLS, ML_COLS, 2 * D_MODEL])

    z_rw = z_rw + (_shift(z_rw, 1) - z_rw) * rw_mu
    r, k, v, w_d, a_d, g_d = _split(z_rw, [RW_WIDTH] * 3 + [DECAY_LORA, AAA_LORA, GATE_LORA])
    w_raw = (rw_w0 + jnp.tanh(w_d) @ rw_w2).astype(f32)
    decay = jnp.exp(-jnp.exp(-jax.nn.softplus(-w_raw) - 0.5))
    a = jax.nn.sigmoid((rw_a0 + a_d @ rw_a2).astype(f32))
    g = (jax.nn.sigmoid(g_d) @ rw_g2).astype(f32)

    def heads(t):
        return t.astype(f32).reshape(bsz, seq, RW_HEADS, RW_HEAD_DIM)

    kf = k.astype(f32)
    kk = heads(kf * rw_k_k)
    kk = kk / jnp.maximum(jnp.linalg.norm(kk, axis=-1, keepdims=True), 1e-12)
    k_mod = heads(kf * (1.0 + (a - 1.0) * rw_k_a))
    r_h, v_h, a_h, w_h = heads(r), heads(v), heads(a), heads(decay)
    y = _rwkv7_scan(r_h, w_h, k_mod, v_h, kk, kk * a_h)
    mu = jnp.mean(y, axis=-1, keepdims=True)
    var = jnp.mean(jnp.square(y - mu), axis=-1, keepdims=True)
    gn_w = rw_gn_w.astype(f32).reshape(RW_HEADS, RW_HEAD_DIM)
    gn_b = rw_gn_b.astype(f32).reshape(RW_HEADS, RW_HEAD_DIM)
    y = (y - mu) * lax.rsqrt(var + GN_EPS) * gn_w + gn_b
    y = y + jnp.sum(r_h * k_mod * rw_r_k, axis=-1, keepdims=True) * v_h
    y_rw = y.reshape(bsz, seq, RW_WIDTH) * g

    q2, k2, v2, o2, i_pre, f_pre = _split(z_ml, [ML_WIDTH] * 4 + [ML_HEADS] * 2)
    qk = jax.nn.silu(_causal_conv(jnp.concatenate([q2, k2], axis=-1), ml_conv_w, ml_conv_b))
    q2, k2 = _split(qk, [ML_WIDTH, ML_WIDTH])

    def mh(t):
        return t.reshape(bsz, seq, ML_HEADS, ML_HEAD_DIM)

    hm = _mlstm_chunkwise(mh(q2), mh(k2), mh(v2), i_pre + ml_i_b, f_pre + ml_f_b)
    mu = jnp.mean(hm, axis=-1, keepdims=True)
    var = jnp.mean(jnp.square(hm - mu), axis=-1, keepdims=True)
    hm = ((hm - mu) * lax.rsqrt(var + ML_NORM_EPS)).reshape(bsz, seq, ML_WIDTH)
    y_ml = hm * ml_norm.astype(f32) * jax.nn.sigmoid(o2.astype(f32))

    g_a, g_b = _split(z_gate, [D_MODEL, D_MODEL])
    dt = h.dtype
    merged = (jax.nn.sigmoid(g_a) * (y_rw.astype(dt) @ w_up_rw)
              + jax.nn.sigmoid(g_b) * (y_ml.astype(dt) @ w_up_ml))
    return merged @ w_out

def _memory_attention(hq, hm, wq, wkv, wo):
    bsz, seq, _ = hq.shape
    mlen = hm.shape[1]
    q = (hq @ wq).reshape(bsz, seq, XA_HEADS, XA_HEAD_DIM)
    k, v = _split(hm @ wkv, [D_MODEL, D_MODEL])
    k = k.reshape(bsz, mlen, XA_HEADS, XA_HEAD_DIM)
    v = v.reshape(bsz, mlen, XA_HEADS, XA_HEAD_DIM)
    s = jnp.einsum('bshd,bmhd->bhsm', q, k).astype(jnp.float32) * (XA_HEAD_DIM ** -0.5)
    p = jax.nn.softmax(s, axis=-1).astype(hq.dtype)
    o = jnp.einsum('bhsm,bmhd->bshd', p, v).reshape(bsz, seq, D_MODEL)
    return o @ wo

def setup_inputs(seed: int = 0) -> dict:
    key = jax.random.key(seed)
    ks = iter(jax.random.split(key, 64))
    d = D_MODEL

    def nrm(shape, scale):
        return jax.random.normal(next(ks), (DEPTH,) + shape, jnp.float32) * scale

    def gain(shape):
        return 1.0 + 0.05 * jax.random.normal(next(ks), (DEPTH,) + shape, jnp.float32)

    def unif(shape, lo, hi):
        return jax.random.uniform(next(ks), (DEPTH,) + shape, jnp.float32, lo, hi)

    return {
        "x": jax.random.normal(next(ks), (BATCH, SEQ, d), jnp.float32),
        "mem": jax.random.normal(next(ks), (BATCH, MEM_LEN, d), jnp.float32),
        "ffn1_norm": gain((d,)),
        "ffn1_w_gate": nrm((d, D_FF), d ** -0.5),
        "ffn1_w_up": nrm((d, D_FF), d ** -0.5),
        "ffn1_w_down": nrm((D_FF, d), D_FF ** -0.5),
        "mix_norm": gain((d,)),
        "w_in": nrm((d, IN_COLS), d ** -0.5),
        "rw_mu": unif((RW_COLS,), 0.0, 1.0),
        "rw_w0": unif((RW_WIDTH,), -4.0, 1.0),
        "rw_w2": nrm((DECAY_LORA, RW_WIDTH), 0.5 * DECAY_LORA ** -0.5),
        "rw_a0": nrm((RW_WIDTH,), 0.1),
        "rw_a2": nrm((AAA_LORA, RW_WIDTH), AAA_LORA ** -0.5),
        "rw_g2": nrm((GATE_LORA, RW_WIDTH), GATE_LORA ** -0.5),
        "rw_k_k": 0.85 + nrm((RW_WIDTH,), 0.05),
        "rw_k_a": gain((RW_WIDTH,)),
        "rw_r_k": nrm((RW_HEADS, RW_HEAD_DIM), 0.1),
        "rw_gn_w": gain((RW_WIDTH,)),
        "rw_gn_b": nrm((RW_WIDTH,), 0.01),
        "ml_conv_w": nrm((ML_CONV, 2 * ML_WIDTH), ML_CONV ** -0.5),
        "ml_conv_b": nrm((2 * ML_WIDTH,), 0.01),
        "ml_i_b": unif((ML_HEADS,), -2.0, 0.0),
        "ml_f_b": unif((ML_HEADS,), 3.0, 6.0),
        "ml_norm": gain((ML_WIDTH,)),
        "w_up_rw": nrm((RW_WIDTH, d), RW_WIDTH ** -0.5),
        "w_up_ml": nrm((ML_WIDTH, d), ML_WIDTH ** -0.5),
        "w_out": nrm((d, d), d ** -0.5),
        "xa_norm": gain((d,)),
        "mem_norm": gain((d,)),
        "xa_wq": nrm((d, d), d ** -0.5),
        "xa_wkv": nrm((d, 2 * d), d ** -0.5),
        "xa_wo": nrm((d, d), d ** -0.5),
        "ffn2_norm": gain((d,)),
        "ffn2_w_gate": nrm((d, D_FF), d ** -0.5),
        "ffn2_w_up": nrm((d, D_FF), d ** -0.5),
        "ffn2_w_down": nrm((D_FF, d), D_FF ** -0.5),
        "final_norm": 1.0 + 0.05 * jax.random.normal(next(ks), (d,), jnp.float32),
    }

def reference(x, mem, ffn1_norm, ffn1_w_gate, ffn1_w_up, ffn1_w_down, mix_norm, w_in,
              rw_mu, rw_w0, rw_w2, rw_a0, rw_a2, rw_g2, rw_k_k, rw_k_a, rw_r_k, rw_gn_w, rw_gn_b,
              ml_conv_w, ml_conv_b, ml_i_b, ml_f_b, ml_norm, w_up_rw, w_up_ml, w_out,
              xa_norm, mem_norm, xa_wq, xa_wkv, xa_wo,
              ffn2_norm, ffn2_w_gate, ffn2_w_up, ffn2_w_down, final_norm):
    for l in range(DEPTH):
        x = x + FFN_HALF * _swiglu(_rmsnorm(x, ffn1_norm[l]), ffn1_w_gate[l], ffn1_w_up[l], ffn1_w_down[l])
        x = x + _token_mix(_rmsnorm(x, mix_norm[l]), w_in[l], rw_mu[l], rw_w0[l], rw_w2[l], rw_a0[l],
                           rw_a2[l], rw_g2[l], rw_k_k[l], rw_k_a[l], rw_r_k[l], rw_gn_w[l], rw_gn_b[l],
                           ml_conv_w[l], ml_conv_b[l], ml_i_b[l], ml_f_b[l], ml_norm[l],
                           w_up_rw[l], w_up_ml[l], w_out[l])
        x = x + _memory_attention(_rmsnorm(x, xa_norm[l]), _rmsnorm(mem, mem_norm[l]),
                                  xa_wq[l], xa_wkv[l], xa_wo[l])
        x = x + FFN_HALF * _swiglu(_rmsnorm(x, ffn2_norm[l]), ffn2_w_gate[l], ffn2_w_up[l], ffn2_w_down[l])
    return _rmsnorm(x, final_norm)


_drawn_inputs = setup_inputs


def setup_inputs(seed=0):
    import zlib

    import numpy as np

    out = dict(_drawn_inputs(seed))
    spreads = {}
    factors = {'rw_w2': 5.193,
     'rw_a0': 5.178,
     'rw_k_k': 8.0,
     'rw_k_a': 4.004,
     'rw_gn_w': 4.241,
     'rw_gn_b': 8.0,
     'ml_conv_b': 8.0,
     'ml_i_b': 8.0,
     'ml_norm': 4.173,
     'xa_norm': 8.0,
     'mem_norm': 7.798,
     'ffn2_norm': 2.974}
    for name, (base, spread) in spreads.items():
        noise = np.random.default_rng([zlib.crc32(name.encode()), seed]).standard_normal(out[name].shape)
        drawn = base * np.exp(spread * noise) if base else spread * noise
        out[name] = __import__('jax').numpy.asarray(drawn.astype(out[name].dtype))
    for name, factor in factors.items():
        out[name] = (out[name] * factor).astype(out[name].dtype)
    return out
```

```python
from contextlib import ExitStack, nullcontext

import numpy as np

import concourse.bass as bass
from concourse import mybir

P = 128
D = 1024
T = 1024
KD = D // P
HALF = 512
NHALF = T // HALF
MEM = 256
FF = 2816
FFC = FF // P
FF_PARTS = (8, 8, 6)
SEG = 128
NSEG = T // SEG
NH = 8
HD = 64
RC = 4
MH = 4
XH = 4
RW_UNITS = 14
ML_UNITS = 16
LEVELS = 7
DEC = SEG + 1

EPS = 1e-5
GN_EPS = 64e-5
ML_EPS = 1e-6
KAPPA = float(np.exp(-0.5)) / 2
ML_SCALE = P ** -0.5
XA_SCALE = (D // XH) ** -0.5

ALU = mybir.AluOpType
ACT = mybir.ActivationFunctionType
F32 = mybir.dt.float32
F32R = mybir.dt.float32r
U32 = mybir.dt.uint32
AX_X = mybir.AxisListType.X

C_ID, C_ONES, C_HONES, C_LOW, C_UP, C_UPEQ, C_LEV = (n * P for n in range(7))
C_ADD = C_LEV + LEVELS * P
C_RST = C_ADD + P
C_SEL = C_RST + RC * DEC
C_RSC = C_SEL + MH * P
C_ZERO = C_RSC + 1
NCONST = C_ZERO + 1
CONSTS = 3

VECS = [("ffn1_norm", 8), ("mix_norm", 8), ("xa_norm", 8), ("mem_norm", 8), ("ffn2_norm", 8), ("final_norm", 8),
        ("rw_mu", 14), ("rw_w0", 4), ("rw_a0", 4), ("rw_k_k", 4), ("rw_k_a", 4), ("rw_r_k", 4), ("rw_gn_w", 4),
        ("rw_gn_b", 4), ("conv_w0", 8), ("conv_w1", 8), ("conv_w2", 8), ("conv_w3", 8), ("conv_b", 8),
        ("ml_norm", 4)]
VCOL = {}
NVEC = 0
for _n, _w in VECS:
    VCOL[_n] = NVEC
    NVEC += _w


class Steps:

    def __init__(self, sem, names):
        self.sem, self.names, self.n = sem, names, len(names)
        self.where = {name: k + 1 for k, name in enumerate(names)}
        self.next = 0
        assert len(self.where) == self.n

    def sig(self, name):
        assert self.names[self.next % self.n] == name, (name, self.names[self.next % self.n])
        self.next += 1
        return self.sem, 1

    def at(self, name, it):
        return self.sem, (it + 1) * self.n + self.where[name]


RW_PE = (["lora", "gate", "ss", "vT", "bonus", "aT", "bT", "kT", "A", "Mu", "Mv", "B", "am1T"]
         + [x for n in range(1, LEVELS) for x in ((f"W{n}", f"D{n}", f"E{n}") if n < LEVELS - 1 else (f"W{n}", f"E{n}"))]
         + ["Z", "Wst", "U", "Y", "dS", "mean", "var"])
RW_ACT = (["th", "ad", "gt", "tw", "ta", "vtok", "lnn", "rinv", "P", "Pi", "gev", "atok", "btok", "ktok"]
          + [f"Wc{n}" for n in range(1, LEVELS)] + ["Zc", "W1c", "Un", "Y0", "Y1", "lnv", "rsv"])
RW_DVE = (["gs", "kkr", "sq", "dec", "scan", "hend", "cc", "av", "u1", "u2", "kmod", "rk", "rkb", "ssc",
           "n1", "n2", "n3", "rin", "kk", "bv", "kka", "alpha", "beta", "kap", "rho", "S0s",
           "A", "am0", "T0", "U0", "am1", "Mv", "Mu", "B", "T1", "U1"]
          + [x for n in range(2, LEVELS) for x in ((f"am{n}", f"T{n}", f"U{n}") if n < LEVELS - 1 else (f"am{n}", f"U{n}"))]
          + ["dS", "S", "yc", "ysq", "ve", "g1", "g2", "g3", "g4", "y1", "y2", "y3", "y4", "y5"])
XA_PE = ["S", "T", "O"]
XA_ACT = ["q", "e", "pt", "hi"]
XA_DVE = ["mx", "nmx", "r", "p", "lo"]
ML_PE = ["bca", "bce", "bcn", "gT", "S", "kT", "vT", "num", "den", "dC", "dN", "mean", "var"]
ML_ACT = ["gst", "E", "nm", "gtok", "ktok", "vtok", "D", "aden", "lnv", "rsv"]
ML_DVE = ["arg", "P", "qe", "kw", "dmax", "rec", "hm", "dec", "C", "yc", "ysq", "ve", "g1", "g2", "g3", "g4",
          "y1", "y2", "y3"]


ROWS_SEQ, ROWS_ACT, FINAL_SEQ = 19, 2, 57


def layer_kernel(nc, a, out):
    ctx = ExitStack()
    sems = {}

    def sem(name):
        if name not in sems:
            sems[name] = ctx.enter_context(nc.semaphore(name))
        return sems[name]

    def dram(name, shape):
        return nc.dram_tensor(name, shape, F32, kind="Internal").ap()

    x_park = dram("x_park", [P, KD, T])
    zrw_d = dram("zrw_d", [RW_UNITS, P, T])
    zml_d = dram("zml_d", [ML_UNITS, P, T])
    if_d = dram("if_d", [2 * MH, T])
    y_d = dram("y_d", [KD, P, T])
    merged_d = dram("merged_d", [KD, P, T])

    base = (nc.sbuf_base + 63) // 64 * 64
    end = nc.sbuf_usable_end
    top = {}

    def place(group, after, name, shape, dt=F32):
        at = top.get(group, top[after] if after else base)
        size = int(np.prod(shape[1:])) * 4
        top[group] = at + (size + 63) // 64 * 64
        assert top[group] <= end, (group, name, top[group] - end)
        return nc.alloc_sbuf_tensor_at(name, shape, dt, offset=at)

    cst = place("common", None, "cst", [P, NCONST])
    vec = place("common", None, "vec", [P, NVEC])
    hw0 = place("common", None, "hw0", [P, 2 * RC])
    gbias = place("common", None, "gbias", [MH, 2])
    raw = place("common", None, "raw", [P, 2, KD * P])
    whi = place("common", None, "whi", [P, 2, KD * P], F32R)
    wlo = place("common", None, "wlo", [P, 2, KD * P], F32R)
    hhi = place("common", None, "hhi", [P, KD, T], F32R)
    hlo = place("common", None, "hlo", [P, KD, T], F32R)
    xT = place("x", "common", "xT", [P, KD, T])
    ahi = place("ffn", "x", "ahi", [P, max(FF_PARTS), T], F32R)
    alo = place("ffn", "x", "alo", [P, max(FF_PARTS), T], F32R)
    s0 = nc.alloc_sbuf_tensor_at("s0", [P, T], F32, offset=end // 64 * 64 - 8192)
    s1 = nc.alloc_sbuf_tensor_at("s1", [P, T], F32, offset=end // 64 * 64 - 4096)
    assert top["ffn"] <= end // 64 * 64 - 8192, top["ffn"] - end
    nsq = place("norm", "x", "nsq", [P, 2, T])
    nms = place("norm", "x", "nms", [P, T])
    nr = place("norm", "x", "nr", [P, T])
    nt = place("norm", "x", "nt", [P, T])
    nh = place("norm", "x", "nh", [P, 2, T])
    stg = place("proj", "common", "stg", [P, 2, T + 3])
    pd = place("proj", "common", "pd", [P, 2, T])
    po = place("proj", "common", "po", [P, 2, T])
    ifs = place("proj", "common", "ifs", [P, T])
    zs = place("rw", "common", "zs", [P, RW_UNITS, SEG])
    loraw = place("rw", "common", "loraw", [P, 2, RC * P])
    lora = place("rw", "common", "lora", [P, SEG])
    gsig = place("rw", "common", "gsig", [P, SEG])
    dec = place("rw", "common", "dec", [P, RC, DEC])
    cum = place("rw", "common", "cum", [P, RC, DEC])
    hend = place("rw", "common", "hend", [P, RC, 1])
    Pp = place("rw", "common", "Pp", [P, RC, DEC])
    Pi = place("rw", "common", "Pi", [P, RC, DEC])

    def rw(name, shape=(P, RC, SEG)):
        return place("rw", "common", name, list(shape))

    kkr, ksq, rkb, ssc, rinv, nw, ga, gu, kmod, kk, kka = (rw(n) for n in (
        "kkr", "ksq", "rkb", "ssc", "rinv", "nw", "ga", "gu", "kmod", "kk", "kka"))
    alpha, beta, kap, rho, gout, bv = (rw(n) for n in ("alpha", "beta", "kap", "rho", "gout", "bv"))
    atok, btok, ktok, vtok = (rw(n) for n in ("atok", "btok", "ktok", "vtok"))
    Am, Bm, Mv, Mu, Tm, Um, Wm, AL = (rw(n, (P, NH, SEG)) for n in ("Am", "Bm", "Mv", "Mu", "Tm", "Um", "Wm", "AL"))
    W1m = rw("W1m")
    Zm = rw("Zm", (P, NH, HD))
    Un = rw("Un", (P, NH, HD))
    St = rw("St", (P, RC, HD))
    S0s = rw("S0s", (P, RC, HD))
    Ys, yo = rw("Ys"), rw("yo")
    zm = place("ml", "common", "zm", [P, ML_UNITS, SEG])
    ifr = nc.alloc_sbuf_tensor_at("ifr", [MH, T], F32, offset=end // 64 * 64 - 7 * 4096)
    mrow, brow, arow, erow, nrow, grow = (
        nc.alloc_sbuf_tensor_at(n, [MH, T], F32, offset=end // 64 * 64 - (6 - k) * 4096)
        for k, n in enumerate(("mrow", "brow", "arow", "erow", "nrow", "grow")))

    def ml(name, shape=(P, MH, SEG)):
        return place("ml", "common", name, list(shape))

    gst = ml("gst", (MH, SEG))
    gtok = ml("gtok", (P, MH))
    Eb, nmb, Db, Pb, qe, kw, mktok, mvtok, aden, hm = (ml(n) for n in (
        "Eb", "nmb", "Db", "Pb", "qe", "kw", "mktok", "mvtok", "aden", "hm"))
    argb, mysq, mve, mrs, mnw, myo = (ml(n) for n in ("argb", "mysq", "mve", "mrs", "mnw", "myo"))
    CN = ml("CN", (P, 2, MH, SEG))
    CNd = ml("CNd", (P, 2, MH, SEG))
    assert top["ml"] <= end // 64 * 64 - 7 * 4096
    yhi = place("merge", "common", "yhi", [P, KD, T], F32R)
    ylo = place("merge", "common", "ylo", [P, KD, T], F32R)
    ysg = place("merge", "common", "ysg", [P, 2, T])
    sga = place("merge", "common", "sga", [P, T])
    sgb = place("merge", "common", "sgb", [P, T])
    mo = place("merge", "common", "mo", [P, 2, T])
    qT = place("xa", "x", "qT", [P, KD, T])
    kTx = place("xa", "x", "kTx", [P, KD, MEM])
    vx = place("xa", "x", "vx", [P, 2, D])
    mem_at = top["xa"]
    qs = place("xa", "x", "qs", [P, KD, SEG])
    sx = place("xa", "x", "sx", [P, XH, MEM])
    px = place("xa", "x", "px", [P, XH, MEM])
    pxt = place("xa", "x", "pxt", [P, XH, 2, SEG])
    mx = place("xa", "x", "mx", [P, 4 * XH])
    ox = place("xa", "x", "ox", [P, KD, SEG])
    memx = nc.alloc_sbuf_tensor_at("memx", [P, KD, MEM], F32, offset=top["norm"] - 2 * T * 4)
    top["mem"] = mem_at
    memhi = place("mem", "x", "memhi", [P, KD, MEM], F32R)
    memlo = place("mem", "x", "memlo", [P, KD, MEM], F32R)
    memr = place("mem", "x", "memr", [P, 3, MEM])
    memq = place("mem", "x", "memq", [P, 2, MEM])
    memh = place("mem", "x", "memh", [P, 2, MEM])

    G = [nc.alloc_psum_tensor(f"G{n}", [P, NHALF, HALF], F32) for n in range(4)]

    def flat(ap):
        return ap.rearrange("p a b -> p (a b)")

    def con(col, n=P, rows=P):
        return cst[0:rows, col:col + n]

    def v1(name, k=0):
        return vec[:, VCOL[name] + k:VCOL[name] + k + 1]

    def vbc(name, width):
        return vec[:, VCOL[name]:VCOL[name] + RC].unsqueeze(2).to_broadcast([P, RC, width])

    const_loads = [(cst[:], a["consts"]), (vec[:], a["vecs"]), (gbias[:], a["gate_b"])]

    credit = 64
    consts_in = sem("consts_in")
    x_in = sem("x_in")
    raw_in = [sem("raw_in0"), sem("raw_in1")]
    hi_made = sem("hi_made")
    split_made = sem("split_made")
    unit_used = sem("unit_used")
    act_free = sem("act_free")
    dve_free = sem("dve_free")
    phase_end = sem("phase_end")
    dve_seq = sem("dve_seq")
    act_seq = sem("act_seq")
    a_hi = sem("a_hi")
    a_lo = sem("a_lo")
    norm_sum = sem("norm_sum")
    norm_ms = sem("norm_ms")
    norm_r = sem("norm_r")
    z_out = [sem("z_out0"), sem("z_out1")]
    silu_made = sem("silu_made")
    store = sem("store")

    nsq_act = Steps(sem("nsq_act"), ["sq0", "sq1"])
    nsq_dve = Steps(sem("nsq_dve"), ["add0", "add1"])
    nh_act = Steps(sem("nh_act"), ["c0", "c1"])
    nh_dve = Steps(sem("nh_dve"), ["h0", "h1", "l0", "l1"])
    rp_dve = Steps(sem("rp_dve"), ["d0", "m0", "d1", "m1"])
    cv_dve = Steps(sem("cv_dve"), [f"t{j}{r}" for r in range(2) for j in range(4)])
    sp_in = [sem("sp_in0"), sem("sp_in1")]
    sp_act = Steps(sem("sp_act"), ["c0", "c1"])
    sp_dve = Steps(sem("sp_dve"), ["l0", "l1"])
    mg_dve = Steps(sem("mg_dve"), ["mo0", "mo1"])
    rw_pe, rw_act, rw_dve = (Steps(sem(n), x) for n, x in (("rw_pe", RW_PE), ("rw_act", RW_ACT), ("rw_dve", RW_DVE)))
    ml_pe, ml_act, ml_dve = (Steps(sem(n), x) for n, x in (("ml_pe", ML_PE), ("ml_act", ML_ACT), ("ml_dve", ML_DVE)))
    xa_pe, xa_act, xa_dve = (Steps(sem(n), x) for n, x in (("xa_pe", XA_PE), ("xa_act", XA_ACT), ("xa_dve", XA_DVE)))
    zs_in, zm_in, y_out = sem("zs_in"), sem("zm_in"), sem("y_out")
    ACT_STEPS = (nsq_act, nh_act, sp_act, rw_act, ml_act, xa_act)
    DVE_STEPS = (nsq_dve, nh_dve, rp_dve, cv_dve, sp_dve, mg_dve, rw_dve, ml_dve, xa_dve)
    PE_STEPS = (rw_pe, ml_pe, xa_pe)

    stream = []
    for f in (1, 2):
        if f == 2:
            stream += [(["rw_in"], RW_UNITS, 8, 0), (["ml_in"], ML_UNITS, 8, 0), (["if_in"], 1, 8, 0),
                       (["ga_in", "gb_in", "up"], KD, 8, 0), (["w_out"], KD, 8, 0), (["wkv"], 2 * KD, 8, 0),
                       (["wq"], KD, 8, 0), (["wo"], KD, 8, 0)]
        first = 0
        for part, c_ in enumerate(FF_PARTS):
            stream.append(([f"wg{f}", f"wu{f}"], c_, 8, first))
            stream.append(([f"wd{f}_{part}"], KD, c_, 0))
            first += c_

    def runs():
        u = 0
        for names, n, tiles, first in stream:
            yield names, n, tiles, first, u
            u += n * len(names)

    block = ctx.enter_context(nc.Block())

    class Count:

        def __init__(self):
            self.unit = self.act = self.dve = self.seq = self.phase = self.a = 0
            self.norm = self.norms = self.z = self.silu = self.split = 0

        def advance(self, unit=0, act=0, dve=0, a=0, z=0, norm=0, norms=0):
            self.unit += unit
            self.act += act
            self.dve += dve
            self.a += a
            self.z += z
            self.norm += norm
            self.norms += norms

    def barrier(eng, c):
        c.phase += 1
        eng.drain().then_inc(phase_end, 1)
        eng.wait_ge(phase_end, 3 * c.phase)

    def loop(eng, n):
        return eng.Fori(0, n) if n > 1 else nullcontext(0)

    def bank_act(n):
        return G[n % 2]

    def bank_dve(n):
        return G[2 + n % 2]

    @block.sync
    def _(sp):
        for names, n, tiles, first, u0 in runs():
            w, m = tiles * P, len(names)

            def load(k, name, idx, u):
                sp.wait_ge(split_made, u + (credit - 1))
                sp.dma_start(raw[:, k, 0:w], a[name][idx]).then_inc(raw_in[k], 16)

            rounds = 1 if m % 2 == 0 or n == 1 else 2
            with loop(sp, n // rounds) as i:
                for r in range(rounds):
                    for j, name in enumerate(names):
                        o = r * m + j
                        load((u0 + o) % 2, name, i * rounds + (r + first), i * (rounds * m) + (u0 + o))

    @block.gpsimd
    def _(pool):
        pool.sem_inc(split_made, credit)
        pool.sem_inc(hi_made, credit)
        pool.wait_ge(consts_in, CONSTS * 16)
        for names, n, tiles, first, u0 in runs():
            w, total = tiles * P, n * len(names)

            def split(k, u, turn):
                pool.wait_ge(unit_used, u + (credit - 1))
                pool.wait_ge(raw_in[k], turn * 16)
                nc.gpsimd.tensor_tensor(whi[:, k, 0:w], raw[:, k, 0:w], cst[:, C_ZERO:C_ZERO + 1].to_broadcast([P, w]),
                                        ALU.add).then_inc(hi_made, 1)
                pool.wait_ge(hi_made, u + (credit + 1))
                nc.gpsimd.tensor_tensor(wlo[:, k, 0:w], raw[:, k, 0:w], whi[:, k, 0:w].bitcast(F32),
                                        ALU.subtract).then_inc(split_made, 1)

            rounds = 2 if total > 1 else 1
            with loop(pool, total // rounds) as i:
                for r in range(rounds):
                    u = u0 + r
                    split(u % 2, i * rounds + u, i + (u // 2 + 1))

    @block.tensor
    def _(pe):
        c = Count()
        pe.sem_inc(unit_used, credit)
        for s in PE_STEPS:
            pe.sem_inc(s.sem, s.n)

        def tile3(dst, k, t, hi, lo, start, stop):
            wh, wl = whi[:, k, t * P:(t + 1) * P], wlo[:, k, t * P:(t + 1) * P]
            nc.tensor.matmul(dst, wh, hi, start=start, stop=False)
            nc.tensor.matmul(dst, wh, lo, start=False, stop=False)
            return nc.tensor.matmul(dst, wl, hi, start=False, stop=stop)

        def product(bank, k, tiles, hi, lo):
            for h in range(NHALF):
                cols = slice(h * HALF, (h + 1) * HALF)
                for n, t in enumerate(tiles):
                    last = tile3(bank[:, h, :], k, t, hi[:, n, cols], lo[:, n, cols], n == 0, n == len(tiles) - 1)
            return last

        def unit_ready(u):
            pe.wait_ge(split_made, u + (credit + 1))

        def act_bank(n):
            pe.wait_ge(act_free, n + (credit - 1))

        def dve_bank(n):
            pe.wait_ge(dve_free, n + (credit - 1))

        def gemm(n, by, tiles=8, hi=hhi, lo=hlo):
            count = c.act if by == "act" else c.dve
            with loop(pe, n // 2 if n > 1 else 1) as i:
                for r in range(min(n, 2)):
                    (act_bank if by == "act" else dve_bank)(i * 2 + (count + r))
                    unit_ready(i * 2 + (c.unit + r))
                    bank = (bank_act if by == "act" else bank_dve)(count + r)
                    product(bank, (c.unit + r) % 2, range(tiles), hi, lo).then_inc(unit_used, 1)
            c.advance(unit=n, act=n if by == "act" else 0, dve=n if by == "dve" else 0)

        def norm(acc, width):
            c.norm += 4
            c.norms += 1
            pe.wait_ge(*nsq_dve.at("add1", c.norm - 1))
            dve_bank(c.dve)
            cols = min(width, HALF)
            for h in range(width // cols):
                last = nc.tensor.matmul(bank_dve(c.dve)[:, h, 0:cols], con(C_ONES), acc[:, h * cols:(h + 1) * cols],
                                        start=True, stop=True)
            last.then_inc(norm_sum, 1)
            c.dve += 1

        def norm_done():
            pe.wait_ge(*nh_dve.at("l1", c.norm - 1))

        def ffn():
            norm(nt, T)
            norm_done()
            for n in FF_PARTS:
                with loop(pe, n // 2) as i:
                    for r in range(2):
                        act_bank(i * 2 + (c.act + r))
                        unit_ready(i * 4 + (c.unit + 2 * r))
                        product(bank_act(c.act + r), (c.unit + 2 * r) % 2, range(KD), hhi, hlo).then_inc(unit_used, 1)
                        dve_bank(i * 2 + (c.dve + r))
                        unit_ready(i * 4 + (c.unit + 2 * r + 1))
                        product(bank_dve(c.dve + r), (c.unit + 2 * r + 1) % 2, range(KD), hhi,
                                hlo).then_inc(unit_used, 1)
                c.advance(unit=2 * n, act=n, dve=n, a=n)
                pe.wait_ge(a_lo, c.a + 1)
                gemm(KD, "dve", tiles=n, hi=ahi, lo=alo)

        def rwkv():
            with pe.Fori(0, NSEG) as i:
                g0, g1, g2, g3 = G
                pe.wait_ge(*rw_act.at("ad", i))
                pe.wait_ge(*rw_act.at("th", i))
                for r in range(RC):
                    nc.tensor.matmul(g0[:, 0, r * P:(r + 1) * P], loraw[0:HD, 0, r * P:(r + 1) * P], lora[0:HD, :],
                                     start=True, stop=True)
                    last = nc.tensor.matmul(g0[:, 1, r * P:(r + 1) * P], loraw[HD:P, 0, r * P:(r + 1) * P],
                                            lora[HD:P, :], start=True, stop=True)
                last.then_inc(*rw_pe.sig("lora"))
                pe.wait_ge(*rw_dve.at("gs", i))
                for r in range(RC):
                    last = nc.tensor.matmul(g1[:, 0, r * P:(r + 1) * P], loraw[:, 1, r * P:(r + 1) * P], gsig[:],
                                            start=True, stop=True)
                last.then_inc(*rw_pe.sig("gate"))
                pe.wait_ge(*rw_dve.at("sq", i))
                nc.tensor.matmul(g1[:, 1, :], con(C_HONES), flat(ksq[:]), start=True,
                                 stop=True).then_inc(*rw_pe.sig("ss"))
                for r in range(RC):
                    last = nc.tensor.transpose(g2[:, 1, r * P:(r + 1) * P], zs[:, 8 + r, :], con(C_ID))
                last.then_inc(*rw_pe.sig("vT"))
                pe.wait_ge(*rw_dve.at("rkb", i))
                nc.tensor.matmul(g2[:, 0, :], con(C_HONES), flat(rkb[:]), start=True,
                                 stop=True).then_inc(*rw_pe.sig("bonus"))
                pe.wait_ge(*rw_dve.at("rho", i))
                for name, src, dst in (("aT", alpha, g0[:, 0, :]), ("bT", beta, g0[:, 1, :]), ("kT", kap, g3[:, 0, :])):
                    for r in range(RC):
                        last = nc.tensor.transpose(dst[:, r * P:(r + 1) * P], src[:, r, :], con(C_ID))
                    last.then_inc(*rw_pe.sig(name))

                def gram(name, left, right, dst):
                    for e in range(2):
                        for r in range(RC):
                            last = nc.tensor.matmul(dst[:, e, r * P:(r + 1) * P], left[e * HD:(e + 1) * HD, r, :],
                                                    right[e * HD:(e + 1) * HD, r, :], start=True, stop=True)
                    last.then_inc(*rw_pe.sig(name))

                pe.wait_ge(*rw_act.at("gev", i))
                pe.wait_ge(*rw_dve.at("ssc", i))
                gram("A", alpha, beta, g1)
                pe.wait_ge(*rw_act.at("vtok", i))
                gram("Mu", beta, rho, g2)
                pe.wait_ge(*rw_act.at("btok", i))
                gram("Mv", kap, rho, g0)
                pe.wait_ge(*rw_act.at("ktok", i))
                gram("B", kap, alpha, g3)
                pe.wait_ge(*rw_dve.at("am0", i))
                for n in range(NH):
                    last = nc.tensor.transpose(flat(g1[:])[:, n * P:(n + 1) * P], AL[:, n, :], con(C_ID))
                last.then_inc(*rw_pe.sig("am1T"))

                def eight(name, dst, left, right):
                    for n in range(NH):
                        last = nc.tensor.matmul(flat(dst[:])[:, n * P:(n + 1) * P], left[:, n, :], right[:, n, :],
                                                start=True, stop=True)
                    last.then_inc(*rw_pe.sig(name))

                for n in range(1, LEVELS):
                    pe.wait_ge(*rw_dve.at(f"am{n}", i))
                    if n == 1:
                        pe.wait_ge(*rw_dve.at("Mv", i))
                    eight(f"W{n}", g0, AL, Um)
                    pe.wait_ge(*rw_act.at(f"Wc{n}", i))
                    if n < LEVELS - 1:
                        eight(f"D{n}", g1, Wm, Tm)
                    if n == 1:
                        pe.wait_ge(*rw_dve.at("Mu", i))
                    eight(f"E{n}", g2, Tm, Wm)
                pe.wait_ge(*rw_dve.at("B", i))
                for n in range(NH):
                    e, r = divmod(n, RC)
                    last = nc.tensor.matmul(g3[:, 0, n * HD:(n + 1) * HD], Bm[:, n, :],
                                            vtok[:, r, e * HD:(e + 1) * HD], start=True, stop=True)
                last.then_inc(*rw_pe.sig("Z"))
                pe.wait_ge(*rw_dve.at(f"U{LEVELS - 1}", i))
                for n in range(NH):
                    e, r = divmod(n, RC)
                    last = nc.tensor.matmul(g3[e * HD:(e + 1) * HD, 1, r * P:(r + 1) * P],
                                            atok[:, r, e * HD:(e + 1) * HD], Um[:, n, :], start=True, stop=True)
                last.then_inc(*rw_pe.sig("Wst"))
                pe.wait_ge(*rw_act.at("W1c", i))
                for n in range(NH):
                    e, r = divmod(n, RC)
                    rows = slice(e * HD, (e + 1) * HD)
                    dst = g0[:, e, r * HD:(r + 1) * HD]
                    nc.tensor.matmul(dst, Um[:, n, :], Zm[:, n, :], start=True, stop=False)
                    last = nc.tensor.matmul(dst, W1m[rows, r, :], S0s[rows, r, :], start=False, stop=True)
                last.then_inc(*rw_pe.sig("U"))
                pe.wait_ge(*rw_act.at("Un", i))
                for n in range(NH):
                    e, r = divmod(n, RC)
                    rows = slice(e * HD, (e + 1) * HD)
                    dst = g1[rows, e, r * P:(r + 1) * P]
                    nc.tensor.matmul(dst, vtok[:, r, rows], Mv[:, n, :], start=True, stop=False)
                    nc.tensor.matmul(dst, S0s[rows, r, :], rho[rows, r, :], start=False, stop=False)
                    last = nc.tensor.matmul(dst, Un[:, n, :], Mu[:, n, :], start=False, stop=True)
                last.then_inc(*rw_pe.sig("Y"))
                for n in range(NH):
                    e, r = divmod(n, RC)
                    rows = slice(e * HD, (e + 1) * HD)
                    dst = g3[rows, 0, r * HD:(r + 1) * HD]
                    nc.tensor.matmul(dst, ktok[:, r, rows], vtok[:, r, rows], start=True, stop=False)
                    last = nc.tensor.matmul(dst, btok[:, r, rows], Un[:, n, :], start=False, stop=True)
                last.then_inc(*rw_pe.sig("dS"))
                pe.wait_ge(*rw_act.at("Y1", i))
                nc.tensor.matmul(g2[:, 0, :], con(C_HONES), flat(Ys[:]), start=True,
                                 stop=True).then_inc(*rw_pe.sig("mean"))
                pe.wait_ge(*rw_dve.at("ysq", i))
                nc.tensor.matmul(g2[:, 1, :], con(C_HONES), flat(ksq[:]), start=True,
                                 stop=True).then_inc(*rw_pe.sig("var"))

        def mlstm():
            with pe.Fori(0, NSEG) as i:
                g0, g1, g2, g3 = G
                at = i * SEG
                for name, row, dst, before in (("bca", arow, g0[:, 0, :], "yc"), ("bce", erow, g0[:, 1, :], "ve"),
                                               ("bcn", mrow, g1[:, 0, :], "y1")):
                    pe.wait_ge(*ml_dve.at(before, i - 1))
                    for h in range(MH):
                        last = nc.tensor.matmul(dst[:, h * SEG:(h + 1) * SEG], cst[0:MH, C_SEL + h * P:C_SEL + (h + 1) * P],
                                                row[:, bass.ds(at, SEG)], start=True, stop=True)
                    last.then_inc(*ml_pe.sig(name))
                pe.wait_ge(*ml_act.at("gst", i))
                nc.tensor.matmul(g1[:, 1, 0:MH], gst[:], cst[0:MH, C_ID:C_ID + MH], start=True,
                                 stop=True).then_inc(*ml_pe.sig("gT"))
                pe.wait_ge(zm_in, i * 16 + 16)
                for h in range(MH):
                    last = nc.tensor.matmul(g2[:, 0, h * SEG:(h + 1) * SEG], zm[:, MH + h, :], zm[:, h, :],
                                            start=True, stop=True)
                last.then_inc(*ml_pe.sig("S"))
                for name, first, dst in (("kT", MH, g2[:, 1, :]), ("vT", 2 * MH, g3[:, 0, :])):
                    for h in range(MH):
                        last = nc.tensor.transpose(dst[:, h * SEG:(h + 1) * SEG], zm[:, first + h, :], con(C_ID))
                    last.then_inc(*ml_pe.sig(name))
                pe.wait_ge(*ml_act.at("vtok", i))
                pe.wait_ge(*ml_dve.at("qe", i))
                for h in range(MH):
                    dst = g3[:, 1, h * SEG:(h + 1) * SEG]
                    nc.tensor.matmul(dst, mvtok[:, h, :], Pb[:, h, :], start=True, stop=False)
                    last = nc.tensor.matmul(dst, CN[:, 0, h, :], qe[:, h, :], start=False, stop=True)
                last.then_inc(*ml_pe.sig("num"))
                pe.wait_ge(*ml_act.at("nm", i))
                for h in range(MH):
                    dst = g1[:, 0, h * SEG:(h + 1) * SEG]
                    nc.tensor.matmul(dst, con(C_ONES), Pb[:, h, :], start=True, stop=False)
                    last = nc.tensor.matmul(dst, CN[:, 1, h, :], qe[:, h, :], start=False, stop=True)
                last.then_inc(*ml_pe.sig("den"))
                pe.wait_ge(*ml_dve.at("kw", i))
                for h in range(MH):
                    last = nc.tensor.matmul(g2[:, 0, h * SEG:(h + 1) * SEG], kw[:, h, :], mvtok[:, h, :],
                                            start=True, stop=True)
                last.then_inc(*ml_pe.sig("dC"))
                for h in range(MH):
                    last = nc.tensor.matmul(g2[:, 1, h * SEG:(h + 1) * SEG], kw[:, h, :], con(C_ONES),
                                            start=True, stop=True)
                last.then_inc(*ml_pe.sig("dN"))
                pe.wait_ge(*ml_dve.at("hm", i))
                nc.tensor.matmul(g0[:, 0, :], con(C_ONES), flat(hm[:]), start=True,
                                 stop=True).then_inc(*ml_pe.sig("mean"))
                pe.wait_ge(*ml_dve.at("ysq", i))
                nc.tensor.matmul(g0[:, 1, :], con(C_ONES), flat(mysq[:]), start=True,
                                 stop=True).then_inc(*ml_pe.sig("var"))

        def merge():
            with pe.Fori(0, KD // 2) as i:
                for r in range(2):
                    u = i * 6 + (c.unit + 3 * r)
                    for n in range(2):
                        act_bank(i * 4 + (c.act + 2 * r + n))
                        unit_ready(u + n)
                        product(bank_act(c.act + n), (c.unit + 3 * r + n) % 2, range(KD), hhi, hlo).then_inc(unit_used, 1)
                    unit_ready(u + 2)
                    for n in range(2):
                        dve_bank(i * 4 + (c.dve + 2 * r + n))
                        last = product(bank_dve(c.dve + n), (c.unit + 3 * r + 2) % 2, range(n * RC, (n + 1) * RC),
                                       yhi[:, n * RC:(n + 1) * RC, :], ylo[:, n * RC:(n + 1) * RC, :])
                    last.then_inc(unit_used, 1)
            c.advance(unit=3 * KD, act=2 * KD, dve=2 * KD)

        def keys_values():
            norm(memr[:, 2, :], MEM)
            norm_done()
            for part in range(2):
                with pe.Fori(0, KD // 2) as i:
                    for r in range(2):
                        act_bank(i * 2 + (c.act + r))
                        unit_ready(i * 2 + (c.unit + r))
                        k = (c.unit + r) % 2
                        bank = bank_act(c.act + r)
                        if part == 0:
                            for t in range(KD):
                                last = tile3(bank[:, 0, 0:MEM], k, t, memhi[:, t, :], memlo[:, t, :], t == 0, t == KD - 1)
                        else:
                            for m in range(2):
                                rows, dst = slice(m * P, (m + 1) * P), bank[:, m, 0:P]
                                for t in range(KD):
                                    wh, wl = whi[:, k, t * P:(t + 1) * P], wlo[:, k, t * P:(t + 1) * P]
                                    nc.tensor.matmul(dst, memhi[:, t, rows], wh, start=t == 0, stop=False)
                                    nc.tensor.matmul(dst, memhi[:, t, rows], wl, start=False, stop=False)
                                    last = nc.tensor.matmul(dst, memlo[:, t, rows], wh, start=False, stop=t == KD - 1)
                        last.then_inc(unit_used, 1)
                c.advance(unit=KD, act=KD)

        def attend():
            with pe.Fori(0, NSEG) as i:
                g0, g1, g2, g3 = G
                pe.wait_ge(*xa_act.at("q", i))
                for h in range(XH):
                    for n in range(2):
                        last = nc.tensor.matmul(flat(g0[:])[:, h * MEM:(h + 1) * MEM], qs[:, 2 * h + n, :],
                                                kTx[:, 2 * h + n, :], start=n == 0, stop=n == 1)
                last.then_inc(*xa_pe.sig("S"))
                pe.wait_ge(*xa_dve.at("p", i))
                for h in range(XH):
                    for m in range(2):
                        last = nc.tensor.transpose(flat(g1[:])[:, (2 * h + m) * P:(2 * h + m + 1) * P],
                                                   px[:, h, m * P:(m + 1) * P], con(C_ID))
                last.then_inc(*xa_pe.sig("T"))
                pe.wait_ge(*xa_act.at("pt", i))
                pe.wait_ge(*xa_dve.at("lo", i - 1))
                for n in range(KD):
                    for m in range(2):
                        last = nc.tensor.matmul(flat(g2[:])[:, n * P:(n + 1) * P], vx[:, m, n * P:(n + 1) * P],
                                                pxt[:, n // 2, m, :], start=m == 0, stop=m == 1)
                last.then_inc(*xa_pe.sig("O"))

        pe.wait_ge(consts_in, CONSTS * 16)
        ffn()
        norm(nt, T)
        norm_done()
        barrier(pe, c)
        gemm(RW_UNITS, "act")
        gemm(ML_UNITS, "act")
        gemm(1, "act")
        barrier(pe, c)
        barrier(pe, c)
        rwkv()
        barrier(pe, c)
        barrier(pe, c)
        mlstm()
        barrier(pe, c)
        pe.wait_ge(*sp_dve.at("l1", 3))
        merge()
        barrier(pe, c)
        pe.wait_ge(*sp_dve.at("l1", 7))
        gemm(KD, "dve")
        barrier(pe, c)
        keys_values()
        norm(nt, T)
        norm_done()
        barrier(pe, c)
        gemm(KD, "act")
        barrier(pe, c)
        attend()
        barrier(pe, c)
        gemm(KD, "dve")
        ffn()
        norm(nt, T)

    @block.scalar
    def _(act):
        c = Count()
        act.sem_inc(act_free, credit)
        for s in (*z_out, silu_made, y_out):
            act.sem_inc(s, 16)
        for s in ACT_STEPS:
            act.sem_inc(s.sem, s.n)
        activation = nc.scalar.activation

        def output_ready(u):
            act.wait_ge(unit_used, u + (credit + 1))

        def norm(src, width, sq, ms, r, t, h, hi):
            with act.Fori(0, KD // 2) as i:
                for n in range(2):
                    act.wait_ge(*nsq_dve.at(f"add{n}", i + (c.norm - 1)))
                    activation(sq[:, n, :], src[:, i * 2 + n, :], ACT.Square).then_inc(*nsq_act.sig(f"sq{n}"))
            act.wait_ge(norm_ms, c.norms + 1)
            activation(r, ms, ACT.Ln).then_inc(act_seq, 1)
            c.seq += 1
            act.wait_ge(act_seq, c.seq)
            activation(r, r, ACT.Exp, scale=-0.5).then_inc(norm_r, 1)
            if hi is not None:
                with act.Fori(0, KD // 2) as i:
                    for n in range(2):
                        act.wait_ge(*nh_dve.at(f"h{n}", i + c.norm))
                        activation(hi[:, i * 2 + n, :], h[:, n, :], ACT.Copy).then_inc(*nh_act.sig(f"c{n}"))
            c.advance(norm=4, norms=1, dve=1)

        def norm_x(hi=hhi):
            norm(xT, T, nsq, nms[:], nr[:], nt[:], nh, hi)

        def ffn():
            act.wait_ge(dve_free, c.dve + credit)
            norm_x()
            for n in FF_PARTS:
                with loop(act, n // 2) as i:
                    for r in range(2):
                        output_ready(i * 4 + (c.unit + 2 * r))
                        act.wait_ge(dve_free, i * 2 + (c.dve + r + credit))
                        act.wait_ge(*nh_dve.at("l1", c.norm - 1))
                        activation(s0[:], flat(bank_act(c.act + r)[:]), ACT.Silu).then_inc(act_free, 1)
                        act.wait_ge(dve_free, i * 2 + (c.dve + r + 1 + credit))
                        activation(ahi[:, i * 2 + r, :], s1[:], ACT.Copy).then_inc(a_hi, 1)
                c.advance(unit=2 * n + KD, act=n, dve=n + KD, a=n)

        def store_z(dst, r, turn):
            act.dma_start(dst, po[:, r, :]).then_inc(z_out[r], 16)

        def po_free(r, turn):
            act.wait_ge(z_out[r], (turn + 1) * 16)

        def project_rw():
            with act.Fori(0, RW_UNITS // 2) as i:
                for r in range(2):
                    output_ready(i * 2 + (c.unit + r))
                    act.wait_ge(*rp_dve.at(f"m{r}", i - 1))
                    activation(stg[:, r, 3:3 + T], flat(bank_act(c.act + r)[:]), ACT.Copy).then_inc(act_free, 1)
                    act.wait_ge(*rp_dve.at(f"m{r}", i))
                    store_z(zrw_d[i * 2 + r], r, 0)
            c.advance(unit=RW_UNITS, act=RW_UNITS, z=RW_UNITS // 2)

        def project_ml():
            with act.Fori(0, MH) as i:
                for r in range(2):
                    output_ready(i * 2 + (c.unit + r))
                    act.wait_ge(*cv_dve.at(f"t3{r}", i - 1))
                    activation(stg[:, r, 3:3 + T], flat(bank_act(c.act + r)[:]), ACT.Copy).then_inc(act_free, 1)
                    act.wait_ge(*cv_dve.at(f"t3{r}", i))
                    po_free(r, i + c.z)
                    activation(po[:, r, :], pd[:, r, :], ACT.Silu).then_inc(silu_made, 1)
                    act.wait_ge(silu_made, i * 2 + (r + 1 + 16))
                    store_z(zml_d[i * 2 + r], r, 0)
            c.advance(unit=2 * MH, act=2 * MH, z=MH)
            for first, func in ((2 * MH, ACT.Copy), (3 * MH, ACT.Sigmoid)):
                with act.Fori(0, MH // 2) as i:
                    for r in range(2):
                        output_ready(i * 2 + (c.unit + r))
                        po_free(r, i + c.z)
                        activation(po[:, r, :], flat(bank_act(c.act + r)[:]), func).then_inc(act_free, 1)
                        act.wait_ge(act_free, i * 2 + (c.act + r + 1 + credit))
                        store_z(zml_d[i * 2 + (first + r)], r, 0)
                c.advance(unit=MH, act=MH, z=MH // 2)
            output_ready(c.unit)
            activation(ifs[:], flat(bank_act(c.act)[:]), ACT.Copy).then_inc(act_free, 1)
            c.advance(unit=1, act=1)
            act.wait_ge(act_free, c.act + credit)
            act.dma_start(if_d, ifs[0:2 * MH, :]).then_inc(store, 16)
            for r in range(2):
                act.wait_ge(z_out[r], (c.z + 1) * 16)
            act.wait_ge(store, 2 * 16)

        def rwkv():
            with act.Fori(0, NSEG) as i:
                g0, g1, g2, g3 = G
                act.wait_ge(*rw_dve.at("rho", i - 1))
                act.wait_ge(*rw_dve.at("bv", i - 1))
                act.dma_start(zs[:], zrw_d.rearrange("u p t -> p u t")[:, :, bass.ds(i * SEG, SEG)]).then_inc(zs_in, 16)
                act.wait_ge(zs_in, i * 16 + 16)
                activation(lora[0:HD, :], zs[0:HD, 12, :], ACT.Tanh).then_inc(*rw_act.sig("th"))
                activation(lora[HD:P, :], zs[HD:P, 12, :], ACT.Copy).then_inc(*rw_act.sig("ad"))
                activation(gsig[:], zs[:, 13, :], ACT.Tanh, scale=0.5).then_inc(*rw_act.sig("gt"))
                act.wait_ge(*rw_pe.at("lora", i))
                for r in range(RC):
                    last = activation(dec[:, r, 1:DEC], g0[:, 0, r * P:(r + 1) * P], ACT.Tanh, scale=0.5,
                                      bias=hw0[:, r:r + 1])
                last.then_inc(*rw_act.sig("tw"))
                for r in range(RC):
                    last = activation(ga[:, r, :], g0[:, 1, r * P:(r + 1) * P], ACT.Tanh, scale=0.5,
                                      bias=hw0[:, RC + r:RC + r + 1])
                last.then_inc(*rw_act.sig("ta"))
                act.wait_ge(*rw_pe.at("vT", i))
                activation(flat(vtok[:]), g2[:, 1, :], ACT.Copy).then_inc(*rw_act.sig("vtok"))
                act.wait_ge(*rw_dve.at("ssc", i))
                activation(flat(rinv[:]), flat(ssc[:]), ACT.Ln, scale=2.0 ** 20).then_inc(*rw_act.sig("lnn"))
                act.wait_ge(*rw_act.at("lnn", i))
                activation(flat(rinv[:]), flat(rinv[:]), ACT.Exp, scale=-0.5,
                           bias=cst[:, C_RSC:C_RSC + 1]).then_inc(*rw_act.sig("rinv"))
                act.wait_ge(*rw_dve.at("cc", i))
                activation(flat(Pp[:]), flat(dec[:]), ACT.Exp, scale=-KAPPA).then_inc(*rw_act.sig("P"))
                activation(flat(Pi[:]), flat(dec[:]), ACT.Exp, scale=KAPPA).then_inc(*rw_act.sig("Pi"))
                act.wait_ge(*rw_pe.at("gate", i))
                activation(flat(gout[:]), g1[:, 0, :], ACT.Copy).then_inc(*rw_act.sig("gev"))
                for name, step, dst, src in (("atok", "aT", atok, g0[:, 0, :]), ("btok", "bT", btok, g0[:, 1, :]),
                                             ("ktok", "kT", ktok, g3[:, 0, :])):
                    act.wait_ge(*rw_pe.at(step, i))
                    activation(flat(dst[:]), src, ACT.Copy).then_inc(*rw_act.sig(name))
                for n in range(1, LEVELS):
                    act.wait_ge(*rw_pe.at(f"W{n}", i))
                    activation(flat(Wm[:]), flat(g0[:]), ACT.Copy).then_inc(*rw_act.sig(f"Wc{n}"))
                act.wait_ge(*rw_pe.at("Z", i))
                activation(flat(Zm[:]), g3[:, 0, :], ACT.Copy).then_inc(*rw_act.sig("Zc"))
                act.wait_ge(*rw_pe.at("Wst", i))
                activation(flat(W1m[:]), g3[:, 1, :], ACT.Copy).then_inc(*rw_act.sig("W1c"))
                act.wait_ge(*rw_pe.at("U", i))
                activation(Un[:].rearrange("p (e r) v -> p e (r v)", e=2), g0[:, :, 0:RC * HD], ACT.Copy,
                           scale=-1.0).then_inc(*rw_act.sig("Un"))
                act.wait_ge(*rw_pe.at("Y", i))
                for e in range(2):
                    rows = slice(e * HD, (e + 1) * HD)
                    activation(flat(Ys[rows]), g1[rows, e, :], ACT.Copy).then_inc(*rw_act.sig(f"Y{e}"))
                act.wait_ge(*rw_dve.at("ve", i))
                activation(flat(rinv[:]), flat(ssc[:]), ACT.Ln).then_inc(*rw_act.sig("lnv"))
                act.wait_ge(*rw_act.at("lnv", i))
                activation(flat(rinv[:]), flat(rinv[:]), ACT.Exp, scale=-0.5).then_inc(*rw_act.sig("rsv"))
                act.wait_ge(*rw_dve.at("y5", i))
                act.dma_start(y_d[0:RC].rearrange("r p t -> p r t")[:, :, bass.ds(i * SEG, SEG)], yo[:]).then_inc(y_out, 16)
            act.wait_ge(y_out, (NSEG + 1) * 16)

        def mlstm_rows():
            act.dma_start(ifr[:], if_d[0:MH]).then_inc(x_in, 16)
            act.dma_start(grow[:], if_d[MH:2 * MH]).then_inc(x_in, 16)
            act.wait_ge(dve_seq, ROWS_SEQ + 1)
            activation(arow[:], grow[:], ACT.Abs).then_inc(act_seq, 1)
            act.wait_ge(act_seq, c.seq + 1)
            activation(nrow[:], arow[:], ACT.Exp, scale=-1.0).then_inc(act_seq, 1)
            act.wait_ge(act_seq, c.seq + 2)
            activation(nrow[:], nrow[:], ACT.Ln, bias=1.0).then_inc(act_seq, 1)
            c.seq += 3

        def mlstm():
            with act.Fori(0, NSEG) as i:
                g0, g1, g2, g3 = G
                act.wait_ge(*ml_dve.at("y3", i - 1))
                act.dma_start(zm[:], zml_d.rearrange("u p t -> p u t")[:, :, bass.ds(i * SEG, SEG)]).then_inc(zm_in, 16)
                activation(gst[:], grow[:, bass.ds(i * SEG, SEG)], ACT.Copy).then_inc(*ml_act.sig("gst"))
                act.wait_ge(*ml_pe.at("bce", i))
                activation(flat(Eb[:]), g0[:, 1, :], ACT.Exp).then_inc(*ml_act.sig("E"))
                act.wait_ge(*ml_pe.at("bcn", i))
                activation(flat(nmb[:]), g1[:, 0, :], ACT.Exp, scale=-1.0).then_inc(*ml_act.sig("nm"))
                act.wait_ge(*ml_pe.at("gT", i))
                activation(gtok[:], g1[:, 1, 0:MH], ACT.Copy).then_inc(*ml_act.sig("gtok"))
                act.wait_ge(*ml_pe.at("kT", i))
                activation(flat(mktok[:]), g2[:, 1, :], ACT.Copy).then_inc(*ml_act.sig("ktok"))
                act.wait_ge(*ml_pe.at("vT", i))
                activation(flat(mvtok[:]), g3[:, 0, :], ACT.Copy).then_inc(*ml_act.sig("vtok"))
                act.wait_ge(*ml_act.at("gtok", i))
                act.wait_ge(*ml_dve.at("arg", i))
                for h in range(MH):
                    last = activation(Db[:, h, :], argb[:, h, :], ACT.Exp, bias=gtok[:, h:h + 1])
                last.then_inc(*ml_act.sig("D"))
                act.wait_ge(*ml_pe.at("den", i))
                activation(flat(aden[:]), g1[:, 0, :], ACT.Abs).then_inc(*ml_act.sig("aden"))
                act.wait_ge(*ml_dve.at("ve", i))
                activation(flat(mrs[:]), flat(mve[:]), ACT.Ln).then_inc(*ml_act.sig("lnv"))
                act.wait_ge(*ml_act.at("lnv", i))
                activation(flat(mrs[:]), flat(mrs[:]), ACT.Exp, scale=-0.5).then_inc(*ml_act.sig("rsv"))
                act.wait_ge(*ml_dve.at("y3", i))
                act.dma_start(y_d[RC:KD].rearrange("r p t -> p r t")[:, :, bass.ds(i * SEG, SEG)],
                              myo[:]).then_inc(y_out, 16)
            act.wait_ge(y_out, (2 * NSEG + 1) * 16)

        def split_load(src, hi):
            with act.Fori(0, KD // 2) as i:
                for r in range(2):
                    act.wait_ge(*sp_dve.at(f"l{r}", i + (c.split - 1)))
                    act.dma_start(ysg[:, r, :], src[i * 2 + r]).then_inc(sp_in[r], 16)
                for r in range(2):
                    act.wait_ge(sp_in[r], (i + (c.split + 1)) * 16)
                    activation(hi[:, i * 2 + r, :], ysg[:, r, :], ACT.Copy).then_inc(*sp_act.sig(f"c{r}"))
            c.split += 4

        def merge():
            with act.Fori(0, KD // 2) as i:
                for r in range(2):
                    for n, dst in enumerate((sga, sgb)):
                        output_ready(i * 6 + (c.unit + 3 * r + n))
                        act.wait_ge(*(mg_dve.at("mo0", i) if r else mg_dve.at("mo1", i - 1)))
                        activation(dst[:], flat(bank_act(c.act + n)[:]), ACT.Sigmoid).then_inc(act_free, 1)
                    act.wait_ge(*mg_dve.at(f"mo{r}", i))
                    act.dma_start(merged_d[i * 2 + r], mo[:, r, :]).then_inc(z_out[r], 16)
            c.advance(unit=3 * KD, act=2 * KD, dve=2 * KD, z=KD // 2)
            for r in range(2):
                act.wait_ge(z_out[r], (c.z + 1) * 16)

        def keys_values():
            norm(memx, MEM, memq, memr[:, 0, :], memr[:, 1, :], memr[:, 2, :], memh, memhi)
            with act.Fori(0, KD // 2) as i:
                for r in range(2):
                    output_ready(i * 2 + (c.unit + r))
                    activation(kTx[:, i * 2 + r, :], bank_act(c.act + r)[:, 0, 0:MEM], ACT.Copy).then_inc(act_free, 1)
            c.advance(unit=KD, act=KD)
            with act.Fori(0, KD // 2) as i:
                for r in range(2):
                    output_ready(i * 2 + (c.unit + r))
                    activation(vx[:, :, bass.ds((i * 2 + r) * P, P)], bank_act(c.act + r)[:, :, 0:P],
                               ACT.Copy).then_inc(act_free, 1)
            c.advance(unit=KD, act=KD)

        def attend():
            with act.Fori(0, NSEG) as i:
                g0, g1, g2, g3 = G
                act.wait_ge(*xa_pe.at("S", i - 1))
                activation(qs[:], qT[:, :, bass.ds(i * SEG, SEG)], ACT.Copy).then_inc(*xa_act.sig("q"))
                act.wait_ge(*xa_dve.at("nmx", i))
                for h in range(XH):
                    last = activation(sx[:, h, :], flat(g0[:])[:, h * MEM:(h + 1) * MEM], ACT.Exp, scale=XA_SCALE,
                                      bias=mx[:, XH + h:XH + h + 1], accum_out=mx[:, 2 * XH + h:2 * XH + h + 1])
                last.then_inc(*xa_act.sig("e"))
                act.wait_ge(*xa_pe.at("T", i))
                activation(pxt[:].rearrange("p h m t -> p (h m t)"), flat(g1[:]), ACT.Copy).then_inc(*xa_act.sig("pt"))
                act.wait_ge(*xa_pe.at("O", i))
                activation(hhi[:, :, bass.ds(i * SEG, SEG)], flat(g2[:]).rearrange("p (k t) -> p k t", k=KD),
                           ACT.Copy).then_inc(*xa_act.sig("hi"))

        for dst, src in const_loads:
            act.dma_start(dst, src).then_inc(consts_in, 16)
        act.dma_start(xT[:], a["x"]).then_inc(x_in, 16)
        act.wait_ge(consts_in, CONSTS * 16)
        act.wait_ge(x_in, 16)
        ffn()
        act.wait_ge(dve_free, c.dve + credit)
        act.dma_start(x_park, xT[:]).then_inc(store, 16)
        norm_x()
        act.wait_ge(store, 16)
        barrier(act, c)
        project_rw()
        project_ml()
        barrier(act, c)
        act.dma_start(loraw[:, 0, :], a["lora_wa"]).then_inc(x_in, 16)
        act.dma_start(loraw[:, 1, :], a["lora_g"]).then_inc(x_in, 16)
        act.wait_ge(x_in, 3 * 16)
        barrier(act, c)
        rwkv()
        barrier(act, c)
        mlstm_rows()
        barrier(act, c)
        mlstm()
        barrier(act, c)
        split_load(y_d, yhi)
        merge()
        barrier(act, c)
        split_load(merged_d, hhi)
        act.dma_start(xT[:], x_park).then_inc(x_in, 16)
        c.advance(unit=KD, dve=KD)
        barrier(act, c)
        act.dma_start(memx[:], a["mem"]).then_inc(x_in, 16)
        act.wait_ge(x_in, 7 * 16)
        keys_values()
        act.wait_ge(dve_free, c.dve + credit)
        norm_x()
        barrier(act, c)
        with act.Fori(0, KD // 2) as i:
            for r in range(2):
                output_ready(i * 2 + (c.unit + r))
                activation(qT[:, i * 2 + r, :], flat(bank_act(c.act + r)[:]), ACT.Copy).then_inc(act_free, 1)
        c.advance(unit=KD, act=KD)
        barrier(act, c)
        attend()
        barrier(act, c)
        c.advance(unit=KD, dve=KD)
        ffn()
        act.wait_ge(dve_free, c.dve + credit)
        norm_x(None)
        for k in range(KD):
            act.wait_ge(dve_seq, FINAL_SEQ + k + 1)
            act.dma_start(out[k], xT[:, k, :]).then_inc(store, 16)
        act.wait_ge(store, (2 + KD) * 16)

    @block.vector
    def _(dve):
        c = Count()
        dve.sem_inc(dve_free, credit)
        dve.sem_inc(a_lo, 1)
        for s in DVE_STEPS:
            dve.sem_inc(s.sem, s.n)
        tt, ts, stt = nc.vector.tensor_tensor, nc.vector.tensor_scalar, nc.vector.scalar_tensor_tensor

        def step(ins):
            c.seq += 1
            ins.then_inc(dve_seq, 1)
            dve.wait_ge(dve_seq, c.seq)

        def output_ready(u):
            dve.wait_ge(unit_used, u + (credit + 1))

        def norm(gain, src, width, sq, ms, r, t, h, hi, lo):
            step(nc.vector.memset(t, 0.0))
            with dve.Fori(0, KD // 2) as i:
                for n in range(2):
                    dve.wait_ge(*nsq_act.at(f"sq{n}", i + c.norm))
                    dve.wait_ge(*(nsq_dve.at("add0", i + c.norm) if n else nsq_dve.at("add1", i + (c.norm - 1))))
                    tt(t, t, sq[:, n, :], ALU.add).then_inc(*nsq_dve.sig(f"add{n}"))
            dve.wait_ge(norm_sum, c.norms + 1)
            src_ps = bank_dve(c.dve)
            src_ps = flat(src_ps[:]) if width == T else src_ps[:, 0, 0:width]
            ts(ms, src_ps, 1.0 / D, EPS, ALU.mult, ALU.add).then_inc(norm_ms, 1)
            dve.wait_ge(norm_r, c.norms + 1)
            step(tt(t, r, r, ALU.mult))
            step(tt(t, t, ms, ALU.mult))
            step(ts(t, t, -0.5, 1.5, ALU.mult, ALU.add))
            step(tt(r, r, t, ALU.mult))
            dve.sem_inc(dve_free, 1)
            if hi is not None:
                with dve.Fori(0, KD // 2) as i:
                    for n in range(2):
                        dve.wait_ge(*nh_dve.at(f"l{n}", i + (c.norm - 1)))
                        col = VCOL[gain] + n
                        stt(h[:, n, :], src[:, i * 2 + n, :], vec[:, bass.ds(i * 2 + col, 1)], r, ALU.mult,
                            ALU.mult).then_inc(*nh_dve.sig(f"h{n}"))
                    for n in range(2):
                        dve.wait_ge(*nh_act.at(f"c{n}", i + c.norm))
                        tt(lo[:, i * 2 + n, :], h[:, n, :], hi[:, i * 2 + n, :].bitcast(F32),
                           ALU.subtract).then_inc(*nh_dve.sig(f"l{n}"))
            c.advance(norm=4, norms=1, dve=1)

        def norm_x(gain, hi=hhi):
            norm(gain, xT, T, nsq, nms[:], nr[:], nt[:], nh, hi, hlo)

        def residual(scale):
            with dve.Fori(0, KD // 2) as i:
                for r in range(2):
                    output_ready(i * 2 + (c.unit + r))
                    x_ = xT[:, i * 2 + r, :]
                    stt(x_, flat(bank_dve(c.dve + r)[:]), scale, x_, ALU.mult, ALU.add).then_inc(dve_free, 1)
            c.advance(unit=KD, dve=KD)

        def ffn(gain):
            dve.wait_ge(dve_free, c.dve + credit)
            norm_x(gain)
            for n in FF_PARTS:
                with loop(dve, n // 2) as i:
                    for r in range(2):
                        dve.wait_ge(act_free, i * 2 + (c.act + r + 1 + credit))
                        output_ready(i * 4 + (c.unit + 2 * r + 1))
                        dve.wait_ge(a_lo, i * 2 + (c.a + r + 1))
                        tt(s1[:], s0[:], flat(bank_dve(c.dve + r)[:]), ALU.mult).then_inc(dve_free, 1)
                        dve.wait_ge(a_hi, i * 2 + (c.a + r + 1))
                        tt(alo[:, i * 2 + r, :], s1[:], ahi[:, i * 2 + r, :].bitcast(F32),
                           ALU.subtract).then_inc(a_lo, 1)
                c.advance(unit=2 * n, act=n, dve=n, a=n)
                residual(0.5)

        def project_rw():
            with dve.Fori(0, RW_UNITS // 2) as i:
                for r in range(2):
                    dve.wait_ge(act_free, i * 2 + (c.act + r + 1 + credit))
                    tt(pd[:, r, :], stg[:, r, 2:2 + T], stg[:, r, 3:3 + T], ALU.subtract).then_inc(*rp_dve.sig(f"d{r}"))
                    dve.wait_ge(*rp_dve.at(f"d{r}", i))
                    dve.wait_ge(z_out[r], (i + 1) * 16)
                    stt(po[:, r, :], pd[:, r, :], vec[:, bass.ds(i * 2 + (VCOL["rw_mu"] + r), 1)], stg[:, r, 3:3 + T],
                        ALU.mult, ALU.add).then_inc(*rp_dve.sig(f"m{r}"))
            c.advance(unit=RW_UNITS, act=RW_UNITS)

        def project_ml():
            with dve.Fori(0, MH) as i:
                for r in range(2):
                    dve.wait_ge(act_free, i * 2 + (c.act + r + 1 + credit))

                    def w(name):
                        return vec[:, bass.ds(i * 2 + (VCOL[name] + r), 1)]

                    dve.wait_ge(silu_made, i * 2 + 16)
                    ts(pd[:, r, :], stg[:, r, 3:3 + T], w("conv_w0"), w("conv_b"), ALU.mult,
                       ALU.add).then_inc(*cv_dve.sig(f"t0{r}"))
                    for j in range(1, 4):
                        dve.wait_ge(*cv_dve.at(f"t{j - 1}{r}", i))
                        stt(pd[:, r, :], stg[:, r, 3 - j:3 - j + T], w(f"conv_w{j}"), pd[:, r, :], ALU.mult,
                            ALU.add).then_inc(*cv_dve.sig(f"t{j}{r}"))
            c.advance(unit=ML_UNITS + 1, act=ML_UNITS + 1)

        def newton(S, names, r, v, w, i):
            tt(flat(w[:]), flat(r[:]), flat(r[:]), ALU.mult).then_inc(*S.sig(names[0]))
            dve.wait_ge(*S.at(names[0], i))
            tt(flat(w[:]), flat(w[:]), flat(v[:]), ALU.mult).then_inc(*S.sig(names[1]))
            dve.wait_ge(*S.at(names[1], i))
            ts(flat(w[:]), flat(w[:]), -0.5, 1.5, ALU.mult, ALU.add).then_inc(*S.sig(names[2]))
            dve.wait_ge(*S.at(names[2], i))
            tt(flat(r[:]), flat(r[:]), flat(w[:]), ALU.mult).then_inc(*S.sig(names[3]))
            dve.wait_ge(*S.at(names[3], i))

        def rwkv():
            S = rw_dve
            with dve.Fori(0, NSEG) as i:
                g0, g1, g2, g3 = G

                def mine(name):
                    dve.wait_ge(*S.at(name, i))

                def copies(col, n):
                    return con(col).unsqueeze(1).to_broadcast([P, n, P])

                dve.wait_ge(zs_in, i * 16 + 16)
                dve.wait_ge(*rw_act.at("gt", i))
                ts(gsig[:], gsig[:], 0.5, 0.5, ALU.mult, ALU.add).then_inc(*S.sig("gs"))
                tt(kkr[:], zs[:, 4:8, :], vbc("rw_k_k", SEG), ALU.mult).then_inc(*S.sig("kkr"))
                mine("kkr")
                tt(ksq[:], kkr[:], kkr[:], ALU.mult).then_inc(*S.sig("sq"))
                dve.wait_ge(*rw_act.at("tw", i))
                ts(dec[:, :, 1:DEC], dec[:, :, 1:DEC], 1.0, None, ALU.add).then_inc(*S.sig("dec"))
                mine("dec")
                nc.vector.tensor_tensor_scan(flat(cum[:]), con(C_RST, RC * DEC), flat(dec[:]), 0.0, ALU.mult,
                                             ALU.add).then_inc(*S.sig("scan"))
                mine("scan")
                ts(hend[:], cum[:, :, DEC - 1:DEC], 0.5, None, ALU.mult).then_inc(*S.sig("hend"))
                mine("hend")
                tt(dec[:], cum[:], hend[:].to_broadcast([P, RC, DEC]), ALU.subtract).then_inc(*S.sig("cc"))
                dve.wait_ge(*rw_act.at("ta", i))
                ts(ga[:], ga[:], 0.5, 0.5, ALU.mult, ALU.add).then_inc(*S.sig("av"))
                mine("av")
                ts(gu[:], ga[:], -1.0, None, ALU.add).then_inc(*S.sig("u1"))
                mine("u1")
                tt(gu[:], gu[:], vbc("rw_k_a", SEG), ALU.mult).then_inc(*S.sig("u2"))
                mine("u2")
                stt(flat(kmod[:]), flat(gu[:]), 1.0, zs[:, 4:8, :].rearrange("p r t -> p (r t)"), ALU.add,
                    ALU.mult).then_inc(*S.sig("kmod"))
                mine("kmod")
                tt(rkb[:], zs[:, 0:4, :], kmod[:], ALU.mult).then_inc(*S.sig("rk"))
                mine("rk")
                tt(rkb[:], rkb[:], vbc("rw_r_k", SEG), ALU.mult).then_inc(*S.sig("rkb"))
                dve.wait_ge(*rw_pe.at("ss", i))
                ts(flat(ssc[:]), g1[:, 1, :], 1e-24, None, ALU.max).then_inc(*S.sig("ssc"))
                dve.wait_ge(*rw_act.at("rinv", i))
                newton(S, ("n1", "n2", "n3", "rin"), rinv, ssc, nw, i)
                tt(kk[:], kkr[:], rinv[:], ALU.mult).then_inc(*S.sig("kk"))
                dve.wait_ge(*rw_pe.at("bonus", i))
                tt(bv[:], g2[:, 0, :].rearrange("p (r t) -> p r t", r=RC), zs[:, 8:12, :], ALU.mult).then_inc(*S.sig("bv"))
                mine("kk")
                tt(kka[:], kk[:], ga[:], ALU.mult).then_inc(*S.sig("kka"))
                dve.wait_ge(*rw_act.at("Pi", i))
                tt(alpha[:], kk[:], Pp[:, :, 0:SEG], ALU.mult).then_inc(*S.sig("alpha"))
                mine("kka")
                tt(beta[:], kka[:], Pi[:, :, 1:DEC], ALU.mult).then_inc(*S.sig("beta"))
                tt(kap[:], kmod[:], Pi[:, :, 1:DEC], ALU.mult).then_inc(*S.sig("kap"))
                tt(rho[:], zs[:, 0:4, :], Pp[:, :, 1:DEC], ALU.mult).then_inc(*S.sig("rho"))
                dve.wait_ge(*rw_pe.at("A", i))
                tt(S0s[:], St[:], Pi[:, :, 0:1].to_broadcast([P, RC, HD]), ALU.mult).then_inc(*S.sig("S0s"))

                def gram(name, dst, src, mask):
                    nc.vector.copy_predicated(dst[:], copies(mask, NH).bitcast(U32),
                                              flat(src[:]).rearrange("p (n t) -> p n t", n=NH)).then_inc(*S.sig(name))

                gram("A", Am, g1, C_LOW)
                mine("A")
                tt(AL[:], Am[:], copies(C_LEV, NH), ALU.mult).then_inc(*S.sig("am0"))
                mine("am0")
                tt(Tm[:], copies(C_ID, NH), AL[:], ALU.subtract).then_inc(*S.sig("T0"))
                dve.wait_ge(*rw_pe.at("am1T", i))
                tt(Um[:], copies(C_ID, NH), flat(g1[:]).rearrange("p (n t) -> p n t", n=NH),
                   ALU.subtract).then_inc(*S.sig("U0"))
                for n in range(1, LEVELS):
                    mine(f"U{n - 1}")
                    tt(AL[:], Am[:], copies(C_LEV + n * P, NH), ALU.mult).then_inc(*S.sig(f"am{n}"))
                    if n == 1:
                        gram("Mv", Mv, g0, C_UPEQ)
                        gram("Mu", Mu, g2, C_UPEQ)
                        gram("B", Bm, g3, C_UP)
                    dve.wait_ge(*rw_pe.at(f"E{n}", i))
                    if n < LEVELS - 1:
                        tt(flat(Tm[:]), flat(Tm[:]), flat(g1[:]), ALU.subtract).then_inc(*S.sig(f"T{n}"))
                    tt(flat(Um[:]), flat(Um[:]), flat(g2[:]), ALU.subtract).then_inc(*S.sig(f"U{n}"))
                dve.wait_ge(*rw_pe.at("dS", i))
                tt(St[:], S0s[:], g3[:, 0, 0:RC * HD].rearrange("p (r v) -> p r v", r=RC), ALU.add).then_inc(*S.sig("dS"))
                mine("dS")
                tt(St[:], St[:], Pp[:, :, DEC - 1:DEC].to_broadcast([P, RC, HD]), ALU.mult).then_inc(*S.sig("S"))
                dve.wait_ge(*rw_act.at("Y1", i))
                dve.wait_ge(*rw_pe.at("mean", i))
                stt(flat(Ys[:]), g2[:, 0, :], -1.0 / HD, flat(Ys[:]), ALU.mult, ALU.add).then_inc(*S.sig("yc"))
                mine("yc")
                tt(ksq[:], Ys[:], Ys[:], ALU.mult).then_inc(*S.sig("ysq"))
                dve.wait_ge(*rw_pe.at("var", i))
                ts(flat(ssc[:]), g2[:, 1, :], 1.0 / HD, GN_EPS, ALU.mult, ALU.add).then_inc(*S.sig("ve"))
                dve.wait_ge(*rw_act.at("rsv", i))
                newton(S, ("g1", "g2", "g3", "g4"), rinv, ssc, nw, i)
                tt(Ys[:], Ys[:], rinv[:], ALU.mult).then_inc(*S.sig("y1"))
                mine("y1")
                tt(Ys[:], Ys[:], vbc("rw_gn_w", SEG), ALU.mult).then_inc(*S.sig("y2"))
                mine("y2")
                tt(Ys[:], Ys[:], vbc("rw_gn_b", SEG), ALU.add).then_inc(*S.sig("y3"))
                mine("y3")
                tt(Ys[:], Ys[:], bv[:], ALU.add).then_inc(*S.sig("y4"))
                mine("y4")
                dve.wait_ge(y_out, (i + 1) * 16)
                tt(yo[:], Ys[:], gout[:], ALU.mult).then_inc(*S.sig("y5"))

        def mlstm_rows():
            assert c.seq == ROWS_SEQ, c.seq
            dve.wait_ge(x_in, 5 * 16)
            step(ts(grow[:], grow[:], gbias[:, 1:2], None, ALU.add))
            step(ts(ifr[:], ifr[:], gbias[:, 0:1], None, ALU.add))
            step(ts(brow[:], grow[:], 0.0, None, ALU.min))
            dve.wait_ge(act_seq, ROWS_ACT + 3)
            step(tt(brow[:], brow[:], nrow[:], ALU.subtract))
            step(nc.vector.tensor_tensor_scan(mrow[:], brow[:], ifr[:], 0.0, ALU.add, ALU.max))
            for n in range(NSEG):
                cols = slice(n * SEG, (n + 1) * SEG)
                step(nc.vector.tensor_tensor_scan(arow[:, cols], con(C_ONES, P, MH), brow[:, cols], 0.0, ALU.mult,
                                                  ALU.add))
            step(tt(grow[:], ifr[:], arow[:], ALU.subtract))
            step(tt(arow[:], arow[:], mrow[:], ALU.subtract))
            step(nc.vector.tensor_copy(erow[:, 0:SEG], arow[:, 0:SEG]))
            before = mrow[:].rearrange("p (n t) -> p n t", n=NSEG)[:, 0:NSEG - 1, SEG - 1:SEG]
            step(tt(erow[:, SEG:T].rearrange("p (n t) -> p n t", n=NSEG - 1),
                    arow[:, SEG:T].rearrange("p (n t) -> p n t", n=NSEG - 1),
                    before.to_broadcast([MH, NSEG - 1, SEG]), ALU.add))
            step(nc.vector.memset(CN[:], 0.0))

        def mlstm():
            S = ml_dve
            with dve.Fori(0, NSEG) as i:
                g0, g1, g2, g3 = G

                def mine(name):
                    dve.wait_ge(*S.at(name, i))

                def heads(ap):
                    return ap.rearrange("p (h t) -> p h t", h=MH)

                dve.wait_ge(*ml_pe.at("bca", i))
                tt(argb[:], heads(g0[:, 0, :]), con(C_ADD).unsqueeze(1).to_broadcast([P, MH, SEG]),
                   ALU.add).then_inc(*S.sig("arg"))
                dve.wait_ge(*ml_act.at("D", i))
                dve.wait_ge(*ml_pe.at("S", i))
                stt(flat(Pb[:]), g2[:, 0, :], ML_SCALE, flat(Db[:]), ALU.mult, ALU.mult).then_inc(*S.sig("P"))
                dve.wait_ge(zm_in, i * 16 + 16)
                stt(flat(qe[:]), zm[:, 0:MH, :].rearrange("p h t -> p (h t)"), ML_SCALE, flat(Eb[:]), ALU.mult,
                    ALU.mult).then_inc(*S.sig("qe"))
                tt(kw[:], mktok[:], Db[:, :, SEG - 1:SEG].to_broadcast([P, MH, SEG]), ALU.mult).then_inc(*S.sig("kw"))
                dve.wait_ge(*ml_act.at("aden", i))
                tt(aden[:], aden[:], nmb[:], ALU.max).then_inc(*S.sig("dmax"))
                mine("dmax")
                nc.vector.reciprocal(flat(aden[:]), flat(aden[:])).then_inc(*S.sig("rec"))
                mine("rec")
                tt(flat(hm[:]), g3[:, 1, :], flat(aden[:]), ALU.mult).then_inc(*S.sig("hm"))
                tt(CNd[:], CN[:], Eb[:, :, SEG - 1:SEG].unsqueeze(1).to_broadcast([P, 2, MH, SEG]),
                   ALU.mult).then_inc(*S.sig("dec"))
                mine("dec")
                dve.wait_ge(*ml_pe.at("dN", i))
                tt(CN[:].rearrange("p a h t -> p (a h t)"), CNd[:].rearrange("p a h t -> p (a h t)"), flat(g2[:]),
                   ALU.add).then_inc(*S.sig("C"))
                dve.wait_ge(*ml_pe.at("mean", i))
                stt(flat(hm[:]), g0[:, 0, :], -1.0 / P, flat(hm[:]), ALU.mult, ALU.add).then_inc(*S.sig("yc"))
                mine("yc")
                tt(mysq[:], hm[:], hm[:], ALU.mult).then_inc(*S.sig("ysq"))
                dve.wait_ge(*ml_pe.at("var", i))
                ts(flat(mve[:]), g0[:, 1, :], 1.0 / P, ML_EPS, ALU.mult, ALU.add).then_inc(*S.sig("ve"))
                dve.wait_ge(*ml_act.at("rsv", i))
                newton(S, ("g1", "g2", "g3", "g4"), mrs, mve, mnw, i)
                tt(hm[:], hm[:], mrs[:], ALU.mult).then_inc(*S.sig("y1"))
                mine("y1")
                tt(hm[:], hm[:], vbc("ml_norm", SEG), ALU.mult).then_inc(*S.sig("y2"))
                mine("y2")
                dve.wait_ge(y_out, (i + (NSEG + 1)) * 16)
                tt(myo[:], hm[:], zm[:, 12:16, :], ALU.mult).then_inc(*S.sig("y3"))

        def split_load(hi, lo):
            with dve.Fori(0, KD // 2) as i:
                for r in range(2):
                    dve.wait_ge(*sp_act.at(f"c{r}", i + c.split))
                    tt(lo[:, i * 2 + r, :], ysg[:, r, :], hi[:, i * 2 + r, :].bitcast(F32),
                       ALU.subtract).then_inc(*sp_dve.sig(f"l{r}"))
            c.split += 4

        def merge():
            with dve.Fori(0, KD // 2) as i:
                for r in range(2):
                    output_ready(i * 6 + (c.unit + 3 * r + 2))
                    dve.wait_ge(act_free, i * 4 + (c.act + 2 * r + 2 + credit))
                    dve.wait_ge(z_out[r], (i + (c.z + 1)) * 16)
                    tt(mo[:, r, :], sga[:], flat(bank_dve(c.dve)[:]), ALU.mult).then_inc(dve_free, 1)
                    tt(sgb[:], sgb[:], flat(bank_dve(c.dve + 1)[:]), ALU.mult).then_inc(dve_free, 1)
                    dve.wait_ge(dve_free, i * 4 + (c.dve + 2 * r + 2 + credit))
                    tt(mo[:, r, :], mo[:, r, :], sgb[:], ALU.add).then_inc(*mg_dve.sig(f"mo{r}"))
            c.advance(unit=3 * KD, act=2 * KD, dve=2 * KD)

        def attend():
            S = xa_dve
            with dve.Fori(0, NSEG) as i:
                g0, g1, g2, g3 = G
                dve.wait_ge(*xa_pe.at("S", i))
                nc.vector.reduce_max(mx[:, 0:XH], flat(g0[:]).rearrange("p (h m) -> p h m", h=XH),
                                     AX_X).then_inc(*S.sig("mx"))
                dve.wait_ge(*S.at("mx", i))
                ts(mx[:, XH:2 * XH], mx[:, 0:XH], -XA_SCALE, None, ALU.mult).then_inc(*S.sig("nmx"))
                dve.wait_ge(*xa_act.at("e", i))
                nc.vector.reciprocal(mx[:, 3 * XH:4 * XH], mx[:, 2 * XH:3 * XH]).then_inc(*S.sig("r"))
                dve.wait_ge(*S.at("r", i))
                tt(px[:], sx[:], mx[:, 3 * XH:4 * XH].unsqueeze(2).to_broadcast([P, XH, MEM]),
                   ALU.mult).then_inc(*S.sig("p"))
                dve.wait_ge(*xa_act.at("hi", i))
                cols = bass.ds(i * SEG, SEG)
                tt(hlo[:, :, cols], flat(g2[:]).rearrange("p (k t) -> p k t", k=KD), hhi[:, :, cols].bitcast(F32),
                   ALU.subtract).then_inc(*S.sig("lo"))

        dve.wait_ge(consts_in, CONSTS * 16)
        dve.wait_ge(x_in, 16)
        step(ts(hw0[:], vec[:, VCOL["rw_w0"]:VCOL["rw_w0"] + 2 * RC], 0.5, None, ALU.mult))
        ffn("ffn1_norm")
        dve.wait_ge(dve_free, c.dve + credit)
        norm_x("mix_norm")
        barrier(dve, c)
        for r in range(2):
            step(nc.vector.memset(stg[:, r, 0:3], 0.0))
        project_rw()
        c.z = RW_UNITS // 2 + MH + MH // 2 * 2
        project_ml()
        barrier(dve, c)
        for m in (Am, Bm, Mv, Mu, St, dec):
            step(nc.vector.memset(m[:], 0.0))
        barrier(dve, c)
        rwkv()
        barrier(dve, c)
        mlstm_rows()
        barrier(dve, c)
        mlstm()
        barrier(dve, c)
        split_load(yhi, ylo)
        merge()
        barrier(dve, c)
        split_load(hhi, hlo)
        dve.wait_ge(x_in, 6 * 16)
        residual(1.0)
        barrier(dve, c)
        dve.wait_ge(x_in, 7 * 16)
        norm("mem_norm", memx, MEM, memq, memr[:, 0, :], memr[:, 1, :], memr[:, 2, :], memh, memhi, memlo)
        c.advance(unit=2 * KD, act=2 * KD)
        norm_x("xa_norm")
        barrier(dve, c)
        c.advance(unit=KD, act=KD)
        barrier(dve, c)
        attend()
        barrier(dve, c)
        residual(1.0)
        ffn("ffn2_norm")
        dve.wait_ge(dve_free, c.dve + credit)
        norm_x("final_norm", None)
        assert c.seq == FINAL_SEQ, c.seq
        for k in range(KD):
            x_ = xT[:, k, :]
            stt(x_, x_, v1("final_norm", k), nr[:], ALU.mult, ALU.mult).then_inc(dve_seq, 1)

    ctx.close()


def constants():
    c = np.zeros((P, NCONST), np.float32)
    p, f = np.arange(P)[:, None], np.arange(P)[None, :]
    c[:, C_ID:C_ID + P] = p == f
    c[:, C_ONES:C_ONES + P] = 1
    c[:, C_HONES:C_HONES + P] = p // HD == f // HD
    c[:, C_LOW:C_LOW + P] = f < p
    c[:, C_UP:C_UP + P] = p < f
    c[:, C_UPEQ:C_UPEQ + P] = p <= f
    for n in range(LEVELS):
        b = 1 << n
        c[:, C_LEV + n * P:C_LEV + (n + 1) * P] = (p // (2 * b) == f // (2 * b)) & (p // b % 2 == 1) & (f // b % 2 == 0)
    c[:, C_ADD:C_ADD + P] = np.where(p <= f, 0.0, -1e30)
    c[:, C_RST:C_RST + RC * DEC] = np.arange(RC * DEC) % DEC != 0
    for h in range(MH):
        c[h, C_SEL + h * P:C_SEL + (h + 1) * P] = 1
    c[:, C_RSC] = 10 * np.log(2.0)
    return c


def kernel(**inputs):
    import concourse.bacc as bacc
    from concourse.bass_utils import run_bass_kernel_spmd

    g = {k: np.asarray(v) for k, v in inputs.items()}

    def units(w):
        k, n = w.shape[0] // P, w.shape[1] // P
        return np.ascontiguousarray(w.reshape(k, P, n, P).transpose(2, 1, 0, 3).reshape(n, P, k * P))

    def cols(v):
        return v.reshape(-1, P).T

    arrays = {}
    for f in ("ffn1", "ffn2"):
        n = f[-1]
        arrays[f"wg{n}"] = units(g[f"{f}_w_gate"][0])
        arrays[f"wu{n}"] = units(g[f"{f}_w_up"][0])
        at = 0
        for part, c in enumerate(FF_PARTS):
            arrays[f"wd{n}_{part}"] = units(g[f"{f}_w_down"][0][at * P:(at + c) * P])
            at += c
    w_in = g["w_in"][0]
    rw, mlc = RW_UNITS * P, ML_UNITS * P
    arrays["rw_in"] = units(w_in[:, :rw])
    arrays["ml_in"] = units(w_in[:, rw:rw + mlc])
    wif = np.zeros((D, P), np.float32)
    wif[:, :2 * MH] = w_in[:, rw + mlc:rw + mlc + 2 * MH]
    arrays["if_in"] = units(wif)
    gates = rw + mlc + 2 * MH
    arrays["ga_in"] = units(w_in[:, gates:gates + D])
    arrays["gb_in"] = units(w_in[:, gates + D:])
    arrays["up"] = units(np.concatenate([g["w_up_rw"][0], g["w_up_ml"][0]], axis=0))
    arrays["w_out"] = units(g["w_out"][0])
    arrays["wq"] = units(g["xa_wq"][0])
    arrays["wkv"] = units(g["xa_wkv"][0])
    arrays["wo"] = units(g["xa_wo"][0])
    arrays["lora_wa"] = np.concatenate([g["rw_w2"][0], g["rw_a2"][0]], axis=0)
    arrays["lora_g"] = np.ascontiguousarray(g["rw_g2"][0])
    arrays["x"] = np.ascontiguousarray(g["x"][0].T.reshape(KD, P, T).transpose(1, 0, 2))
    arrays["mem"] = np.ascontiguousarray(g["mem"][0].T.reshape(KD, P, MEM).transpose(1, 0, 2))
    vecs = {n: g[n] if n == "final_norm" else g[n][0] for n, _ in VECS if n in g}
    for j in range(4):
        vecs[f"conv_w{j}"] = g["ml_conv_w"][0, j]
    vecs["conv_b"] = g["ml_conv_b"][0]
    arrays["vecs"] = np.ascontiguousarray(np.concatenate([cols(vecs[n].reshape(-1)) for n, _ in VECS], axis=1))
    arrays["gate_b"] = np.ascontiguousarray(np.stack([g["ml_i_b"][0], g["ml_f_b"][0]], axis=1))
    arrays["consts"] = constants()

    nc = bacc.Bacc("TRN2", target_bir_lowering=False, num_devices=1)
    aps = {n: nc.dram_tensor(f"in_{n}", v.shape, F32, kind="ExternalInput").ap() for n, v in arrays.items()}
    out = nc.dram_tensor("out", [KD, P, T], F32, kind="ExternalOutput").ap()
    layer_kernel(nc, aps, out)
    res = run_bass_kernel_spmd(nc, [{f"in_{n}": v for n, v in arrays.items()}], core_ids=[0])
    return res.results[0]["out"].reshape(D, T).T.reshape(1, T, D)
```

```python
from contextlib import ExitStack, nullcontext

import numpy as np

import concourse.bass as bass
from concourse import mybir

P = 128
D = 1024
T = 1024
KD = D // P
HALF = 512
NHALF = T // HALF
MEM = 256
FF = 2816
FFC = FF // P
FF_PARTS = (8, 8, 6)
SEG = 128
NSEG = T // SEG
NH = 8
HD = 64
RC = 4
MH = 4
XH = 4
RW_UNITS = 14
ML_UNITS = 16
LEVELS = 7
DEC = SEG + 1

EPS = 1e-5
GN_EPS = 64e-5
ML_EPS = 1e-6
KAPPA = float(np.exp(-0.5)) / 2
ML_SCALE = P ** -0.5
XA_SCALE = (D // XH) ** -0.5

ALU = mybir.AluOpType
ACT = mybir.ActivationFunctionType
F32 = mybir.dt.float32
F32R = mybir.dt.float32r
U32 = mybir.dt.uint32
AX_X = mybir.AxisListType.X

C_ID, C_ONES, C_HONES, C_LOW, C_UP, C_UPEQ, C_LEV = (n * P for n in range(7))
C_ADD = C_LEV + LEVELS * P
C_RST = C_ADD + P
C_SEL = C_RST + RC * DEC
C_RSC = C_SEL + MH * P
C_ZERO = C_RSC + 1
NCONST = C_ZERO + 1
CONSTS = 3

VECS = [("ffn1_norm", 8), ("mix_norm", 8), ("xa_norm", 8), ("mem_norm", 8), ("ffn2_norm", 8), ("final_norm", 8),
        ("rw_mu", 14), ("rw_w0", 4), ("rw_a0", 4), ("rw_k_k", 4), ("rw_k_a", 4), ("rw_r_k", 4), ("rw_gn_w", 4),
        ("rw_gn_b", 4), ("conv_w0", 8), ("conv_w1", 8), ("conv_w2", 8), ("conv_w3", 8), ("conv_b", 8),
        ("ml_norm", 4)]
VCOL = {}
NVEC = 0
for _n, _w in VECS:
    VCOL[_n] = NVEC
    NVEC += _w


class Steps:

    def __init__(self, sem, names):
        self.sem, self.names, self.n = sem, names, len(names)
        self.where = {name: k + 1 for k, name in enumerate(names)}
        self.next = 0
        assert len(self.where) == self.n

    def sig(self, name):
        assert self.names[self.next % self.n] == name, (name, self.names[self.next % self.n])
        self.next += 1
        return self.sem, 1

    def at(self, name, it):
        return self.sem, (it + 1) * self.n + self.where[name]


F_PE = (["lora", "ss", "vT", "bonus", "aT", "bT", "kT", "A", "Mu", "am0T", "B", "W1", "Mv", "E1"]
        + [x for n in range(2, LEVELS) for x in (f"W{n}", f"V{n - 1}", f"E{n}")]
        + ["F", f"V{LEVELS - 1}", "UQ", "gate", "Z", "Wst"])
F_ACT = (["th", "ad", "gt", "tw", "ta", "P", "Pi", "lnn", "rinv", "vtok", "atok", "btok", "ktok", "Wc1"]
         + [x for n in range(2, LEVELS) for x in (f"Wc{n}", f"Tc{n - 1}")] + [f"Tc{LEVELS - 1}", "gev", "Zc", "W1c"])
F_DVE = (["gs", "dec", "scan", "hend", "cc", "av", "gu", "kmod", "ssc", "n1", "n2", "n3", "rin", "kk", "kka", "bv",
          "alpha", "beta", "pend", "A", "am0", "Mu", "U0", "B", "U1", "S0s", "Mv"]
         + [f"U{n}" for n in range(2, LEVELS)] + ["Q", "Uf"])
F_POOL = ["kkr", "sq", "rk", "rkb", "kap", "rho", "T0"] + [f"am{n}" for n in range(1, LEVELS)] + ["IU"]
B_PE = ["U", "Y", "dS", "mean", "var"]
B_ACT = ["Un", "Y0", "Y1", "lnv", "rsv"]
B_DVE = ["dS", "S", "yc", "ve", "g1", "g2", "g3", "g4", "y1"]
B_POOL = ["bvb", "ysq", "y2", "y3", "y4"]
M_PE = ["bca", "bce", "bcn", "gT", "kT", "vT", "S", "num", "den", "dC", "dN", "mean", "var"]
M_ACT = ["gst", "E", "nm", "gtok", "ktok", "vtok", "D", "aden", "lnv", "rsv"]
M_DVE = ["arg", "P", "qe", "dmax", "rec", "hm", "C", "yc", "ve", "g1", "g2", "g3", "g4", "y1"]
M_POOL = ["kw", "dec", "ysq", "y2", "y3"]
XA_PE = ["S", "T", "O"]
XA_ACT = ["q", "e", "pt", "hi"]
XA_DVE = ["mx", "nmx", "r", "p", "lo"]


ROWS_SEQ, ROWS_ACT, FINAL_SEQ = 13, 2, 58


def layer_kernel(nc, a, out):
    ctx = ExitStack()
    sems = {}

    def sem(name):
        if name not in sems:
            sems[name] = ctx.enter_context(nc.semaphore(name))
        return sems[name]

    def dram(name, shape):
        return nc.dram_tensor(name, shape, F32, kind="Internal").ap()

    x_park = dram("x_park", [P, KD, T])
    zrw_d = dram("zrw_d", [RW_UNITS, P, T])
    zml_d = dram("zml_d", [ML_UNITS, P, T])
    gates_d = dram("gates_d", [2, KD, P, T])
    y_d = dram("y_d", [KD, P, T])

    base = (nc.sbuf_base + 63) // 64 * 64
    end = nc.sbuf_usable_end
    top = {}

    def place(group, after, name, shape, dt=F32):
        at = top.get(group, top[after] if after else base)
        size = int(np.prod(shape[1:])) * 4
        top[group] = at + (size + 63) // 64 * 64
        assert top[group] <= end, (group, name, top[group] - end)
        return nc.alloc_sbuf_tensor_at(name, shape, dt, offset=at)

    cst = place("small", None, "cst", [P, NCONST])
    vec = place("small", None, "vec", [P, NVEC])
    hw0 = place("small", None, "hw0", [P, 2 * RC])
    gbias = place("small", None, "gbias", [MH, 2])
    raw = place("common", "small", "raw", [P, 2, KD * P])
    whi = place("common", "small", "whi", [P, 2, KD * P], F32R)
    wlo = place("common", "small", "wlo", [P, 2, KD * P], F32R)
    hhi = place("common", "small", "hhi", [P, KD, T], F32R)
    hlo = place("common", "small", "hlo", [P, KD, T], F32R)
    xT = place("x", "common", "xT", [P, KD, T])
    ahi = place("ffn", "x", "ahi", [P, max(FF_PARTS), T], F32R)
    alo = place("ffn", "x", "alo", [P, max(FF_PARTS), T], F32R)
    s0 = nc.alloc_sbuf_tensor_at("s0", [P, T], F32, offset=end // 64 * 64 - 8192)
    s1 = nc.alloc_sbuf_tensor_at("s1", [P, T], F32, offset=end // 64 * 64 - 4096)
    assert top["ffn"] <= end // 64 * 64 - 8192, top["ffn"] - end
    def at_x(name, kib, shape):
        at = top["x"] + kib * 1024
        assert at + int(np.prod(shape[1:])) * 4 <= end
        return nc.alloc_sbuf_tensor_at(name, shape, F32, offset=at)

    nh = at_x("nh", 0, [P, 2, T])
    nr = at_x("nr", 8, [P, T])
    nsq = at_x("nsq", 24, [P, 2, T])
    nt = at_x("nt", 56, [P, T])
    nms = at_x("nms", 60, [P, T])
    stg = place("proj", "common", "stg", [P, 2, T + 3])
    pd = place("proj", "common", "pd", [P, 2, T])
    po = place("proj", "common", "po", [P, 2, T])
    ifs = place("proj", "common", "ifs", [P, T])
    zs = place("mix", "small", "zs", [P, RW_UNITS, SEG])
    loraw = place("mix", "small", "loraw", [P, 2, RC * P])
    lora = place("mix", "small", "lora", [P, SEG])
    gsig = place("mix", "small", "gsig", [P, SEG])
    dec, cum, Pp, Pi = (place("mix", "small", n, [P, RC, DEC]) for n in ("dec", "cum", "Pp", "Pi"))
    hend, pend = (place("mix", "small", n, [P, RC, 1]) for n in ("hend", "pend"))
    idr = place("mix", "small", "idr", [P, P], F32R)

    def mix(name, shape=(P, RC, SEG), dt=F32):
        return place("mix", "small", name, list(shape), dt)

    kk, ksq, rkb, ssc, rinv, nw, ga, kmod, alpha, beta, kap, rho, gout, bv, atok, btok, ktok, vtok, W1m = (
        mix(n) for n in ("kk", "ksq", "rkb", "ssc", "rinv", "nw", "ga", "kmod", "alpha", "beta", "kap", "rho", "gout",
                         "bv", "atok", "btok", "ktok", "vtok", "W1m"))
    gu, kka = rkb, nw
    Am, Bm, Mv, Mu, Uf = (mix(n, (P, NH, SEG)) for n in ("Am", "Bm", "Mv", "Mu", "Uf"))
    Ur, Tr, Wr, Qr = (mix(n, (P, NH, SEG), F32R) for n in ("Ur", "Tr", "Wr", "Qr"))
    AL = mix("AL", (P, 2, NH, SEG), F32R)
    Zm, Un = mix("Zm", (P, NH, HD)), mix("Un", (P, NH, HD))
    St, S0s = mix("St", (P, RC, HD)), mix("S0s", (P, RC, HD))
    Ys, ysq, yve, yrs, bvb, yo = (mix(n) for n in ("Ys", "ysq", "yve", "yrs", "bvb", "yo"))
    ynw = ysq
    zm = mix("zm", (P, ML_UNITS, SEG))
    gst, gtok = mix("gst", (MH, SEG)), mix("gtok", (P, MH))
    Eb, nmb, Db, Pb, qe, kw, mktok, mvtok, aden, hm, myo = (mix(n) for n in (
        "Eb", "nmb", "Db", "Pb", "qe", "kw", "mktok", "mvtok", "aden", "hm", "myo"))
    argb, mysq, mve, mrs, mnw = hm, Pb, qe, nmb, aden
    CN = mix("CN", (P, 2, MH, SEG))
    ifr, brow, nrow, mrow, arow, erow, grow = (
        nc.alloc_sbuf_tensor_at(n, [MH, T], F32, offset=end // 64 * 64 - (7 - k) * 4096)
        for k, n in enumerate(("ifr", "brow", "nrow", "mrow", "arow", "erow", "grow")))
    assert top["mix"] <= end // 64 * 64 - 4 * 4096 and top["proj"] <= end // 64 * 64 - 7 * 4096
    yhi = place("merge", "common", "yhi", [P, KD, T], F32R)
    ylo = place("merge", "common", "ylo", [P, KD, T], F32R)
    ysg = place("merge", "common", "ysg", [P, 2, T])
    sg = place("merge", "common", "sg", [P, 2, 2, T])
    mo = place("merge", "common", "mo", [P, 2, T])
    qT = place("xa", "x", "qT", [P, KD, T])
    kTx = place("xa", "x", "kTx", [P, KD, MEM])
    vx = place("xa", "x", "vx", [P, 2, D])
    qs = place("xa", "x", "qs", [P, KD, SEG])
    sx = place("xa", "x", "sx", [P, XH, MEM])
    px = place("xa", "x", "px", [P, XH, MEM])
    pxt = place("xa", "x", "pxt", [P, XH, 2, SEG])
    mx = place("xa", "x", "mx", [P, 4 * XH])
    ox = place("xa", "x", "ox", [P, KD, SEG])
    memx = at_x("memx", 12, [P, KD, MEM])
    memq = at_x("memq", 20, [P, 2, MEM])
    memh = at_x("memh", 22, [P, 2, MEM])
    memhi = nc.alloc_sbuf_tensor_at("memhi", [P, KD, MEM], F32R, offset=top["x"] + 48 * 1024)
    memlo = nc.alloc_sbuf_tensor_at("memlo", [P, KD, MEM], F32R, offset=top["x"] + 64 * 1024)
    memr = at_x("memr", 72, [P, 3, MEM])

    G = [nc.alloc_psum_tensor(f"G{n}", [P, NHALF, HALF], F32) for n in range(4)]

    def flat(ap):
        return ap.rearrange("p a b -> p (a b)")

    def con(col, n=P, rows=P):
        return cst[0:rows, col:col + n]

    def v1(name, k=0):
        return vec[:, VCOL[name] + k:VCOL[name] + k + 1]

    def vbc(name, width):
        return vec[:, VCOL[name]:VCOL[name] + RC].unsqueeze(2).to_broadcast([P, RC, width])

    const_loads = [(cst[:], a["consts"]), (vec[:], a["vecs"]), (gbias[:], a["gate_b"])]

    credit = 64
    consts_in = sem("consts_in")
    x_in = sem("x_in")
    raw_in = [sem("raw_in0"), sem("raw_in1")]
    hi_made = sem("hi_made")
    split_made = sem("split_made")
    unit_used = sem("unit_used")
    act_free = sem("act_free")
    dve_free = sem("dve_free")
    phase_end = sem("phase_end")
    dve_seq = sem("dve_seq")
    act_seq = sem("act_seq")
    a_hi = sem("a_hi")
    a_lo = sem("a_lo")
    norm_sum = sem("norm_sum")
    norm_ms = sem("norm_ms")
    norm_r = sem("norm_r")
    z_out = [sem("z_out0"), sem("z_out1")]
    silu_made = sem("silu_made")
    store = sem("store")

    nsq_act = Steps(sem("nsq_act"), ["sq0", "sq1"])
    nsq_dve = Steps(sem("nsq_dve"), ["add0", "add1"])
    nh_act = Steps(sem("nh_act"), ["c0", "c1"])
    nh_dve = Steps(sem("nh_dve"), ["h0", "h1", "l0", "l1"])
    rp_dve = Steps(sem("rp_dve"), ["d0", "m0", "d1", "m1"])
    cv_dve = Steps(sem("cv_dve"), [f"t{j}{r}" for r in range(2) for j in range(4)])
    sp_in = [sem("sp_in0"), sem("sp_in1")]
    sp_act = Steps(sem("sp_act"), ["c0", "c1"])
    sp_dve = Steps(sem("sp_dve"), ["l0", "l1"])
    sg_in = [sem("sg_in0"), sem("sg_in1")]
    mg_act = Steps(sem("mg_act"), ["h0", "h1"])
    mg_dve = Steps(sem("mg_dve"), ["p0", "q0", "mo0", "l0", "p1", "q1", "mo1", "l1"])
    f_pe, f_act, f_dve, f_pool = (Steps(sem(n), x) for n, x in (
        ("f_pe", F_PE), ("f_act", F_ACT), ("f_dve", F_DVE), ("f_pool", F_POOL)))
    b_pe, b_act, b_dve, b_pool = (Steps(sem(n), x) for n, x in (
        ("b_pe", B_PE), ("b_act", B_ACT), ("b_dve", B_DVE), ("b_pool", B_POOL)))
    m_pe, m_act, m_dve, m_pool = (Steps(sem(n), x) for n, x in (
        ("m_pe", M_PE), ("m_act", M_ACT), ("m_dve", M_DVE), ("m_pool", M_POOL)))
    xa_pe, xa_act, xa_dve = (Steps(sem(n), x) for n, x in (("xa_pe", XA_PE), ("xa_act", XA_ACT), ("xa_dve", XA_DVE)))
    zs_in, zm_in = sem("zs_in"), sem("zm_in")
    yr_out, ym_out = sem("yr_out"), sem("ym_out")
    ACT_STEPS = (nsq_act, nh_act, sp_act, mg_act, f_act, b_act, m_act, xa_act)
    DVE_STEPS = (nsq_dve, nh_dve, rp_dve, cv_dve, sp_dve, mg_dve, f_dve, b_dve, m_dve, xa_dve)
    PE_STEPS = (f_pe, b_pe, m_pe, xa_pe)
    POOL_STEPS = (f_pool, b_pool, m_pool)
    MIX_FREE, MIX_READY, MIX_DONE = 2, 3, 4

    stream = []
    for f in (1, 2):
        if f == 2:
            stream += [(["rw_in"], RW_UNITS, 8, 0), (["ml_in"], ML_UNITS, 8, 0), (["if_in"], 1, 8, 0),
                       (["ga_in", "gb_in"], KD, 8, 0), (["up"], KD, 8, 0), (["w_out"], KD, 8, 0), (["wkv"], 2 * KD, 8, 0),
                       (["wq"], KD, 8, 0), (["wo"], KD, 8, 0)]
        first = 0
        for part, c_ in enumerate(FF_PARTS):
            stream.append(([f"wg{f}", f"wu{f}"], c_, 8, first))
            stream.append(([f"wd{f}_{part}"], KD, c_, 0))
            first += c_

    def runs():
        u = 0
        for names, n, tiles, first in stream:
            yield names, n, tiles, first, u
            u += n * len(names)

    block = ctx.enter_context(nc.Block())

    class Count:

        def __init__(self):
            self.unit = self.act = self.dve = self.seq = self.phase = self.a = 0
            self.norm = self.norms = self.sq = self.z = self.silu = self.split = 0

        def advance(self, unit=0, act=0, dve=0, a=0, z=0, norm=0, norms=0):
            self.unit += unit
            self.act += act
            self.dve += dve
            self.a += a
            self.z += z
            self.norm += norm
            self.norms += norms

    def barrier(eng, c):
        c.phase += 1
        eng.drain().then_inc(phase_end, 1)
        eng.wait_ge(phase_end, 3 * c.phase)

    def loop(eng, n):
        return eng.Fori(0, n) if n > 1 else nullcontext(0)

    def mixers(eng, iteration):
        iteration(0, True, False)
        with eng.Fori(1, NSEG) as i:
            iteration(i, True, True)
        iteration(NSEG, False, True)

    def bank_act(n):
        return G[n % 2]

    def bank_dve(n):
        return G[2 + n % 2]

    @block.sync
    def _(sp):
        def segment(ap, i):
            return ap.rearrange("u p t -> p u t")[:, :, bass.ds(i * SEG, SEG)]

        def iteration(i, front, back):
            if front:
                sp.wait_ge(*f_dve.at("Mu", i - 1))
                sp.dma_start(zs[:], segment(zrw_d, i)).then_inc(zs_in, 16)
            if back:
                sp.wait_ge(*m_pool.at("y3", i - 1))
                sp.dma_start(segment(y_d[RC:KD], i - 1), myo[:]).then_inc(ym_out, 16)
            if front:
                sp.dma_start(zm[:], segment(zml_d, i)).then_inc(zm_in, 16)

        def mixers_io():
            sp.wait_ge(phase_end, 3 * MIX_FREE)
            mixers(sp, iteration)
            sp.wait_ge(phase_end, 3 * MIX_DONE)

        for names, n, tiles, first, u0 in runs():
            w, m = tiles * P, len(names)

            def load(k, name, idx, u):
                sp.wait_ge(split_made, u + (credit - 1))
                sp.dma_start(raw[:, k, 0:w], a[name][idx]).then_inc(raw_in[k], 16)

            if names == ["up"]:
                mixers_io()
            rounds = 1 if m % 2 == 0 or n == 1 else 2
            with loop(sp, n // rounds) as i:
                for r in range(rounds):
                    for j, name in enumerate(names):
                        o = r * m + j
                        load((u0 + o) % 2, name, i * rounds + (r + first), i * (rounds * m) + (u0 + o))

    @block.gpsimd
    def _(pool):
        pool.sem_inc(split_made, credit)
        pool.sem_inc(hi_made, credit)
        for s in POOL_STEPS:
            pool.sem_inc(s.sem, s.n)
        tt = nc.gpsimd.tensor_tensor

        def copies(col):
            return con(col).unsqueeze(1).to_broadcast([P, NH, P])

        def iteration(i, front, back):
            F, B, M = f_pool, b_pool, m_pool
            j = i - 1
            def output():
                pool.wait_ge(*b_dve.at("y1", j))
                tt(Ys[:], Ys[:], vbc("rw_gn_w", SEG), ALU.mult).then_inc(*B.sig("y2"))
                pool.wait_ge(*B.at("y2", j))
                tt(Ys[:], Ys[:], bvb[:], ALU.add).then_inc(*B.sig("y3"))
                pool.wait_ge(*B.at("y3", j))
                pool.wait_ge(yr_out, i * 16)
                tt(yo[:], Ys[:], gout[:], ALU.mult).then_inc(*B.sig("y4"))

            if front:
                pool.wait_ge(zs_in, i * 16 + 16)
                tt(kk[:], zs[:, 4:8, :], vbc("rw_k_k", SEG), ALU.mult).then_inc(*F.sig("kkr"))
                pool.wait_ge(*F.at("kkr", i))
                tt(ksq[:], kk[:], kk[:], ALU.mult).then_inc(*F.sig("sq"))
            if back:
                tt(bvb[:], bv[:], vbc("rw_gn_b", SEG), ALU.add).then_inc(*B.sig("bvb"))
            if front:
                pool.wait_ge(*f_dve.at("kmod", i))
                tt(rkb[:], zs[:, 0:4, :], kmod[:], ALU.mult).then_inc(*F.sig("rk"))
                pool.wait_ge(*F.at("rk", i))
                tt(rkb[:], rkb[:], vbc("rw_r_k", SEG), ALU.mult).then_inc(*F.sig("rkb"))
                pool.wait_ge(*f_act.at("Pi", i))
                tt(kap[:], kmod[:], Pi[:, :, 1:DEC], ALU.mult).then_inc(*F.sig("kap"))
                pool.wait_ge(*b_pe.at("Y", j))
                tt(rho[:], zs[:, 0:4, :], Pp[:, :, 1:DEC], ALU.mult).then_inc(*F.sig("rho"))
            if back:
                pool.wait_ge(*b_dve.at("yc", j))
                tt(ysq[:], Ys[:], Ys[:], ALU.mult).then_inc(*B.sig("ysq"))
            if not front:
                output()
                return
            pool.wait_ge(*m_act.at("D", i))
            tt(kw[:], mktok[:], Db[:, :, SEG - 1:SEG].to_broadcast([P, MH, SEG]), ALU.mult).then_inc(*M.sig("kw"))
            pool.wait_ge(*f_dve.at("am0", i))
            tt(Tr[:], copies(C_ID), AL[:, 0].bitcast(F32), ALU.subtract).then_inc(*F.sig("T0"))
            for n in range(1, LEVELS):
                if n == 2:
                    pool.wait_ge(*F.at("T0", i))
                if n >= 2:
                    pool.wait_ge(*f_pe.at("am0T" if n == 2 else f"W{n - 2}", i))
                tt(AL[:, n % 2], Am[:], copies(C_LEV + n * P), ALU.mult).then_inc(*F.sig(f"am{n}"))
                if n == 3 and back:
                    output()
                if n == 4:
                    pool.wait_ge(*m_pe.at("den", i))
                    tt(CN[:], CN[:], Eb[:, :, SEG - 1:SEG].unsqueeze(1).to_broadcast([P, 2, MH, SEG]),
                       ALU.mult).then_inc(*M.sig("dec"))
            pool.wait_ge(*m_dve.at("yc", i))
            tt(mysq[:], hm[:], hm[:], ALU.mult).then_inc(*M.sig("ysq"))
            pool.wait_ge(*f_dve.at(f"U{LEVELS - 1}", i))
            tt(Uf[:], copies(C_ID), Ur[:].bitcast(F32), ALU.subtract).then_inc(*F.sig("IU"))
            pool.wait_ge(*m_dve.at("y1", i))
            tt(hm[:], hm[:], vbc("ml_norm", SEG), ALU.mult).then_inc(*M.sig("y2"))
            pool.wait_ge(*M.at("y2", i))
            pool.wait_ge(ym_out, i * 16 + 16)
            tt(myo[:], hm[:], zm[:, 12:16, :], ALU.mult).then_inc(*M.sig("y3"))

        pool.wait_ge(consts_in, CONSTS * 16)
        for names, n, tiles, first, u0 in runs():
            w, total = tiles * P, n * len(names)

            def split(k, u, turn):
                pool.wait_ge(unit_used, u + (credit - 1))
                pool.wait_ge(raw_in[k], turn * 16)
                nc.gpsimd.tensor_tensor(whi[:, k, 0:w], raw[:, k, 0:w], cst[:, C_ZERO:C_ZERO + 1].to_broadcast([P, w]),
                                        ALU.add).then_inc(hi_made, 1)
                pool.wait_ge(hi_made, u + (credit + 1))
                nc.gpsimd.tensor_tensor(wlo[:, k, 0:w], raw[:, k, 0:w], whi[:, k, 0:w].bitcast(F32),
                                        ALU.subtract).then_inc(split_made, 1)

            if names == ["up"]:
                pool.wait_ge(phase_end, 3 * MIX_READY)
                mixers(pool, iteration)
            rounds = 2 if total > 1 else 1
            with loop(pool, total // rounds) as i:
                for r in range(rounds):
                    u = u0 + r
                    split(u % 2, i * rounds + u, i + (u // 2 + 1))

    @block.tensor
    def _(pe):
        c = Count()
        pe.sem_inc(unit_used, credit)
        for s in PE_STEPS:
            pe.sem_inc(s.sem, s.n)

        def tile3(dst, k, t, hi, lo, start, stop):
            wh, wl = whi[:, k, t * P:(t + 1) * P], wlo[:, k, t * P:(t + 1) * P]
            nc.tensor.matmul(dst, wh, hi, start=start, stop=False)
            nc.tensor.matmul(dst, wh, lo, start=False, stop=False)
            return nc.tensor.matmul(dst, wl, hi, start=False, stop=stop)

        def product(bank, k, tiles, hi, lo, chunk_ready=None):
            if chunk_ready:
                for n, t in enumerate(tiles):
                    chunk_ready(t)
                    for h in range(NHALF):
                        cols = slice(h * HALF, (h + 1) * HALF)
                        last = tile3(bank[:, h, :], k, t, hi[:, n, cols], lo[:, n, cols], n == 0, n == len(tiles) - 1)
                return last
            for h in range(NHALF):
                cols = slice(h * HALF, (h + 1) * HALF)
                for n, t in enumerate(tiles):
                    last = tile3(bank[:, h, :], k, t, hi[:, n, cols], lo[:, n, cols], n == 0, n == len(tiles) - 1)
            return last

        def unit_ready(u):
            pe.wait_ge(split_made, u + (credit + 1))

        def act_bank(n):
            pe.wait_ge(act_free, n + (credit - 1))

        def dve_bank(n):
            pe.wait_ge(dve_free, n + (credit - 1))

        def pairs(n, first, body):
            if first:
                body(0, True)
                with pe.Fori(1, n // 2) as i:
                    body(i, False)
            else:
                with loop(pe, n // 2 if n > 1 else 1) as i:
                    body(i, False)

        def gemm(n, by, tiles=8, hi=hhi, lo=hlo, chunk_ready=None):
            count = c.act if by == "act" else c.dve

            def body(i, first):
                for r in range(min(n, 2)):
                    (act_bank if by == "act" else dve_bank)(i * 2 + (count + r))
                    unit_ready(i * 2 + (c.unit + r))
                    bank = (bank_act if by == "act" else bank_dve)(count + r)
                    product(bank, (c.unit + r) % 2, range(tiles), hi, lo,
                            chunk_ready if first and r == 0 else None).then_inc(unit_used, 1)

            pairs(n, chunk_ready, body)
            c.advance(unit=n, act=n if by == "act" else 0, dve=n if by == "dve" else 0)

        def norm(acc, width, squares=4):
            c.sq += squares
            c.norm += 4
            c.norms += 1
            pe.wait_ge(*nsq_dve.at("add1", c.sq - 1))
            dve_bank(c.dve)
            cols = min(width, HALF)
            for h in range(width // cols):
                last = nc.tensor.matmul(bank_dve(c.dve)[:, h, 0:cols], con(C_ONES), acc[:, h * cols:(h + 1) * cols],
                                        start=True, stop=True)
            last.then_inc(norm_sum, 1)
            c.dve += 1

        def norm_done():
            pe.wait_ge(*nh_dve.at("l1", c.norm - 1))

        def norm_chunk(t):
            pe.wait_ge(*nh_dve.at(f"l{t % 2}", c.norm - 4 + t // 2))

        def arrive():
            c.phase += 1
            pe.drain().then_inc(phase_end, 1)

        def ffn():
            norm(nt, T)
            for part, n in enumerate(FF_PARTS):
                def body(i, first):
                    for r in range(2):
                        act_bank(i * 2 + (c.act + r))
                        unit_ready(i * 4 + (c.unit + 2 * r))
                        product(bank_act(c.act + r), (c.unit + 2 * r) % 2, range(KD), hhi, hlo,
                                norm_chunk if first and r == 0 else None).then_inc(unit_used, 1)
                        dve_bank(i * 2 + (c.dve + r))
                        unit_ready(i * 4 + (c.unit + 2 * r + 1))
                        product(bank_dve(c.dve + r), (c.unit + 2 * r + 1) % 2, range(KD), hhi,
                                hlo).then_inc(unit_used, 1)

                pairs(n, part == 0, body)
                c.advance(unit=2 * n, act=n, dve=n, a=n)
                pe.wait_ge(a_lo, c.a + 1)
                gemm(KD, "dve", tiles=n, hi=ahi, lo=alo)

        def iteration(i, front, back):
            F, B, M = f_pe, b_pe, m_pe
            j = i - 1
            g0, g1, g2, m0, m1 = G[0], G[1], G[2], G[3][:, 0, :], G[3][:, 1, :]
            heads = [(n, n // RC, n % RC, slice(n // RC * HD, (n // RC + 1) * HD)) for n in range(NH)]

            def turn(dst, src):
                for r in range(RC):
                    last = nc.tensor.transpose(dst[:, r * P:(r + 1) * P], src[:, r, :], con(C_ID))
                return last

            def gram(left, right, dst):
                for n, e, r, rows in heads:
                    last = nc.tensor.matmul(dst[:, e, r * P:(r + 1) * P], left[rows, r, :], right[rows, r, :],
                                            start=True, stop=True)
                return last

            def eight(dst, left, right):
                for n in range(NH):
                    last = nc.tensor.matmul(flat(dst[:])[:, n * P:(n + 1) * P], left[:, n, :], right[:, n, :],
                                            start=True, stop=True)
                return last

            def rows_out(dst, row):
                for h in range(MH):
                    last = nc.tensor.matmul(dst[:, h * SEG:(h + 1) * SEG], cst[0:MH, C_SEL + h * P:C_SEL + (h + 1) * P],
                                            row[:, bass.ds(i * SEG, SEG)], start=True, stop=True)
                return last

            if front:
                pe.wait_ge(*f_dve.at("Uf", i - 1))
                pe.wait_ge(*f_act.at("ad", i))
                for r in range(RC):
                    nc.tensor.matmul(g0[:, 0, r * P:(r + 1) * P], loraw[0:HD, 0, r * P:(r + 1) * P], lora[0:HD, :],
                                     start=True, stop=True)
                    last = nc.tensor.matmul(g0[:, 1, r * P:(r + 1) * P], loraw[HD:P, 0, r * P:(r + 1) * P],
                                            lora[HD:P, :], start=True, stop=True)
                last.then_inc(*F.sig("lora"))
            if back:
                pe.wait_ge(*f_act.at("W1c", j))
                for n, e, r, rows in heads:
                    dst = g2[:, e, r * HD:(r + 1) * HD]
                    nc.tensor.matmul(dst, Uf[:, n, :], Zm[:, n, :], start=True, stop=False)
                    last = nc.tensor.matmul(dst, W1m[rows, r, :], S0s[rows, r, :], start=False, stop=True)
                last.then_inc(*B.sig("U"))
            if front:
                pe.wait_ge(*f_act.at("ta", i))
                pe.wait_ge(*f_pool.at("sq", i))
                nc.tensor.matmul(g0[:, 0, :], con(C_HONES), flat(ksq[:]), start=True, stop=True).then_inc(*F.sig("ss"))
                pe.wait_ge(*m_dve.at("ve", i - 1))
                rows_out(m0, arow).then_inc(*M.sig("bca"))
                rows_out(m1, erow).then_inc(*M.sig("bce"))
            if back:
                pe.wait_ge(*b_act.at("Un", j))
                for n, e, r, rows in heads:
                    dst = g2[rows, e, r * P:(r + 1) * P]
                    nc.tensor.matmul(dst, vtok[:, r, rows], Mv[:, n, :], start=True, stop=False)
                    nc.tensor.matmul(dst, S0s[rows, r, :], rho[rows, r, :], start=False, stop=False)
                    last = nc.tensor.matmul(dst, Un[:, n, :], Mu[:, n, :], start=False, stop=True)
                last.then_inc(*B.sig("Y"))
                pe.wait_ge(*f_dve.at("Q", j))
                for n, e, r, rows in heads:
                    dst = g1[rows, 1, r * HD:(r + 1) * HD]
                    nc.tensor.matmul(dst, ktok[:, r, rows], vtok[:, r, rows], start=True, stop=False)
                    last = nc.tensor.matmul(dst, btok[:, r, rows], Un[:, n, :], start=False, stop=True)
                last.then_inc(*B.sig("dS"))
            if front:
                pe.wait_ge(*m_dve.at("arg", i))
                rows_out(m0, mrow).then_inc(*M.sig("bcn"))
                pe.wait_ge(*m_act.at("E", i))
                nc.tensor.matmul(m1[:, 0:MH], gst[:], cst[0:MH, C_ID:C_ID + MH], start=True,
                                 stop=True).then_inc(*M.sig("gT"))
                pe.wait_ge(*b_dve.at("dS", j))
                pe.wait_ge(*f_dve.at("Q", i - 1))
                turn(g1[:, 1, :], zs[:, 8:12, :]).then_inc(*F.sig("vT"))
                pe.wait_ge(*f_pool.at("rkb", i))
                nc.tensor.matmul(g0[:, 1, :], con(C_HONES), flat(rkb[:]), start=True,
                                 stop=True).then_inc(*F.sig("bonus"))
                pe.wait_ge(zm_in, i * 16 + 16)
                pe.wait_ge(*m_act.at("nm", i))
                turn(m0, zm[:, MH:2 * MH, :]).then_inc(*M.sig("kT"))
                pe.wait_ge(*m_act.at("gtok", i))
                turn(m1, zm[:, 2 * MH:3 * MH, :]).then_inc(*M.sig("vT"))
                pe.wait_ge(*f_dve.at("alpha", i))
                turn(g0[:, 0, :], alpha).then_inc(*F.sig("aT"))
                pe.wait_ge(*f_dve.at("beta", i))
                turn(g0[:, 1, :], beta).then_inc(*F.sig("bT"))
                pe.wait_ge(*f_pool.at("kap", i))
                turn(g1[:, 0, :], kap).then_inc(*F.sig("kT"))
            if back:
                pe.wait_ge(*b_act.at("Y1", j))
                nc.tensor.matmul(g2[:, 0, :], con(C_HONES), flat(Ys[:]), start=True, stop=True).then_inc(*B.sig("mean"))
            if front:
                pe.wait_ge(*f_act.at("ktok", i))
                gram(alpha, beta, g1).then_inc(*F.sig("A"))
                pe.wait_ge(*f_pool.at("rho", i))
                gram(beta, rho, g0).then_inc(*F.sig("Mu"))
            if back:
                pe.wait_ge(*b_pool.at("ysq", j))
                nc.tensor.matmul(g2[:, 1, :], con(C_HONES), flat(ysq[:]), start=True, stop=True).then_inc(*B.sig("var"))
            if not front:
                return
            pe.wait_ge(*m_act.at("ktok", i))
            for h in range(MH):
                last = nc.tensor.matmul(m0[:, h * SEG:(h + 1) * SEG], zm[:, MH + h, :], zm[:, h, :], start=True, stop=True)
            last.then_inc(*M.sig("S"))
            pe.wait_ge(*f_dve.at("am0", i))
            for n in range(NH):
                last = nc.tensor.matmul(flat(g1[:])[:, n * P:(n + 1) * P], AL[:, 0, n, :], idr[:], start=True, stop=True)
            last.then_inc(*F.sig("am0T"))
            pe.wait_ge(*f_dve.at("Mu", i))
            gram(kap, alpha, g0).then_inc(*F.sig("B"))
            for n in range(1, LEVELS):
                pe.wait_ge(*f_dve.at(f"U{n - 1}", i))
                pe.wait_ge(*f_pool.at(f"am{n}", i))
                eight(g1, AL[:, n % 2], Ur).then_inc(*F.sig(f"W{n}"))
                if n == 1:
                    pe.wait_ge(*b_dve.at("ve", j))
                    gram(kap, rho, g2).then_inc(*F.sig("Mv"))
                    pe.wait_ge(*f_pool.at("T0", i))
                    pe.wait_ge(*f_dve.at("B", i))
                else:
                    pe.wait_ge(*(f_dve.at("Mv", i) if n == 2 else f_act.at(f"Tc{n - 2}", i)))
                    for h in range(NH):
                        last = nc.tensor.matmul(flat(g2[:])[:, h * P:(h + 1) * P], Ur[:, h, :], idr[:], start=True,
                                                stop=True)
                    last.then_inc(*F.sig(f"V{n - 1}"))
                if n == 3:
                    nc.tensor.matmul(m0, con(C_ONES), flat(Pb[:]), start=True, stop=False)
                    for h in range(MH):
                        last = nc.tensor.matmul(m0[:, h * SEG:(h + 1) * SEG], CN[:, 1, h, :], qe[:, h, :],
                                                start=False, stop=h == MH - 1)
                    last.then_inc(*M.sig("den"))
                if n == 4:
                    pe.wait_ge(*m_pool.at("kw", i))
                    pe.wait_ge(*m_act.at("aden", i))
                    for h in range(MH):
                        last = nc.tensor.matmul(m0[:, h * SEG:(h + 1) * SEG], kw[:, h, :], mvtok[:, h, :],
                                                start=True, stop=True)
                    last.then_inc(*M.sig("dC"))
                    pe.wait_ge(*m_dve.at("hm", i))
                    for h in range(MH):
                        last = nc.tensor.matmul(m1[:, h * SEG:(h + 1) * SEG], kw[:, h, :], con(C_ONES),
                                                start=True, stop=True)
                    last.then_inc(*M.sig("dN"))
                if n == 5:
                    pe.wait_ge(*m_dve.at("C", i))
                    nc.tensor.matmul(m0, con(C_ONES), flat(hm[:]), start=True, stop=True).then_inc(*M.sig("mean"))
                if n == 6:
                    pe.wait_ge(*m_pool.at("ysq", i))
                    nc.tensor.matmul(m1, con(C_ONES), flat(mysq[:]), start=True, stop=True).then_inc(*M.sig("var"))
                pe.wait_ge(*f_act.at(f"Wc{n}" if n == 1 else f"Tc{n - 1}", i))
                eight(g0, Tr, Wr).then_inc(*F.sig(f"E{n}"))
                if n == 2:
                    pe.wait_ge(*m_act.at("vtok", i))
                    pe.wait_ge(*m_dve.at("qe", i))
                    for h in range(MH):
                        dst = m1[:, h * SEG:(h + 1) * SEG]
                        nc.tensor.matmul(dst, mvtok[:, h, :], Pb[:, h, :], start=True, stop=False)
                        last = nc.tensor.matmul(dst, CN[:, 0, h, :], qe[:, h, :], start=False, stop=True)
                    last.then_inc(*M.sig("num"))
            pe.wait_ge(*f_dve.at(f"U{LEVELS - 1}", i))
            eight(g1, Am, Ur[:].bitcast(F32)).then_inc(*F.sig("F"))
            pe.wait_ge(*f_act.at(f"Tc{LEVELS - 2}", i))
            for n in range(NH):
                last = nc.tensor.matmul(flat(g2[:])[:, n * P:(n + 1) * P], Ur[:, n, :], idr[:], start=True, stop=True)
            last.then_inc(*F.sig(f"V{LEVELS - 1}"))
            pe.wait_ge(*f_act.at(f"Tc{LEVELS - 1}", i))
            pe.wait_ge(*f_dve.at("Q", i))
            eight(g0, Tr, Qr).then_inc(*F.sig("UQ"))
            for r in range(RC):
                last = nc.tensor.matmul(g2[:, 0, r * P:(r + 1) * P], loraw[:, 1, r * P:(r + 1) * P], gsig[:],
                                        start=True, stop=True)
            last.then_inc(*F.sig("gate"))
            for n, e, r, rows in heads:
                last = nc.tensor.matmul(g1[:, 0, n * HD:(n + 1) * HD], Bm[:, n, :], vtok[:, r, rows],
                                        start=True, stop=True)
            last.then_inc(*F.sig("Z"))
            pe.wait_ge(*f_dve.at("Uf", i))
            for n, e, r, rows in heads:
                last = nc.tensor.matmul(g2[rows, 1, r * P:(r + 1) * P], atok[:, r, rows], Uf[:, n, :],
                                        start=True, stop=True)
            last.then_inc(*F.sig("Wst"))

        def merge():
            def output_chunk(t):
                pe.wait_ge(*sp_dve.at(f"l{t % 2}", t // 2))

            def body(i, first):
                for r in range(2):
                    for n in range(2):
                        dve_bank(i * 4 + (c.dve + 2 * r + n))
                        if n == 0:
                            unit_ready(i * 2 + (c.unit + r))
                        last = product(bank_dve(c.dve + n), (c.unit + r) % 2, range(n * RC, (n + 1) * RC),
                                       yhi[:, n * RC:(n + 1) * RC, :], ylo[:, n * RC:(n + 1) * RC, :],
                                       output_chunk if first and r == 0 else None)
                    last.then_inc(unit_used, 1)

            pairs(KD, True, body)
            c.advance(unit=KD, dve=2 * KD)

        def keys_values():
            norm(memr[:, 2, :], MEM, squares=8)
            norm_done()
            for part in range(2):
                with pe.Fori(0, KD // 2) as i:
                    for r in range(2):
                        act_bank(i * 2 + (c.act + r))
                        unit_ready(i * 2 + (c.unit + r))
                        k = (c.unit + r) % 2
                        bank = bank_act(c.act + r)
                        if part == 0:
                            for t in range(KD):
                                last = tile3(bank[:, 0, 0:MEM], k, t, memhi[:, t, :], memlo[:, t, :], t == 0, t == KD - 1)
                        else:
                            for m in range(2):
                                rows, dst = slice(m * P, (m + 1) * P), bank[:, m, 0:P]
                                for t in range(KD):
                                    wh, wl = whi[:, k, t * P:(t + 1) * P], wlo[:, k, t * P:(t + 1) * P]
                                    nc.tensor.matmul(dst, memhi[:, t, rows], wh, start=t == 0, stop=False)
                                    nc.tensor.matmul(dst, memhi[:, t, rows], wl, start=False, stop=False)
                                    last = nc.tensor.matmul(dst, memlo[:, t, rows], wh, start=False, stop=t == KD - 1)
                        last.then_inc(unit_used, 1)
                c.advance(unit=KD, act=KD)

        def attend():
            with pe.Fori(0, NSEG) as i:
                g0, g1, g2, g3 = G
                pe.wait_ge(*xa_act.at("q", i))
                for h in range(XH):
                    for n in range(2):
                        last = nc.tensor.matmul(flat(g0[:])[:, h * MEM:(h + 1) * MEM], qs[:, 2 * h + n, :],
                                                kTx[:, 2 * h + n, :], start=n == 0, stop=n == 1)
                last.then_inc(*xa_pe.sig("S"))
                pe.wait_ge(*xa_dve.at("p", i))
                for h in range(XH):
                    for m in range(2):
                        last = nc.tensor.transpose(flat(g1[:])[:, (2 * h + m) * P:(2 * h + m + 1) * P],
                                                   px[:, h, m * P:(m + 1) * P], con(C_ID))
                last.then_inc(*xa_pe.sig("T"))
                pe.wait_ge(*xa_act.at("pt", i))
                pe.wait_ge(*xa_dve.at("lo", i - 1))
                for n in range(KD):
                    for m in range(2):
                        last = nc.tensor.matmul(flat(g2[:])[:, n * P:(n + 1) * P], vx[:, m, n * P:(n + 1) * P],
                                                pxt[:, n // 2, m, :], start=m == 0, stop=m == 1)
                last.then_inc(*xa_pe.sig("O"))

        pe.wait_ge(consts_in, CONSTS * 16)
        ffn()
        norm(nt, T)
        arrive()
        gemm(RW_UNITS, "act", chunk_ready=norm_chunk)
        gemm(ML_UNITS, "act")
        gemm(1, "act")
        gemm(2 * KD, "act")
        barrier(pe, c)
        barrier(pe, c)
        mixers(pe, iteration)
        barrier(pe, c)
        merge()
        pe.wait_ge(*mg_dve.at("l1", 3))
        barrier(pe, c)
        gemm(KD, "dve")
        barrier(pe, c)
        keys_values()
        norm(nt, T, squares=0)
        arrive()
        gemm(KD, "act", chunk_ready=norm_chunk)
        barrier(pe, c)
        attend()
        barrier(pe, c)
        gemm(KD, "dve")
        ffn()
        norm(nt, T)

    @block.scalar
    def _(act):
        c = Count()
        act.sem_inc(act_free, credit)
        for s in (*z_out, silu_made, yr_out, ym_out):
            act.sem_inc(s, 16)
        for s in ACT_STEPS:
            act.sem_inc(s.sem, s.n)
        activation = nc.scalar.activation

        def output_ready(u):
            act.wait_ge(unit_used, u + (credit + 1))

        def squares(src, sq, residual=False):
            with act.Fori(0, KD // 2) as i:
                for n in range(2):
                    if residual:
                        act.wait_ge(dve_free, i * 2 + (c.dve + n + 1 + credit))
                    act.wait_ge(*nsq_dve.at(f"add{n}", i + (c.sq - 1)))
                    activation(sq[:, n, :], src[:, i * 2 + n, :], ACT.Square).then_inc(*nsq_act.sig(f"sq{n}"))
            c.sq += 4
            if residual:
                c.advance(unit=KD, dve=KD)

        def norm(ms, r, h, hi):
            act.wait_ge(norm_ms, c.norms + 1)
            activation(r, ms, ACT.Ln).then_inc(act_seq, 1)
            c.seq += 1
            act.wait_ge(act_seq, c.seq)
            activation(r, r, ACT.Exp, scale=-0.5).then_inc(norm_r, 1)
            if hi is not None:
                with act.Fori(0, KD // 2) as i:
                    for n in range(2):
                        act.wait_ge(*nh_dve.at(f"h{n}", i + c.norm))
                        activation(hi[:, i * 2 + n, :], h[:, n, :], ACT.Copy).then_inc(*nh_act.sig(f"c{n}"))
            c.advance(norm=4, norms=1, dve=1)

        def norm_x(hi=hhi):
            norm(nms[:], nr[:], nh, hi)

        def ffn():
            norm_x()
            for n in FF_PARTS:
                with loop(act, n // 2) as i:
                    for r in range(2):
                        output_ready(i * 4 + (c.unit + 2 * r))
                        act.wait_ge(dve_free, i * 2 + (c.dve + r + credit))
                        act.wait_ge(*nh_dve.at("l1", c.norm - 1))
                        activation(s0[:], flat(bank_act(c.act + r)[:]), ACT.Silu).then_inc(act_free, 1)
                        act.wait_ge(dve_free, i * 2 + (c.dve + r + 1 + credit))
                        activation(ahi[:, i * 2 + r, :], s1[:], ACT.Copy).then_inc(a_hi, 1)
                c.advance(unit=2 * n, act=n, dve=n, a=n)
                if n != FF_PARTS[-1]:
                    c.advance(unit=KD, dve=KD)
            squares(xT, nsq, residual=True)

        def store_z(dst, r, turn):
            act.dma_start(dst, po[:, r, :]).then_inc(z_out[r], 16)

        def po_free(r, turn):
            act.wait_ge(z_out[r], (turn + 1) * 16)

        def project_rw():
            with act.Fori(0, RW_UNITS // 2) as i:
                for r in range(2):
                    output_ready(i * 2 + (c.unit + r))
                    act.wait_ge(*rp_dve.at(f"m{r}", i - 1))
                    activation(stg[:, r, 3:3 + T], flat(bank_act(c.act + r)[:]), ACT.Copy).then_inc(act_free, 1)
                    act.wait_ge(*rp_dve.at(f"m{r}", i))
                    store_z(zrw_d[i * 2 + r], r, 0)
            c.advance(unit=RW_UNITS, act=RW_UNITS, z=RW_UNITS // 2)

        def project_ml():
            with act.Fori(0, MH) as i:
                for r in range(2):
                    output_ready(i * 2 + (c.unit + r))
                    act.wait_ge(*cv_dve.at(f"t3{r}", i - 1))
                    activation(stg[:, r, 3:3 + T], flat(bank_act(c.act + r)[:]), ACT.Copy).then_inc(act_free, 1)
                    act.wait_ge(*cv_dve.at(f"t3{r}", i))
                    po_free(r, i + c.z)
                    activation(po[:, r, :], pd[:, r, :], ACT.Silu).then_inc(silu_made, 1)
                    act.wait_ge(silu_made, i * 2 + (r + 1 + 16))
                    store_z(zml_d[i * 2 + r], r, 0)
            c.advance(unit=2 * MH, act=2 * MH, z=MH)
            for first, func in ((2 * MH, ACT.Copy), (3 * MH, ACT.Sigmoid)):
                with act.Fori(0, MH // 2) as i:
                    for r in range(2):
                        output_ready(i * 2 + (c.unit + r))
                        po_free(r, i + c.z)
                        activation(po[:, r, :], flat(bank_act(c.act + r)[:]), func).then_inc(act_free, 1)
                        act.wait_ge(act_free, i * 2 + (c.act + r + 1 + credit))
                        store_z(zml_d[i * 2 + (first + r)], r, 0)
                c.advance(unit=MH, act=MH, z=MH // 2)
            output_ready(c.unit)
            activation(ifs[:], flat(bank_act(c.act)[:]), ACT.Copy).then_inc(act_free, 1)
            c.advance(unit=1, act=1)
            act.wait_ge(act_free, c.act + credit)
            act.dma_start(ifr[:], ifs[0:MH, :]).then_inc(x_in, 16)
            act.dma_start(grow[:], ifs[MH:2 * MH, :]).then_inc(x_in, 16)
            mlstm_rows()
            with act.Fori(0, KD) as i:
                for r, dst in enumerate((gates_d[0], gates_d[1])):
                    output_ready(i * 2 + (c.unit + r))
                    po_free(r, i + c.z)
                    activation(po[:, r, :], flat(bank_act(c.act + r)[:]), ACT.Sigmoid).then_inc(act_free, 1)
                    act.wait_ge(act_free, i * 2 + (c.act + r + 1 + credit))
                    store_z(dst[i], r, 0)
            c.advance(unit=2 * KD, act=2 * KD, z=KD)
            for r in range(2):
                act.wait_ge(z_out[r], (c.z + 1) * 16)

        def store_output(j):
            act.wait_ge(*b_pool.at("y4", j))
            act.dma_start(y_d[0:RC].rearrange("r p t -> p r t")[:, :, bass.ds(j * SEG, SEG)], yo[:]).then_inc(yr_out, 16)

        def iteration(i, front, back):
            F, B, M = f_act, b_act, m_act
            j = i - 1
            g0, g1, g2, m0, m1 = G[0], G[1], G[2], G[3][:, 0, :], G[3][:, 1, :]
            if front:
                act.wait_ge(zs_in, i * 16 + 16)
                activation(lora[0:HD, :], zs[0:HD, 12, :], ACT.Tanh).then_inc(*F.sig("th"))
                activation(lora[HD:P, :], zs[HD:P, 12, :], ACT.Copy).then_inc(*F.sig("ad"))
                activation(gsig[:], zs[:, 13, :], ACT.Tanh, scale=0.5).then_inc(*F.sig("gt"))
                act.wait_ge(*f_pe.at("lora", i))
                for r in range(RC):
                    last = activation(dec[:, r, 1:DEC], g0[:, 0, r * P:(r + 1) * P], ACT.Tanh, scale=0.5,
                                      bias=hw0[:, r:r + 1])
                last.then_inc(*F.sig("tw"))
                for r in range(RC):
                    last = activation(ga[:, r, :], g0[:, 1, r * P:(r + 1) * P], ACT.Tanh, scale=0.5,
                                      bias=hw0[:, RC + r:RC + r + 1])
                last.then_inc(*F.sig("ta"))
            if back:
                act.wait_ge(*b_pe.at("U", j))
                activation(Un[:].rearrange("p (e r) v -> p e (r v)", e=2), g2[:, :, 0:RC * HD], ACT.Copy,
                           scale=-1.0).then_inc(*B.sig("Un"))
            if front:
                activation(gst[:], grow[:, bass.ds(i * SEG, SEG)], ACT.Copy).then_inc(*M.sig("gst"))
                act.wait_ge(*m_pe.at("bce", i))
                activation(flat(Eb[:]), m1, ACT.Exp).then_inc(*M.sig("E"))
                act.wait_ge(*f_dve.at("cc", i))
                activation(flat(Pp[:]), flat(dec[:]), ACT.Exp, scale=-KAPPA).then_inc(*F.sig("P"))
                activation(flat(Pi[:]), flat(dec[:]), ACT.Exp, scale=KAPPA).then_inc(*F.sig("Pi"))
                act.wait_ge(*f_dve.at("ssc", i))
                activation(flat(rinv[:]), flat(ssc[:]), ACT.Ln, scale=2.0 ** 20).then_inc(*F.sig("lnn"))
                act.wait_ge(*F.at("lnn", i))
                activation(flat(rinv[:]), flat(rinv[:]), ACT.Exp, scale=-0.5,
                           bias=cst[:, C_RSC:C_RSC + 1]).then_inc(*F.sig("rinv"))
            if back:
                act.wait_ge(*b_pe.at("Y", j))
                act.wait_ge(*b_pool.at("y4", j - 1))
                for e in range(2):
                    rows = slice(e * HD, (e + 1) * HD)
                    activation(flat(Ys[rows]), g2[rows, e, :], ACT.Copy).then_inc(*B.sig(f"Y{e}"))
            if front:
                act.wait_ge(*m_pe.at("bcn", i))
                act.wait_ge(*m_dve.at("y1", i - 1))
                activation(flat(nmb[:]), m0, ACT.Exp, scale=-1.0).then_inc(*M.sig("nm"))
                act.wait_ge(*m_pe.at("gT", i))
                activation(gtok[:], m1[:, 0:MH], ACT.Copy).then_inc(*M.sig("gtok"))
                act.wait_ge(*f_pe.at("vT", i))
                act.wait_ge(*b_pe.at("dS", j))
                activation(flat(vtok[:]), g1[:, 1, :], ACT.Copy).then_inc(*F.sig("vtok"))
                act.wait_ge(*m_pe.at("kT", i))
                activation(flat(mktok[:]), m0, ACT.Copy).then_inc(*M.sig("ktok"))
                act.wait_ge(*m_pe.at("vT", i))
                activation(flat(mvtok[:]), m1, ACT.Copy).then_inc(*M.sig("vtok"))
                act.wait_ge(*M.at("gtok", i))
                act.wait_ge(*m_dve.at("arg", i))
                for h in range(MH):
                    last = activation(Db[:, h, :], argb[:, h, :], ACT.Exp, bias=gtok[:, h:h + 1])
                last.then_inc(*M.sig("D"))
                for name, dst, src in (("a", atok, g0[:, 0, :]), ("b", btok, g0[:, 1, :]), ("k", ktok, g1[:, 0, :])):
                    act.wait_ge(*f_pe.at(f"{name}T", i))
                    activation(flat(dst[:]), src, ACT.Copy).then_inc(*F.sig(f"{name}tok"))
            if back:
                act.wait_ge(*b_dve.at("ve", j))
                activation(flat(yrs[:]), flat(yve[:]), ACT.Ln).then_inc(*B.sig("lnv"))
                act.wait_ge(*B.at("lnv", j))
                activation(flat(yrs[:]), flat(yrs[:]), ACT.Exp, scale=-0.5).then_inc(*B.sig("rsv"))
            if not front:
                store_output(j)
                return
            for n in range(1, LEVELS):
                act.wait_ge(*f_pe.at(f"W{n}", i))
                activation(flat(Wr[:]), flat(g1[:]), ACT.Copy).then_inc(*F.sig(f"Wc{n}"))
                if n > 1:
                    act.wait_ge(*f_pe.at(f"V{n - 1}", i))
                    activation(flat(Tr[:]), flat(g2[:]), ACT.Copy).then_inc(*F.sig(f"Tc{n - 1}"))
                if n == 3:
                    act.wait_ge(*m_pe.at("den", i))
                    activation(flat(aden[:]), m0, ACT.Abs).then_inc(*M.sig("aden"))
            act.wait_ge(*m_dve.at("ve", i))
            activation(flat(mrs[:]), flat(mve[:]), ACT.Ln).then_inc(*M.sig("lnv"))
            act.wait_ge(*M.at("lnv", i))
            activation(flat(mrs[:]), flat(mrs[:]), ACT.Exp, scale=-0.5).then_inc(*M.sig("rsv"))
            act.wait_ge(*f_pe.at(f"V{LEVELS - 1}", i))
            activation(flat(Tr[:]), flat(g2[:]), ACT.Copy).then_inc(*F.sig(f"Tc{LEVELS - 1}"))
            act.wait_ge(*f_pe.at("gate", i))
            if back:
                store_output(j)
            activation(flat(gout[:]), g2[:, 0, :], ACT.Copy).then_inc(*F.sig("gev"))
            act.wait_ge(*f_pe.at("Z", i))
            activation(flat(Zm[:]), g1[:, 0, :], ACT.Copy).then_inc(*F.sig("Zc"))
            act.wait_ge(*f_pe.at("Wst", i))
            activation(flat(W1m[:]), g2[:, 1, :], ACT.Copy).then_inc(*F.sig("W1c"))

        def mlstm_rows():
            act.wait_ge(dve_seq, ROWS_SEQ + 1)
            activation(arow[:], grow[:], ACT.Abs).then_inc(act_seq, 1)
            act.wait_ge(act_seq, c.seq + 1)
            activation(nrow[:], arow[:], ACT.Exp, scale=-1.0).then_inc(act_seq, 1)
            act.wait_ge(act_seq, c.seq + 2)
            activation(nrow[:], nrow[:], ACT.Ln, bias=1.0).then_inc(act_seq, 1)
            c.seq += 3

        def split_load(src, hi):
            with act.Fori(0, KD // 2) as i:
                for r in range(2):
                    act.wait_ge(*sp_dve.at(f"l{r}", i + (c.split - 1)))
                    act.dma_start(ysg[:, r, :], src[i * 2 + r]).then_inc(sp_in[r], 16)
                for r in range(2):
                    act.wait_ge(sp_in[r], (i + (c.split + 1)) * 16)
                    activation(hi[:, i * 2 + r, :], ysg[:, r, :], ACT.Copy).then_inc(*sp_act.sig(f"c{r}"))
            c.split += 4

        def merge():
            def load_gates(i, r):
                for n in range(2):
                    act.dma_start(sg[:, r, n, :], gates_d[n, i * 2 + r]).then_inc(sg_in[r], 16)

            for r in range(2):
                load_gates(0, r)

            def chunks(i, more):
                for r in range(2):
                    act.wait_ge(*mg_dve.at(f"mo{r}", i))
                    activation(hhi[:, i * 2 + r, :], mo[:, r, :], ACT.Copy).then_inc(*mg_act.sig(f"h{r}"))
                    if more:
                        load_gates(i + 1, r)

            with act.Fori(0, KD // 2 - 1) as i:
                chunks(i, True)
            chunks(KD // 2 - 1, False)
            c.advance(unit=KD, dve=2 * KD)

        def keys_values():
            squares(memx, memq)
            norm(memr[:, 0, :], memr[:, 1, :], memh, memhi)
            with act.Fori(0, KD // 2) as i:
                for r in range(2):
                    output_ready(i * 2 + (c.unit + r))
                    activation(kTx[:, i * 2 + r, :], bank_act(c.act + r)[:, 0, 0:MEM], ACT.Copy).then_inc(act_free, 1)
            c.advance(unit=KD, act=KD)
            with act.Fori(0, KD // 2) as i:
                for r in range(2):
                    output_ready(i * 2 + (c.unit + r))
                    activation(vx[:, :, bass.ds((i * 2 + r) * P, P)], bank_act(c.act + r)[:, :, 0:P],
                               ACT.Copy).then_inc(act_free, 1)
            c.advance(unit=KD, act=KD)

        def attend():
            with act.Fori(0, NSEG) as i:
                g0, g1, g2, g3 = G
                act.wait_ge(*xa_pe.at("S", i - 1))
                activation(qs[:], qT[:, :, bass.ds(i * SEG, SEG)], ACT.Copy).then_inc(*xa_act.sig("q"))
                act.wait_ge(*xa_dve.at("nmx", i))
                for h in range(XH):
                    last = activation(sx[:, h, :], flat(g0[:])[:, h * MEM:(h + 1) * MEM], ACT.Exp, scale=XA_SCALE,
                                      bias=mx[:, XH + h:XH + h + 1], accum_out=mx[:, 2 * XH + h:2 * XH + h + 1])
                last.then_inc(*xa_act.sig("e"))
                act.wait_ge(*xa_pe.at("T", i))
                activation(pxt[:].rearrange("p h m t -> p (h m t)"), flat(g1[:]), ACT.Copy).then_inc(*xa_act.sig("pt"))
                act.wait_ge(*xa_pe.at("O", i))
                activation(hhi[:, :, bass.ds(i * SEG, SEG)], flat(g2[:]).rearrange("p (k t) -> p k t", k=KD),
                           ACT.Copy).then_inc(*xa_act.sig("hi"))

        for dst, src in const_loads:
            act.dma_start(dst, src).then_inc(consts_in, 16)
        act.dma_start(xT[:], a["x"]).then_inc(x_in, 16)
        act.wait_ge(consts_in, CONSTS * 16)
        act.wait_ge(x_in, 16)
        squares(xT, nsq)
        ffn()
        act.wait_ge(dve_free, c.dve + credit)
        act.dma_start(x_park, xT[:]).then_inc(store, 16)
        norm_x()
        act.wait_ge(store, 16)
        barrier(act, c)
        project_rw()
        project_ml()
        barrier(act, c)
        act.dma_start(loraw[:, 0, :], a["lora_wa"]).then_inc(x_in, 16)
        act.dma_start(loraw[:, 1, :], a["lora_g"]).then_inc(x_in, 16)
        act.wait_ge(x_in, 5 * 16)
        barrier(act, c)
        mixers(act, iteration)
        act.wait_ge(yr_out, (NSEG + 1) * 16)
        act.wait_ge(ym_out, (NSEG + 1) * 16)
        barrier(act, c)
        split_load(y_d, yhi)
        merge()
        barrier(act, c)
        act.dma_start(xT[:], x_park).then_inc(x_in, 16)
        squares(xT, nsq, residual=True)
        barrier(act, c)
        act.dma_start(memx[:], a["mem"]).then_inc(x_in, 16)
        act.wait_ge(x_in, 7 * 16)
        keys_values()
        norm_x()
        barrier(act, c)
        with act.Fori(0, KD // 2) as i:
            for r in range(2):
                output_ready(i * 2 + (c.unit + r))
                activation(qT[:, i * 2 + r, :], flat(bank_act(c.act + r)[:]), ACT.Copy).then_inc(act_free, 1)
        c.advance(unit=KD, act=KD)
        barrier(act, c)
        attend()
        barrier(act, c)
        squares(xT, nsq, residual=True)
        ffn()
        norm_x(None)
        for k in range(KD):
            act.wait_ge(dve_seq, FINAL_SEQ + k + 1)
            act.dma_start(out[k], xT[:, k, :]).then_inc(store, 16)
        act.wait_ge(store, (1 + KD) * 16)

    @block.vector
    def _(dve):
        c = Count()
        dve.sem_inc(dve_free, credit)
        dve.sem_inc(a_lo, 1)
        for s in DVE_STEPS:
            dve.sem_inc(s.sem, s.n)
        tt, ts, stt = nc.vector.tensor_tensor, nc.vector.tensor_scalar, nc.vector.scalar_tensor_tensor

        def step(ins):
            c.seq += 1
            ins.then_inc(dve_seq, 1)
            dve.wait_ge(dve_seq, c.seq)

        def output_ready(u):
            dve.wait_ge(unit_used, u + (credit + 1))

        def add_squares(i, n, sq, t):
            dve.wait_ge(*nsq_act.at(f"sq{n}", i + c.sq))
            dve.wait_ge(*(nsq_dve.at("add0", i + c.sq) if n else nsq_dve.at("add1", i + (c.sq - 1))))
            tt(t, t, sq[:, n, :], ALU.add).then_inc(*nsq_dve.sig(f"add{n}"))

        def squares(sq, t):
            step(nc.vector.memset(t, 0.0))
            with dve.Fori(0, KD // 2) as i:
                for n in range(2):
                    add_squares(i, n, sq, t)
            c.sq += 4

        def norm(gain, src, width, ms, r, t, h, hi, lo):
            dve.wait_ge(norm_sum, c.norms + 1)
            src_ps = bank_dve(c.dve)
            src_ps = flat(src_ps[:]) if width == T else src_ps[:, 0, 0:width]
            ts(ms, src_ps, 1.0 / D, EPS, ALU.mult, ALU.add).then_inc(norm_ms, 1)
            dve.wait_ge(norm_r, c.norms + 1)
            step(tt(t, r, r, ALU.mult))
            step(tt(t, t, ms, ALU.mult))
            step(ts(t, t, -0.5, 1.5, ALU.mult, ALU.add))
            step(tt(r, r, t, ALU.mult))
            dve.sem_inc(dve_free, 1)
            if hi is not None:
                with dve.Fori(0, KD // 2) as i:
                    for n in range(2):
                        dve.wait_ge(*nh_dve.at(f"l{n}", i + (c.norm - 1)))
                        col = VCOL[gain] + n
                        stt(h[:, n, :], src[:, i * 2 + n, :], vec[:, bass.ds(i * 2 + col, 1)], r, ALU.mult,
                            ALU.mult).then_inc(*nh_dve.sig(f"h{n}"))
                    for n in range(2):
                        dve.wait_ge(*nh_act.at(f"c{n}", i + c.norm))
                        tt(lo[:, i * 2 + n, :], h[:, n, :], hi[:, i * 2 + n, :].bitcast(F32),
                           ALU.subtract).then_inc(*nh_dve.sig(f"l{n}"))
            c.advance(norm=4, norms=1, dve=1)

        def norm_x(gain, hi=hhi):
            norm(gain, xT, T, nms[:], nr[:], nt[:], nh, hi, hlo)

        def residual(scale, last=True):
            if last:
                step(nc.vector.memset(nt[:], 0.0))
            with dve.Fori(0, KD // 2) as i:
                for r in range(2):
                    output_ready(i * 2 + (c.unit + r))
                    x_ = xT[:, i * 2 + r, :]
                    stt(x_, flat(bank_dve(c.dve + r)[:]), scale, x_, ALU.mult, ALU.add).then_inc(dve_free, 1)
                    if last:
                        add_squares(i, r, nsq, nt[:])
            c.advance(unit=KD, dve=KD)
            c.sq += 4 if last else 0

        def ffn(gain):
            norm_x(gain)
            for n in FF_PARTS:
                with loop(dve, n // 2) as i:
                    for r in range(2):
                        dve.wait_ge(act_free, i * 2 + (c.act + r + 1 + credit))
                        output_ready(i * 4 + (c.unit + 2 * r + 1))
                        dve.wait_ge(a_lo, i * 2 + (c.a + r + 1))
                        tt(s1[:], s0[:], flat(bank_dve(c.dve + r)[:]), ALU.mult).then_inc(dve_free, 1)
                        dve.wait_ge(a_hi, i * 2 + (c.a + r + 1))
                        tt(alo[:, i * 2 + r, :], s1[:], ahi[:, i * 2 + r, :].bitcast(F32),
                           ALU.subtract).then_inc(a_lo, 1)
                c.advance(unit=2 * n, act=n, dve=n, a=n)
                residual(0.5, last=n == FF_PARTS[-1])

        def project_rw():
            with dve.Fori(0, RW_UNITS // 2) as i:
                for r in range(2):
                    dve.wait_ge(act_free, i * 2 + (c.act + r + 1 + credit))
                    tt(pd[:, r, :], stg[:, r, 2:2 + T], stg[:, r, 3:3 + T], ALU.subtract).then_inc(*rp_dve.sig(f"d{r}"))
                    dve.wait_ge(*rp_dve.at(f"d{r}", i))
                    dve.wait_ge(z_out[r], (i + 1) * 16)
                    stt(po[:, r, :], pd[:, r, :], vec[:, bass.ds(i * 2 + (VCOL["rw_mu"] + r), 1)], stg[:, r, 3:3 + T],
                        ALU.mult, ALU.add).then_inc(*rp_dve.sig(f"m{r}"))
            c.advance(unit=RW_UNITS, act=RW_UNITS)

        def project_ml():
            with dve.Fori(0, MH) as i:
                for r in range(2):
                    dve.wait_ge(act_free, i * 2 + (c.act + r + 1 + credit))

                    def w(name):
                        return vec[:, bass.ds(i * 2 + (VCOL[name] + r), 1)]

                    dve.wait_ge(silu_made, i * 2 + 16)
                    ts(pd[:, r, :], stg[:, r, 3:3 + T], w("conv_w0"), w("conv_b"), ALU.mult,
                       ALU.add).then_inc(*cv_dve.sig(f"t0{r}"))
                    for j in range(1, 4):
                        dve.wait_ge(*cv_dve.at(f"t{j - 1}{r}", i))
                        stt(pd[:, r, :], stg[:, r, 3 - j:3 - j + T], w(f"conv_w{j}"), pd[:, r, :], ALU.mult,
                            ALU.add).then_inc(*cv_dve.sig(f"t{j}{r}"))
            c.advance(unit=ML_UNITS + 1, act=ML_UNITS + 1)

        def newton(S, names, r, v, w, i):
            tt(flat(w[:]), flat(r[:]), flat(r[:]), ALU.mult).then_inc(*S.sig(names[0]))
            dve.wait_ge(*S.at(names[0], i))
            tt(flat(w[:]), flat(w[:]), flat(v[:]), ALU.mult).then_inc(*S.sig(names[1]))
            dve.wait_ge(*S.at(names[1], i))
            ts(flat(w[:]), flat(w[:]), -0.5, 1.5, ALU.mult, ALU.add).then_inc(*S.sig(names[2]))
            dve.wait_ge(*S.at(names[2], i))
            tt(flat(r[:]), flat(r[:]), flat(w[:]), ALU.mult).then_inc(*S.sig(names[3]))
            dve.wait_ge(*S.at(names[3], i))

        def iteration(i, front, back):
            F, B, M = f_dve, b_dve, m_dve
            j = i - 1
            g0, g1, g2, m0, m1 = G[0], G[1], G[2], G[3][:, 0, :], G[3][:, 1, :]

            def copies(col, n=NH):
                return con(col).unsqueeze(1).to_broadcast([P, n, P])

            def three(ap):
                return ap.rearrange("p (n t) -> p n t", t=SEG)

            def gram(name, dst, src, mask):
                nc.vector.copy_predicated(dst[:], copies(mask).bitcast(U32), three(flat(src[:]))).then_inc(*F.sig(name))

            def output_variance():
                dve.wait_ge(*b_pe.at("var", j))
                ts(flat(yve[:]), g2[:, 1, :], 1.0 / HD, GN_EPS, ALU.mult, ALU.add).then_inc(*B.sig("ve"))

            def output_norm():
                dve.wait_ge(*b_act.at("rsv", j))
                newton(B, ("g1", "g2", "g3", "g4"), yrs, yve, ynw, j)
                tt(Ys[:], Ys[:], yrs[:], ALU.mult).then_inc(*B.sig("y1"))

            if front:
                dve.wait_ge(*f_act.at("gt", i))
                ts(gsig[:], gsig[:], 0.5, 0.5, ALU.mult, ALU.add).then_inc(*F.sig("gs"))
                dve.wait_ge(*f_act.at("tw", i))
                ts(dec[:, :, 1:DEC], dec[:, :, 1:DEC], 1.0, None, ALU.add).then_inc(*F.sig("dec"))
                dve.wait_ge(*F.at("dec", i))
                nc.vector.tensor_tensor_scan(flat(cum[:]), con(C_RST, RC * DEC), flat(dec[:]), 0.0, ALU.mult,
                                             ALU.add).then_inc(*F.sig("scan"))
                dve.wait_ge(*F.at("scan", i))
                ts(hend[:], cum[:, :, DEC - 1:DEC], 0.5, None, ALU.mult).then_inc(*F.sig("hend"))
                dve.wait_ge(*F.at("hend", i))
                tt(dec[:], cum[:], hend[:].to_broadcast([P, RC, DEC]), ALU.subtract).then_inc(*F.sig("cc"))
                dve.wait_ge(*m_pe.at("bca", i))
                dve.wait_ge(*m_pool.at("y3", i - 1))
                tt(argb[:], three(m0), copies(C_ADD, MH), ALU.add).then_inc(*M.sig("arg"))
                dve.wait_ge(*f_act.at("ta", i))
                ts(ga[:], ga[:], 0.5, 0.5, ALU.mult, ALU.add).then_inc(*F.sig("av"))
                dve.wait_ge(*F.at("av", i))
                stt(gu[:], ga[:], -1.0, vbc("rw_k_a", SEG), ALU.add, ALU.mult).then_inc(*F.sig("gu"))
                dve.wait_ge(*F.at("gu", i))
                stt(flat(kmod[:]), flat(gu[:]), 1.0, zs[:, 4:8, :].rearrange("p r t -> p (r t)"), ALU.add,
                    ALU.mult).then_inc(*F.sig("kmod"))
                dve.wait_ge(*f_pe.at("ss", i))
                ts(flat(ssc[:]), g0[:, 0, :], 1e-24, None, ALU.max).then_inc(*F.sig("ssc"))
            if front:
                dve.wait_ge(*f_act.at("rinv", i))
                newton(F, ("n1", "n2", "n3", "rin"), rinv, ssc, nw, i)
                tt(kk[:], kk[:], rinv[:], ALU.mult).then_inc(*F.sig("kk"))
                dve.wait_ge(*F.at("kk", i))
                tt(kka[:], kk[:], ga[:], ALU.mult).then_inc(*F.sig("kka"))
            if back:
                dve.wait_ge(*b_pe.at("dS", j))
                tt(St[:], S0s[:], g1[:, 1, 0:RC * HD].rearrange("p (r v) -> p r v", r=RC), ALU.add).then_inc(*B.sig("dS"))
                dve.wait_ge(*B.at("dS", j))
                tt(St[:], St[:], pend[:].to_broadcast([P, RC, HD]), ALU.mult).then_inc(*B.sig("S"))
            if front:
                dve.wait_ge(*f_pe.at("bonus", i))
                dve.wait_ge(*b_pool.at("bvb", j))
                tt(bv[:], three(g0[:, 1, :]), zs[:, 8:12, :], ALU.mult).then_inc(*F.sig("bv"))
                dve.wait_ge(*f_act.at("Pi", i))
                tt(alpha[:], kk[:], Pp[:, :, 0:SEG], ALU.mult).then_inc(*F.sig("alpha"))
                dve.wait_ge(*F.at("kka", i))
                tt(beta[:], kka[:], Pi[:, :, 1:DEC], ALU.mult).then_inc(*F.sig("beta"))
            if back:
                dve.wait_ge(*b_pe.at("mean", j))
                stt(flat(Ys[:]), g2[:, 0, :], -1.0 / HD, flat(Ys[:]), ALU.mult, ALU.add).then_inc(*B.sig("yc"))
            if not front:
                output_variance()
                output_norm()
                return
            dve.wait_ge(*f_pe.at("A", i))
            tt(pend[:], Pp[:, :, DEC - 1:DEC], con(C_ONES, 1).unsqueeze(1).to_broadcast([P, RC, 1]),
               ALU.mult).then_inc(*F.sig("pend"))
            gram("A", Am, g1, C_LOW)
            dve.wait_ge(*F.at("A", i))
            tt(AL[:, 0], Am[:], copies(C_LEV), ALU.mult).then_inc(*F.sig("am0"))
            if back:
                output_variance()
            dve.wait_ge(*m_act.at("D", i))
            dve.wait_ge(*m_pe.at("S", i))
            stt(flat(Pb[:]), m0, ML_SCALE, flat(Db[:]), ALU.mult, ALU.mult).then_inc(*M.sig("P"))
            gram("Mu", Mu, g0, C_UPEQ)
            dve.wait_ge(*f_pe.at("am0T", i))
            tt(Ur[:], copies(C_ID), three(flat(g1[:])), ALU.subtract).then_inc(*F.sig("U0"))
            dve.wait_ge(*f_pe.at("B", i))
            stt(flat(qe[:]), zm[:, 0:MH, :].rearrange("p h t -> p (h t)"), ML_SCALE, flat(Eb[:]), ALU.mult,
                ALU.mult).then_inc(*M.sig("qe"))
            gram("B", Bm, g0, C_UP)
            for n in range(1, LEVELS):
                if n == 4:
                    dve.wait_ge(*m_act.at("aden", i))
                    tt(aden[:], aden[:], nmb[:], ALU.max).then_inc(*M.sig("dmax"))
                    dve.wait_ge(*M.at("dmax", i))
                    nc.vector.reciprocal(flat(aden[:]), flat(aden[:])).then_inc(*M.sig("rec"))
                    dve.wait_ge(*M.at("rec", i))
                    tt(flat(hm[:]), m1, flat(aden[:]), ALU.mult).then_inc(*M.sig("hm"))
                dve.wait_ge(*f_pe.at(f"E{n}", i))
                tt(flat(Ur[:]), flat(Ur[:]).bitcast(F32), flat(g0[:]), ALU.subtract).then_inc(*F.sig(f"U{n}"))
                if n == 1:
                    dve.wait_ge(*b_dve.at("S", j))
                    dve.wait_ge(*f_pe.at("Mv", i))
                    tt(S0s[:], St[:], Pi[:, :, 0:1].to_broadcast([P, RC, HD]), ALU.mult).then_inc(*F.sig("S0s"))
                    gram("Mv", Mv, g2, C_UPEQ)
                    if back:
                        output_norm()
                if n == 4:
                    dve.wait_ge(*m_pool.at("dec", i))
                    dve.wait_ge(*m_pe.at("dN", i))
                    tt(CN[:].rearrange("p a h t -> p (a h t)"), CN[:].rearrange("p a h t -> p (a h t)"), flat(G[3][:]),
                       ALU.add).then_inc(*M.sig("C"))
                if n == 5:
                    dve.wait_ge(*m_pe.at("mean", i))
                    stt(flat(hm[:]), m0, -1.0 / P, flat(hm[:]), ALU.mult, ALU.add).then_inc(*M.sig("yc"))
            dve.wait_ge(*m_pe.at("var", i))
            ts(flat(mve[:]), m1, 1.0 / P, ML_EPS, ALU.mult, ALU.add).then_inc(*M.sig("ve"))
            dve.wait_ge(*f_pool.at("IU", i))
            dve.wait_ge(*f_pe.at("F", i))
            tt(flat(Qr[:]), flat(Uf[:]), flat(g1[:]), ALU.subtract).then_inc(*F.sig("Q"))
            dve.wait_ge(*f_pe.at("UQ", i))
            tt(flat(Uf[:]), flat(Ur[:]).bitcast(F32), flat(g0[:]), ALU.add).then_inc(*F.sig("Uf"))
            dve.wait_ge(*m_act.at("rsv", i))
            newton(M, ("g1", "g2", "g3", "g4"), mrs, mve, mnw, i)
            tt(hm[:], hm[:], mrs[:], ALU.mult).then_inc(*M.sig("y1"))

        def mlstm_rows():
            assert c.seq == ROWS_SEQ, c.seq
            dve.wait_ge(x_in, 3 * 16)
            step(ts(grow[:], grow[:], gbias[:, 1:2], None, ALU.add))
            step(ts(ifr[:], ifr[:], gbias[:, 0:1], None, ALU.add))
            step(ts(brow[:], grow[:], 0.0, None, ALU.min))
            dve.wait_ge(act_seq, ROWS_ACT + 3)
            step(tt(brow[:], brow[:], nrow[:], ALU.subtract))
            step(nc.vector.tensor_tensor_scan(mrow[:], brow[:], ifr[:], 0.0, ALU.add, ALU.max))
            for n in range(NSEG):
                cols = slice(n * SEG, (n + 1) * SEG)
                step(nc.vector.tensor_tensor_scan(arow[:, cols], con(C_ONES, P, MH), brow[:, cols], 0.0, ALU.mult,
                                                  ALU.add))
            step(tt(grow[:], ifr[:], arow[:], ALU.subtract))
            step(tt(arow[:], arow[:], mrow[:], ALU.subtract))
            step(nc.vector.tensor_copy(erow[:, 0:SEG], arow[:, 0:SEG]))
            before = mrow[:].rearrange("p (n t) -> p n t", n=NSEG)[:, 0:NSEG - 1, SEG - 1:SEG]
            step(tt(erow[:, SEG:T].rearrange("p (n t) -> p n t", n=NSEG - 1),
                    arow[:, SEG:T].rearrange("p (n t) -> p n t", n=NSEG - 1),
                    before.to_broadcast([MH, NSEG - 1, SEG]), ALU.add))

        def split_load(hi, lo):
            with dve.Fori(0, KD // 2) as i:
                for r in range(2):
                    dve.wait_ge(*sp_act.at(f"c{r}", i + c.split))
                    tt(lo[:, i * 2 + r, :], ysg[:, r, :], hi[:, i * 2 + r, :].bitcast(F32),
                       ALU.subtract).then_inc(*sp_dve.sig(f"l{r}"))
            c.split += 4

        def merge():
            S = mg_dve
            with dve.Fori(0, KD // 2) as i:
                for r in range(2):
                    output_ready(i * 2 + (c.unit + r))
                    dve.wait_ge(sg_in[r], i * 32 + 32)
                    dve.wait_ge(*S.at(f"l{r}", i - 1))
                    tt(mo[:, r, :], sg[:, r, 0, :], flat(bank_dve(c.dve)[:]), ALU.mult).then_inc(*S.sig(f"p{r}"))
                    tt(sg[:, r, 1, :], sg[:, r, 1, :], flat(bank_dve(c.dve + 1)[:]), ALU.mult).then_inc(*S.sig(f"q{r}"))
                    dve.wait_ge(*S.at(f"q{r}", i))
                    dve.sem_inc(dve_free, 2)
                    tt(mo[:, r, :], mo[:, r, :], sg[:, r, 1, :], ALU.add).then_inc(*S.sig(f"mo{r}"))
                    dve.wait_ge(*mg_act.at(f"h{r}", i))
                    tt(hlo[:, i * 2 + r, :], mo[:, r, :], hhi[:, i * 2 + r, :].bitcast(F32),
                       ALU.subtract).then_inc(*S.sig(f"l{r}"))
            c.advance(unit=KD, dve=2 * KD)

        def attend():
            S = xa_dve
            with dve.Fori(0, NSEG) as i:
                g0, g1, g2, g3 = G
                dve.wait_ge(*xa_pe.at("S", i))
                nc.vector.reduce_max(mx[:, 0:XH], flat(g0[:]).rearrange("p (h m) -> p h m", h=XH),
                                     AX_X).then_inc(*S.sig("mx"))
                dve.wait_ge(*S.at("mx", i))
                ts(mx[:, XH:2 * XH], mx[:, 0:XH], -XA_SCALE, None, ALU.mult).then_inc(*S.sig("nmx"))
                dve.wait_ge(*xa_act.at("e", i))
                nc.vector.reciprocal(mx[:, 3 * XH:4 * XH], mx[:, 2 * XH:3 * XH]).then_inc(*S.sig("r"))
                dve.wait_ge(*S.at("r", i))
                tt(px[:], sx[:], mx[:, 3 * XH:4 * XH].unsqueeze(2).to_broadcast([P, XH, MEM]),
                   ALU.mult).then_inc(*S.sig("p"))
                dve.wait_ge(*xa_act.at("hi", i))
                cols = bass.ds(i * SEG, SEG)
                tt(hlo[:, :, cols], flat(g2[:]).rearrange("p (k t) -> p k t", k=KD), hhi[:, :, cols].bitcast(F32),
                   ALU.subtract).then_inc(*S.sig("lo"))

        dve.wait_ge(consts_in, CONSTS * 16)
        dve.wait_ge(x_in, 16)
        step(ts(hw0[:], vec[:, VCOL["rw_w0"]:VCOL["rw_w0"] + 2 * RC], 0.5, None, ALU.mult))
        squares(nsq, nt[:])
        ffn("ffn1_norm")
        dve.wait_ge(dve_free, c.dve + credit)
        norm_x("mix_norm")
        barrier(dve, c)
        for r in range(2):
            step(nc.vector.memset(stg[:, r, 0:3], 0.0))
        project_rw()
        c.z = RW_UNITS // 2 + MH + MH // 2 * 2
        project_ml()
        mlstm_rows()
        c.advance(unit=2 * KD, act=2 * KD)
        barrier(dve, c)
        step(nc.vector.tensor_copy(idr[:], con(C_ID)))
        for m in (Am, Bm, Mv, Mu, St, dec, CN):
            step(nc.vector.memset(m[:], 0.0))
        barrier(dve, c)
        mixers(dve, iteration)
        barrier(dve, c)
        split_load(yhi, ylo)
        merge()
        barrier(dve, c)
        dve.wait_ge(x_in, 6 * 16)
        residual(1.0)
        barrier(dve, c)
        dve.wait_ge(x_in, 7 * 16)
        squares(memq, memr[:, 2, :])
        norm("mem_norm", memx, MEM, memr[:, 0, :], memr[:, 1, :], memr[:, 2, :], memh, memhi, memlo)
        c.advance(unit=2 * KD, act=2 * KD)
        norm_x("xa_norm")
        barrier(dve, c)
        c.advance(unit=KD, act=KD)
        barrier(dve, c)
        attend()
        barrier(dve, c)
        residual(1.0)
        ffn("ffn2_norm")
        dve.wait_ge(dve_free, c.dve + credit)
        norm_x("final_norm", None)
        assert c.seq == FINAL_SEQ, c.seq
        for k in range(KD):
            x_ = xT[:, k, :]
            stt(x_, x_, v1("final_norm", k), nr[:], ALU.mult, ALU.mult).then_inc(dve_seq, 1)

    ctx.close()


def constants():
    c = np.zeros((P, NCONST), np.float32)
    p, f = np.arange(P)[:, None], np.arange(P)[None, :]
    c[:, C_ID:C_ID + P] = p == f
    c[:, C_ONES:C_ONES + P] = 1
    c[:, C_HONES:C_HONES + P] = p // HD == f // HD
    c[:, C_LOW:C_LOW + P] = f < p
    c[:, C_UP:C_UP + P] = p < f
    c[:, C_UPEQ:C_UPEQ + P] = p <= f
    for n in range(LEVELS):
        b = 1 << n
        c[:, C_LEV + n * P:C_LEV + (n + 1) * P] = (p // (2 * b) == f // (2 * b)) & (p // b % 2 == 1) & (f // b % 2 == 0)
    c[:, C_ADD:C_ADD + P] = np.where(p <= f, 0.0, -1e30)
    c[:, C_RST:C_RST + RC * DEC] = np.arange(RC * DEC) % DEC != 0
    for h in range(MH):
        c[h, C_SEL + h * P:C_SEL + (h + 1) * P] = 1
    c[:, C_RSC] = 10 * np.log(2.0)
    return c


def kernel(**inputs):
    import concourse.bacc as bacc
    from concourse.bass_utils import run_bass_kernel_spmd

    g = {k: np.asarray(v) for k, v in inputs.items()}

    def units(w):
        k, n = w.shape[0] // P, w.shape[1] // P
        return np.ascontiguousarray(w.reshape(k, P, n, P).transpose(2, 1, 0, 3).reshape(n, P, k * P))

    def cols(v):
        return v.reshape(-1, P).T

    arrays = {}
    for f in ("ffn1", "ffn2"):
        n = f[-1]
        arrays[f"wg{n}"] = units(g[f"{f}_w_gate"][0])
        arrays[f"wu{n}"] = units(g[f"{f}_w_up"][0])
        at = 0
        for part, c in enumerate(FF_PARTS):
            arrays[f"wd{n}_{part}"] = units(g[f"{f}_w_down"][0][at * P:(at + c) * P])
            at += c
    w_in = g["w_in"][0]
    rw, mlc = RW_UNITS * P, ML_UNITS * P
    arrays["rw_in"] = units(w_in[:, :rw])
    arrays["ml_in"] = units(w_in[:, rw:rw + mlc])
    wif = np.zeros((D, P), np.float32)
    wif[:, :2 * MH] = w_in[:, rw + mlc:rw + mlc + 2 * MH]
    arrays["if_in"] = units(wif)
    gates = rw + mlc + 2 * MH
    arrays["ga_in"] = units(w_in[:, gates:gates + D])
    arrays["gb_in"] = units(w_in[:, gates + D:])
    arrays["up"] = units(np.concatenate([g["w_up_rw"][0], g["w_up_ml"][0]], axis=0))
    arrays["w_out"] = units(g["w_out"][0])
    arrays["wq"] = units(g["xa_wq"][0])
    arrays["wkv"] = units(g["xa_wkv"][0])
    arrays["wo"] = units(g["xa_wo"][0])
    arrays["lora_wa"] = np.concatenate([g["rw_w2"][0], g["rw_a2"][0]], axis=0)
    arrays["lora_g"] = np.ascontiguousarray(g["rw_g2"][0])
    arrays["x"] = np.ascontiguousarray(g["x"][0].T.reshape(KD, P, T).transpose(1, 0, 2))
    arrays["mem"] = np.ascontiguousarray(g["mem"][0].T.reshape(KD, P, MEM).transpose(1, 0, 2))
    vecs = {n: g[n] if n == "final_norm" else g[n][0] for n, _ in VECS if n in g}
    for j in range(4):
        vecs[f"conv_w{j}"] = g["ml_conv_w"][0, j]
    vecs["conv_b"] = g["ml_conv_b"][0]
    arrays["vecs"] = np.ascontiguousarray(np.concatenate([cols(vecs[n].reshape(-1)) for n, _ in VECS], axis=1))
    arrays["gate_b"] = np.ascontiguousarray(np.stack([g["ml_i_b"][0], g["ml_f_b"][0]], axis=1))
    arrays["consts"] = constants()

    nc = bacc.Bacc("TRN2", target_bir_lowering=False, num_devices=1)
    aps = {n: nc.dram_tensor(f"in_{n}", v.shape, F32, kind="ExternalInput").ap() for n, v in arrays.items()}
    out = nc.dram_tensor("out", [KD, P, T], F32, kind="ExternalOutput").ap()
    layer_kernel(nc, aps, out)
    res = run_bass_kernel_spmd(nc, [{f"in_{n}": v for n, v in arrays.items()}], core_ids=[0])
    return res.results[0]["out"].reshape(D, T).T.reshape(1, T, D)
```

```python
from contextlib import ExitStack, nullcontext

import numpy as np

import concourse.bass as bass
from concourse import mybir

P = 128
D = 1024
T = 1024
KD = D // P
HALF = 512
NHALF = T // HALF
MEM = 256
FF = 2816
FFC = FF // P
FF_PARTS = (8, 8, 6)
SEG = 128
NSEG = T // SEG
NH = 8
HD = 64
RC = 4
MH = 4
XH = 4
RW_UNITS = 14
ML_UNITS = 16
LEVELS = 7
DEC = SEG + 1

EPS = 1e-5
GN_EPS = 64e-5
ML_EPS = 1e-6
KAPPA = float(np.exp(-0.5)) / 2
ML_SCALE = P ** -0.5
XA_SCALE = (D // XH) ** -0.5

ALU = mybir.AluOpType
ACT = mybir.ActivationFunctionType
F32 = mybir.dt.float32
F32R = mybir.dt.float32r
U32 = mybir.dt.uint32
AX_X = mybir.AxisListType.X

C_ID, C_ONES, C_HONES, C_LOW, C_UP, C_UPEQ, C_LEV = (n * P for n in range(7))
C_ADD = C_LEV + LEVELS * P
C_RST = C_ADD + P
C_SEL = C_RST + RC * DEC
C_RSC = C_SEL + MH * P
C_ZERO = C_RSC + 1
NCONST = C_ZERO + 1
CONSTS = 3

VECS = [("ffn1_norm", 8), ("mix_norm", 8), ("xa_norm", 8), ("mem_norm", 8), ("ffn2_norm", 8), ("final_norm", 8),
        ("rw_mu", 14), ("rw_w0", 4), ("rw_a0", 4), ("rw_k_k", 4), ("rw_k_a", 4), ("rw_r_k", 4), ("rw_gn_w", 4),
        ("rw_gn_b", 4), ("conv_w0", 8), ("conv_w1", 8), ("conv_w2", 8), ("conv_w3", 8), ("conv_b", 8),
        ("ml_norm", 4)]
VCOL = {}
NVEC = 0
for _n, _w in VECS:
    VCOL[_n] = NVEC
    NVEC += _w


class Steps:

    def __init__(self, sem, names):
        self.sem, self.names, self.n = sem, names, len(names)
        self.where = {name: k + 1 for k, name in enumerate(names)}
        self.next = 0
        assert len(self.where) == self.n

    def sig(self, name):
        assert self.names[self.next % self.n] == name, (name, self.names[self.next % self.n])
        self.next += 1
        return self.sem, 1

    def at(self, name, it):
        return self.sem, (it + 1) * self.n + self.where[name]


L_PE, L_ACT, L_POOL = ["lora"], ["th", "ad", "tw", "ta", "gt"], ["kkr", "sq"]
F_PE = (["ss", "bonus", "aT", "vT", "bT", "kT", "A", "Mu", "am0T", "B", "W1", "E1", "Mv"]
        + [x for n in range(2, LEVELS) for x in (f"W{n}", f"V{n - 1}", f"E{n}")]
        + ["F", f"V{LEVELS - 1}", "UQ", "Wst", "Z", "gate"])
F_ACT = (["P", "Pi", "lnn", "rinv", "atok", "vtok", "btok", "ktok", "Wc1"]
         + [x for n in range(2, LEVELS) for x in (f"Wc{n}", f"Tc{n - 1}")] + [f"Tc{LEVELS - 1}", "W1c", "Zc", "gev"])
F_DVE = (["dec", "scan", "hend", "cc", "gs", "av", "gu", "kmod", "ssc", "n1", "n2", "rin", "kk", "kka",
          "alpha", "beta", "bv", "pend", "A", "am0", "Mu", "U0", "B", "U1", "S0s", "Mv"]
         + [f"U{n}" for n in range(2, LEVELS)] + ["Q", "Uf"])
F_POOL = ["rk", "rkb", "kap", "rho", "T0"] + [f"am{n}" for n in range(1, LEVELS)] + ["IU"]
B_PE = ["U", "Y", "dS", "mean", "var"]
B_ACT = ["Un", "Y0", "Y1", "lnv", "rsv"]
B_DVE = ["dS", "S", "yc", "ve", "g1", "g2", "g3", "y1"]
B_POOL = ["bvb", "ysq", "y2", "y3", "y4"]
M_PE = ["bca", "bce", "bcn", "gT", "kT", "vT", "S", "num", "den", "dC", "dN", "mean", "var"]
M_ACT = ["gst", "E", "nm", "gtok", "ktok", "vtok", "D", "aden", "lnv", "rsv"]
M_DVE = ["arg", "P", "qe", "dmax", "rec", "hm", "C", "yc", "ve", "g1", "g2", "g3", "y1"]
M_POOL = ["kw", "dec", "ysq", "y2", "y3"]
XP_PE, XP_ACT, XP_DVE = ["S"], ["q", "e"], ["mx", "nmx", "r", "p"]
XO_PE, XO_ACT, XO_DVE = ["T", "O"], ["pt", "hi"], ["lo"]


ROWS_SEQ, ROWS_ACT, FINAL_SEQ = 11, 2, 52


def layer_kernel(nc, a, out):
    ctx = ExitStack()
    sems = {}

    def sem(name):
        if name not in sems:
            sems[name] = ctx.enter_context(nc.semaphore(name))
        return sems[name]

    def dram(name, shape):
        return nc.dram_tensor(name, shape, F32, kind="Internal").ap()

    x_park = dram("x_park", [P, KD, T])
    zrw_d = dram("zrw_d", [RW_UNITS, P, T])
    zml_d = dram("zml_d", [ML_UNITS, P, T])
    gates_d = dram("gates_d", [2, KD, P, T])
    y_d = dram("y_d", [KD, P, T])

    base = (nc.sbuf_base + 63) // 64 * 64
    end = nc.sbuf_usable_end
    top = {}

    def place(group, after, name, shape, dt=F32):
        at = top.get(group, top[after] if after else base)
        size = int(np.prod(shape[1:])) * 4
        top[group] = at + (size + 63) // 64 * 64
        assert top[group] <= end, (group, name, top[group] - end)
        return nc.alloc_sbuf_tensor_at(name, shape, dt, offset=at)

    cst = place("small", None, "cst", [P, NCONST])
    vec = place("small", None, "vec", [P, NVEC])
    hw0 = place("small", None, "hw0", [P, 2 * RC])
    gbias = place("small", None, "gbias", [MH, 2])
    raw = place("common", "small", "raw", [P, 2, KD * P])
    whi = place("common", "small", "whi", [P, 2, KD * P], F32R)
    wlo = place("common", "small", "wlo", [P, 2, KD * P], F32R)
    hhi = place("common", "small", "hhi", [P, KD, T], F32R)
    hlo = place("common", "small", "hlo", [P, KD, T], F32R)
    xT = place("x", "common", "xT", [P, KD, T])
    ahi = place("ffn", "x", "ahi", [P, max(FF_PARTS), T], F32R)
    alo = place("ffn", "x", "alo", [P, max(FF_PARTS), T], F32R)
    s0 = nc.alloc_sbuf_tensor_at("s0", [P, T], F32, offset=end // 64 * 64 - 8192)
    s1 = nc.alloc_sbuf_tensor_at("s1", [P, T], F32, offset=end // 64 * 64 - 4096)
    assert top["ffn"] <= end // 64 * 64 - 8192, top["ffn"] - end
    def at_x(name, kib, shape):
        at = top["x"] + kib * 1024
        assert at + int(np.prod(shape[1:])) * 4 <= end
        return nc.alloc_sbuf_tensor_at(name, shape, F32, offset=at)

    nh = at_x("nh", 0, [P, 2, T])
    nr = at_x("nr", 8, [P, T])
    nsq = at_x("nsq", 24, [P, 2, T])
    nt = at_x("nt", 56, [P, T])
    nms = at_x("nms", 60, [P, T])
    stg = place("proj", "common", "stg", [P, 2, T + 3])
    pd = place("proj", "common", "pd", [P, 2, T])
    po = place("proj", "common", "po", [P, 2, T])
    ifs = place("proj", "common", "ifs", [P, T])
    zs = place("mix", "small", "zs", [P, RW_UNITS, SEG])
    loraw = place("mix", "small", "loraw", [P, 2, RC * P])
    lora = place("mix", "small", "lora", [P, SEG])
    gsig = place("mix", "small", "gsig", [P, SEG])
    dec, cum, Pp, Pi = (place("mix", "small", n, [P, RC, DEC]) for n in ("dec", "cum", "Pp", "Pi"))
    hend, pend = (place("mix", "small", n, [P, RC, 1]) for n in ("hend", "pend"))
    idr = place("mix", "small", "idr", [P, RC * P], F32R)

    def mix(name, shape=(P, RC, SEG), dt=F32):
        return place("mix", "small", name, list(shape), dt)

    kk, ksq, rkb, ssc, rinv, nw, ga, kmod, alpha, beta, kap, rho, gout, bv, atok, btok, ktok, vtok, W1m = (
        mix(n) for n in ("kk", "ksq", "rkb", "ssc", "rinv", "nw", "ga", "kmod", "alpha", "beta", "kap", "rho", "gout",
                         "bv", "atok", "btok", "ktok", "vtok", "W1m"))
    gu, kka = rkb, nw
    Am, Bm, Mv, Mu, Uf = (mix(n, (P, NH, SEG)) for n in ("Am", "Bm", "Mv", "Mu", "Uf"))
    Ur, Tr, Wr, Qr = (mix(n, (P, NH, SEG), F32R) for n in ("Ur", "Tr", "Wr", "Qr"))
    AL = mix("AL", (P, 2, NH, SEG), F32R)
    Zm, Un = mix("Zm", (P, NH, HD)), mix("Un", (P, NH, HD))
    St, S0s = mix("St", (P, RC, HD)), mix("S0s", (P, RC, HD))
    Ys, ysq, yve, yrs, bvb, yo = (mix(n) for n in ("Ys", "ysq", "yve", "yrs", "bvb", "yo"))
    ynw = ysq
    zm = mix("zm", (P, ML_UNITS, SEG))
    gst, gtok = mix("gst", (MH, SEG)), mix("gtok", (P, MH))
    Eb, nmb, Db, Pb, qe, kw, mktok, mvtok, aden, hm, myo = (mix(n) for n in (
        "Eb", "nmb", "Db", "Pb", "qe", "kw", "mktok", "mvtok", "aden", "hm", "myo"))
    argb, mysq, mve, mrs, mnw = hm, Pb, qe, nmb, aden
    CN = mix("CN", (P, 2, MH, SEG))
    ifr, brow, nrow, mrow, arow, erow, grow = (
        nc.alloc_sbuf_tensor_at(n, [MH, T], F32, offset=end // 64 * 64 - (7 - k) * 4096)
        for k, n in enumerate(("ifr", "brow", "nrow", "mrow", "arow", "erow", "grow")))
    assert top["mix"] <= end // 64 * 64 - 4 * 4096 and top["proj"] <= end // 64 * 64 - 7 * 4096
    yhi = place("merge", "common", "yhi", [P, KD, T], F32R)
    ylo = place("merge", "common", "ylo", [P, KD, T], F32R)
    ysg = place("merge", "common", "ysg", [P, 2, T])
    sg = place("merge", "common", "sg", [P, 2, 2, T])
    mo = place("merge", "common", "mo", [P, 2, T])
    qT = place("xa", "x", "qT", [P, KD, T])
    kTx = place("xa", "x", "kTx", [P, KD, MEM])
    vx = place("xa", "x", "vx", [P, 2, D])
    qs = place("xa", "x", "qs", [P, KD, SEG])
    sx = place("xa", "x", "sx", [P, XH, MEM])
    px = place("xa", "x", "px", [P, XH, MEM])
    pxt = place("xa", "x", "pxt", [P, XH, 2, SEG])
    mx = place("xa", "x", "mx", [P, 4 * XH])
    ox = place("xa", "x", "ox", [P, KD, SEG])
    memx = at_x("memx", 12, [P, KD, MEM])
    memq = at_x("memq", 20, [P, 2, MEM])
    memh = at_x("memh", 22, [P, 2, MEM])
    memhi = nc.alloc_sbuf_tensor_at("memhi", [P, KD, MEM], F32R, offset=top["x"] + 48 * 1024)
    memlo = nc.alloc_sbuf_tensor_at("memlo", [P, KD, MEM], F32R, offset=top["x"] + 64 * 1024)
    memr = at_x("memr", 72, [P, 3, MEM])

    G = [nc.alloc_psum_tensor(f"G{n}", [P, NHALF, HALF], F32) for n in range(4)]

    def flat(ap):
        return ap.rearrange("p a b -> p (a b)")

    def con(col, n=P, rows=P):
        return cst[0:rows, col:col + n]

    def v1(name, k=0):
        return vec[:, VCOL[name] + k:VCOL[name] + k + 1]

    def vbc(name, width):
        return vec[:, VCOL[name]:VCOL[name] + RC].unsqueeze(2).to_broadcast([P, RC, width])

    const_loads = [(cst[:], a["consts"]), (vec[:], a["vecs"]), (gbias[:], a["gate_b"])]

    credit = 64
    consts_in = sem("consts_in")
    x_in = sem("x_in")
    xc_in = [sem(f"xc_in{n}") for n in range(KD // 2)]
    raw_in = [sem("raw_in0"), sem("raw_in1")]
    hi_made = sem("hi_made")
    split_made = sem("split_made")
    unit_used = sem("unit_used")
    act_free = sem("act_free")
    dve_free = sem("dve_free")
    phase_end = sem("phase_end")
    dve_seq = sem("dve_seq")
    act_seq = sem("act_seq")
    a_hi = sem("a_hi")
    a_lo = sem("a_lo")
    norm_sum = sem("norm_sum")
    norm_ms = sem("norm_ms")
    norm_r = sem("norm_r")
    z_out = [sem("z_out0"), sem("z_out1")]
    silu_made = sem("silu_made")
    store = sem("store")

    nsq_act = Steps(sem("nsq_act"), ["sq0", "sq1"])
    nsq_dve = Steps(sem("nsq_dve"), ["add0", "add1"])
    nh_act = Steps(sem("nh_act"), ["c0", "c1"])
    nh_dve = Steps(sem("nh_dve"), ["h0", "h1", "l0", "l1"])
    rp_dve = Steps(sem("rp_dve"), ["d0", "m0", "d1", "m1"])
    cv_dve = Steps(sem("cv_dve"), [f"t{j}{r}" for r in range(2) for j in range(4)])
    sp_in = [sem("sp_in0"), sem("sp_in1")]
    sp_act = Steps(sem("sp_act"), ["c0", "c1"])
    sp_dve = Steps(sem("sp_dve"), ["l0", "l1"])
    sg_in = [sem("sg_in0"), sem("sg_in1")]
    mg_act = Steps(sem("mg_act"), ["h0", "h1"])
    mg_dve = Steps(sem("mg_dve"), ["p0", "q0", "mo0", "l0", "p1", "q1", "mo1", "l1"])
    l_pe, l_act, l_pool = (Steps(sem(n), x) for n, x in (("l_pe", L_PE), ("l_act", L_ACT), ("l_pool", L_POOL)))
    f_pe, f_act, f_dve, f_pool = (Steps(sem(n), x) for n, x in (
        ("f_pe", F_PE), ("f_act", F_ACT), ("f_dve", F_DVE), ("f_pool", F_POOL)))
    b_pe, b_act, b_dve, b_pool = (Steps(sem(n), x) for n, x in (
        ("b_pe", B_PE), ("b_act", B_ACT), ("b_dve", B_DVE), ("b_pool", B_POOL)))
    m_pe, m_act, m_dve, m_pool = (Steps(sem(n), x) for n, x in (
        ("m_pe", M_PE), ("m_act", M_ACT), ("m_dve", M_DVE), ("m_pool", M_POOL)))
    xp_pe, xp_act, xp_dve = (Steps(sem(n), x) for n, x in (("xp_pe", XP_PE), ("xp_act", XP_ACT), ("xp_dve", XP_DVE)))
    xo_pe, xo_act, xo_dve = (Steps(sem(n), x) for n, x in (("xo_pe", XO_PE), ("xo_act", XO_ACT), ("xo_dve", XO_DVE)))
    zs_in, zm_in = sem("zs_in"), sem("zm_in")
    yr_out, ym_out = sem("yr_out"), sem("ym_out")
    ACT_STEPS = (nsq_act, nh_act, sp_act, mg_act, l_act, f_act, b_act, m_act, xp_act, xo_act)
    DVE_STEPS = (nsq_dve, nh_dve, rp_dve, cv_dve, sp_dve, mg_dve, f_dve, b_dve, m_dve, xp_dve, xo_dve)
    PE_STEPS = (l_pe, f_pe, b_pe, m_pe, xp_pe, xo_pe)
    POOL_STEPS = (l_pool, f_pool, b_pool, m_pool)
    MIX_FREE, MIX_READY, MIX_DONE = 2, 3, 4

    stream = []
    for f in (1, 2):
        if f == 2:
            stream += [(["rw_in"], RW_UNITS, 8, 0), (["ml_in"], ML_UNITS, 8, 0), (["if_in"], 1, 8, 0),
                       (["ga_in", "gb_in"], KD, 8, 0), (["up"], KD, 8, 0), (["w_out"], KD, 8, 0), (["wkv"], 2 * KD, 8, 0),
                       (["wq"], KD, 8, 0), (["wo"], KD, 8, 0)]
        first = 0
        for part, c_ in enumerate(FF_PARTS):
            stream.append(([f"wg{f}", f"wu{f}"], c_, 8, first))
            stream.append(([f"wd{f}_{part}"], KD, c_, 0))
            first += c_

    def runs():
        u = 0
        for names, n, tiles, first in stream:
            yield names, n, tiles, first, u
            u += n * len(names)

    block = ctx.enter_context(nc.Block())

    class Count:

        def __init__(self):
            self.unit = self.act = self.dve = self.seq = self.phase = self.a = 0
            self.norm = self.norms = self.sq = self.z = self.silu = self.split = 0

        def advance(self, unit=0, act=0, dve=0, a=0, z=0, norm=0, norms=0):
            self.unit += unit
            self.act += act
            self.dve += dve
            self.a += a
            self.z += z
            self.norm += norm
            self.norms += norms

    def barrier(eng, c):
        c.phase += 1
        eng.drain().then_inc(phase_end, 1)
        eng.wait_ge(phase_end, 3 * c.phase)

    def loop(eng, n):
        return eng.Fori(0, n) if n > 1 else nullcontext(0)

    def pipelined(eng, iteration, ahead=None):
        if ahead:
            ahead(0)
            iteration(0, True, False)
            with eng.Fori(1, NSEG - 1) as i:
                iteration(i, True, True)
            iteration(NSEG - 1, True, True, more=False)
        else:
            iteration(0, True, False)
            with eng.Fori(1, NSEG) as i:
                iteration(i, True, True)
        iteration(NSEG, False, True)

    def bank_act(n):
        return G[n % 2]

    def bank_dve(n):
        return G[2 + n % 2]

    @block.sync
    def _(sp):
        def segment(ap, i):
            return ap.rearrange("u p t -> p u t")[:, :, bass.ds(i * SEG, SEG)]

        def iteration(i, front, back):
            if front:
                sp.wait_ge(*f_dve.at("Mu", i - 1))
                sp.dma_start(zs[:], segment(zrw_d, i)).then_inc(zs_in, 16)
            if back:
                sp.wait_ge(*m_pool.at("y3", i - 1))
                sp.dma_start(segment(y_d[RC:KD], i - 1), myo[:]).then_inc(ym_out, 16)
            if front:
                sp.dma_start(zm[:], segment(zml_d, i)).then_inc(zm_in, 16)

        def mixers_io():
            sp.wait_ge(phase_end, 3 * MIX_FREE)
            pipelined(sp, iteration)
            sp.wait_ge(phase_end, 3 * MIX_DONE)

        for names, n, tiles, first, u0 in runs():
            w, m = tiles * P, len(names)

            def load(k, name, idx, u):
                sp.wait_ge(split_made, u + (credit - 1))
                sp.dma_start(raw[:, k, 0:w], a[name][idx]).then_inc(raw_in[k], 16)

            if names == ["up"]:
                mixers_io()
            rounds = 1 if m % 2 == 0 or n == 1 else 2
            with loop(sp, n // rounds) as i:
                for r in range(rounds):
                    for j, name in enumerate(names):
                        o = r * m + j
                        load((u0 + o) % 2, name, i * rounds + (r + first), i * (rounds * m) + (u0 + o))

    @block.gpsimd
    def _(pool):
        pool.sem_inc(split_made, credit)
        pool.sem_inc(hi_made, credit)
        for s in POOL_STEPS:
            pool.sem_inc(s.sem, s.n)
        tt = nc.gpsimd.tensor_tensor

        def copies(col):
            return con(col).unsqueeze(1).to_broadcast([P, NH, P])

        def ahead(i):
            pool.wait_ge(zs_in, i * 16 + 16)
            tt(kk[:], zs[:, 4:8, :], vbc("rw_k_k", SEG), ALU.mult).then_inc(*l_pool.sig("kkr"))
            pool.wait_ge(*l_pool.at("kkr", i))
            tt(ksq[:], kk[:], kk[:], ALU.mult).then_inc(*l_pool.sig("sq"))

        def iteration(i, front, back, more=True):
            F, B, M = f_pool, b_pool, m_pool
            j = i - 1
            def output():
                pool.wait_ge(*b_dve.at("y1", j))
                tt(Ys[:], Ys[:], vbc("rw_gn_w", SEG), ALU.mult).then_inc(*B.sig("y2"))
                pool.wait_ge(*B.at("y2", j))
                tt(Ys[:], Ys[:], bvb[:], ALU.add).then_inc(*B.sig("y3"))
                pool.wait_ge(*B.at("y3", j))
                pool.wait_ge(yr_out, i * 16)
                tt(yo[:], Ys[:], gout[:], ALU.mult).then_inc(*B.sig("y4"))

            if back:
                tt(bvb[:], bv[:], vbc("rw_gn_b", SEG), ALU.add).then_inc(*B.sig("bvb"))
            if front:
                pool.wait_ge(*f_dve.at("kmod", i))
                tt(rkb[:], zs[:, 0:4, :], kmod[:], ALU.mult).then_inc(*F.sig("rk"))
                pool.wait_ge(*F.at("rk", i))
                tt(rkb[:], rkb[:], vbc("rw_r_k", SEG), ALU.mult).then_inc(*F.sig("rkb"))
                pool.wait_ge(*f_act.at("Pi", i))
                tt(kap[:], kmod[:], Pi[:, :, 1:DEC], ALU.mult).then_inc(*F.sig("kap"))
                pool.wait_ge(*b_pe.at("Y", j))
                tt(rho[:], zs[:, 0:4, :], Pp[:, :, 1:DEC], ALU.mult).then_inc(*F.sig("rho"))
            if back:
                pool.wait_ge(*b_dve.at("yc", j))
                tt(ysq[:], Ys[:], Ys[:], ALU.mult).then_inc(*B.sig("ysq"))
            if not front:
                output()
                return
            pool.wait_ge(*m_act.at("D", i))
            tt(kw[:], mktok[:], Db[:, :, SEG - 1:SEG].to_broadcast([P, MH, SEG]), ALU.mult).then_inc(*M.sig("kw"))
            pool.wait_ge(*f_dve.at("am0", i))
            tt(Tr[:], copies(C_ID), AL[:, 0].bitcast(F32), ALU.subtract).then_inc(*F.sig("T0"))
            for n in range(1, LEVELS):
                if n == 2:
                    pool.wait_ge(*F.at("T0", i))
                if n >= 2:
                    pool.wait_ge(*f_pe.at("am0T" if n == 2 else f"W{n - 2}", i))
                tt(AL[:, n % 2], Am[:], copies(C_LEV + n * P), ALU.mult).then_inc(*F.sig(f"am{n}"))
                if n == 3 and back:
                    output()
                if n == 4:
                    pool.wait_ge(*m_pe.at("den", i))
                    tt(CN[:], CN[:], Eb[:, :, SEG - 1:SEG].unsqueeze(1).to_broadcast([P, 2, MH, SEG]),
                       ALU.mult).then_inc(*M.sig("dec"))
            pool.wait_ge(*m_dve.at("yc", i))
            tt(mysq[:], hm[:], hm[:], ALU.mult).then_inc(*M.sig("ysq"))
            pool.wait_ge(*f_dve.at(f"U{LEVELS - 1}", i))
            tt(Uf[:], copies(C_ID), Ur[:].bitcast(F32), ALU.subtract).then_inc(*F.sig("IU"))
            if more:
                ahead(i + 1)
            pool.wait_ge(*m_dve.at("y1", i))
            tt(hm[:], hm[:], vbc("ml_norm", SEG), ALU.mult).then_inc(*M.sig("y2"))
            pool.wait_ge(*M.at("y2", i))
            pool.wait_ge(ym_out, i * 16 + 16)
            tt(myo[:], hm[:], zm[:, 12:16, :], ALU.mult).then_inc(*M.sig("y3"))

        pool.wait_ge(consts_in, CONSTS * 16)
        for names, n, tiles, first, u0 in runs():
            w, total = tiles * P, n * len(names)

            def split(k, u, turn):
                pool.wait_ge(unit_used, u + (credit - 1))
                pool.wait_ge(raw_in[k], turn * 16)
                nc.gpsimd.tensor_tensor(whi[:, k, 0:w], raw[:, k, 0:w], cst[:, C_ZERO:C_ZERO + 1].to_broadcast([P, w]),
                                        ALU.add).then_inc(hi_made, 1)
                pool.wait_ge(hi_made, u + (credit + 1))
                nc.gpsimd.tensor_tensor(wlo[:, k, 0:w], raw[:, k, 0:w], whi[:, k, 0:w].bitcast(F32),
                                        ALU.subtract).then_inc(split_made, 1)

            if names == ["up"]:
                pool.wait_ge(phase_end, 3 * MIX_READY)
                pipelined(pool, iteration, ahead)
            rounds = 2 if total > 1 else 1
            with loop(pool, total // rounds) as i:
                for r in range(rounds):
                    u = u0 + r
                    split(u % 2, i * rounds + u, i + (u // 2 + 1))

    @block.tensor
    def _(pe):
        c = Count()
        pe.sem_inc(unit_used, credit)
        for s in PE_STEPS:
            pe.sem_inc(s.sem, s.n)

        def tile3(dst, k, t, hi, lo, start, stop):
            wh, wl = whi[:, k, t * P:(t + 1) * P], wlo[:, k, t * P:(t + 1) * P]
            nc.tensor.matmul(dst, wh, hi, start=start, stop=False)
            nc.tensor.matmul(dst, wh, lo, start=False, stop=False)
            return nc.tensor.matmul(dst, wl, hi, start=False, stop=stop)

        def product(bank, k, tiles, hi, lo, chunk_ready=None):
            if chunk_ready:
                for n, t in enumerate(tiles):
                    chunk_ready(t)
                    for h in range(NHALF):
                        cols = slice(h * HALF, (h + 1) * HALF)
                        last = tile3(bank[:, h, :], k, t, hi[:, n, cols], lo[:, n, cols], n == 0, n == len(tiles) - 1)
                return last
            for h in range(NHALF):
                cols = slice(h * HALF, (h + 1) * HALF)
                for n, t in enumerate(tiles):
                    last = tile3(bank[:, h, :], k, t, hi[:, n, cols], lo[:, n, cols], n == 0, n == len(tiles) - 1)
            return last

        def unit_ready(u):
            pe.wait_ge(split_made, u + (credit + 1))

        def act_bank(n):
            pe.wait_ge(act_free, n + (credit - 1))

        def dve_bank(n):
            pe.wait_ge(dve_free, n + (credit - 1))

        def pairs(n, first, body):
            if first:
                body(0, True)
                with pe.Fori(1, n // 2) as i:
                    body(i, False)
            else:
                with loop(pe, n // 2 if n > 1 else 1) as i:
                    body(i, False)

        def gemm(n, by, tiles=8, hi=hhi, lo=hlo, chunk_ready=None):
            count = c.act if by == "act" else c.dve

            def body(i, first):
                for r in range(min(n, 2)):
                    (act_bank if by == "act" else dve_bank)(i * 2 + (count + r))
                    unit_ready(i * 2 + (c.unit + r))
                    bank = (bank_act if by == "act" else bank_dve)(count + r)
                    product(bank, (c.unit + r) % 2, range(tiles), hi, lo,
                            chunk_ready if first and r == 0 else None).then_inc(unit_used, 1)

            pairs(n, chunk_ready, body)
            c.advance(unit=n, act=n if by == "act" else 0, dve=n if by == "dve" else 0)

        def norm(acc, width, squares=4):
            c.sq += squares
            c.norm += 4
            c.norms += 1
            pe.wait_ge(*nsq_dve.at("add1", c.sq - 1))
            dve_bank(c.dve)
            cols = min(width, HALF)
            for h in range(width // cols):
                last = nc.tensor.matmul(bank_dve(c.dve)[:, h, 0:cols], con(C_ONES), acc[:, h * cols:(h + 1) * cols],
                                        start=True, stop=True)
            last.then_inc(norm_sum, 1)
            c.dve += 1

        def norm_chunk(t):
            pe.wait_ge(*nh_dve.at(f"l{t % 2}", c.norm - 4 + t // 2))

        def arrive():
            c.phase += 1
            pe.drain().then_inc(phase_end, 1)

        def ffn():
            norm(nt, T)
            for part, n in enumerate(FF_PARTS):
                def body(i, first):
                    for r in range(2):
                        act_bank(i * 2 + (c.act + r))
                        unit_ready(i * 4 + (c.unit + 2 * r))
                        product(bank_act(c.act + r), (c.unit + 2 * r) % 2, range(KD), hhi, hlo,
                                norm_chunk if first and r == 0 else None).then_inc(unit_used, 1)
                        dve_bank(i * 2 + (c.dve + r))
                        unit_ready(i * 4 + (c.unit + 2 * r + 1))
                        product(bank_dve(c.dve + r), (c.unit + 2 * r + 1) % 2, range(KD), hhi,
                                hlo).then_inc(unit_used, 1)

                pairs(n, part == 0, body)
                c.advance(unit=2 * n, act=n, dve=n, a=n)

                def activation_chunk(t):
                    pe.wait_ge(a_lo, c.a + 2 - n + t)

                gemm(KD, "dve", tiles=n, hi=ahi, lo=alo, chunk_ready=activation_chunk)

        def ahead(i):
            pe.wait_ge(*f_dve.at("Q", i - 1))
            pe.wait_ge(*l_act.at("ad", i))
            for r in range(RC):
                nc.tensor.matmul(G[1][:, 0, r * P:(r + 1) * P], loraw[0:HD, 0, r * P:(r + 1) * P], lora[0:HD, :],
                                 start=True, stop=True)
                last = nc.tensor.matmul(G[1][:, 1, r * P:(r + 1) * P], loraw[HD:P, 0, r * P:(r + 1) * P],
                                        lora[HD:P, :], start=True, stop=True)
            last.then_inc(*l_pe.sig("lora"))

        def iteration(i, front, back, more=True):
            F, B, M = f_pe, b_pe, m_pe
            j = i - 1
            g0, g1, g2, m0, m1 = G[0], G[1], G[2], G[3][:, 0, :], G[3][:, 1, :]
            heads = [(n, n // RC, n % RC, slice(n // RC * HD, (n // RC + 1) * HD)) for n in range(NH)]

            def turn(dst, src):
                for r in range(RC):
                    last = nc.tensor.transpose(dst[:, r * P:(r + 1) * P], src[:, r, :], con(C_ID))
                return last

            def gram(left, right, dst):
                for n, e, r, rows in heads:
                    last = nc.tensor.matmul(dst[:, e, r * P:(r + 1) * P], left[rows, r, :], right[rows, r, :],
                                            start=True, stop=True)
                return last

            def eight(dst, left, right):
                for n in range(NH):
                    last = nc.tensor.matmul(flat(dst[:])[:, n * P:(n + 1) * P], left[:, n, :], right[:, n, :],
                                            start=True, stop=True)
                return last

            def rows_out(dst, row):
                for h in range(MH):
                    last = nc.tensor.matmul(dst[:, h * SEG:(h + 1) * SEG], cst[0:MH, C_SEL + h * P:C_SEL + (h + 1) * P],
                                            row[:, bass.ds(i * SEG, SEG)], start=True, stop=True)
                return last

            def stay_awake(bank, n):
                for _ in range(n):
                    nc.tensor.matmul(bank, idr[:, 0:P], idr[:], start=True, stop=True)

            if front:
                stay_awake(g0[:, 1, :], 6)
                pe.wait_ge(*f_act.at("Zc", i - 1))
                pe.wait_ge(*l_pool.at("sq", i))
                nc.tensor.matmul(g0[:, 0, :], con(C_HONES), flat(ksq[:]), start=True, stop=True).then_inc(*F.sig("ss"))
                pe.wait_ge(*m_dve.at("ve", i - 1))
                rows_out(m0, arow).then_inc(*M.sig("bca"))
                rows_out(m1, erow).then_inc(*M.sig("bce"))
            if back:
                pe.wait_ge(*f_act.at("gev", j))
                for n, e, r, rows in heads:
                    dst = g2[:, e, r * HD:(r + 1) * HD]
                    nc.tensor.matmul(dst, Uf[:, n, :], Zm[:, n, :], start=True, stop=False)
                    last = nc.tensor.matmul(dst, W1m[rows, r, :], S0s[rows, r, :], start=False, stop=True)
                last.then_inc(*B.sig("U"))
            if front:
                pe.wait_ge(*m_dve.at("arg", i))
                rows_out(m0, mrow).then_inc(*M.sig("bcn"))
                pe.wait_ge(*m_act.at("E", i))
                nc.tensor.matmul(m1[:, 0:MH], gst[:], cst[0:MH, C_ID:C_ID + MH], start=True,
                                 stop=True).then_inc(*M.sig("gT"))
            if back:
                pe.wait_ge(*b_act.at("Un", j))
                for n, e, r, rows in heads:
                    dst = g2[rows, e, r * P:(r + 1) * P]
                    nc.tensor.matmul(dst, vtok[:, r, rows], Mv[:, n, :], start=True, stop=False)
                    nc.tensor.matmul(dst, S0s[rows, r, :], rho[rows, r, :], start=False, stop=False)
                    last = nc.tensor.matmul(dst, Un[:, n, :], Mu[:, n, :], start=False, stop=True)
                last.then_inc(*B.sig("Y"))
                if front:
                    pe.wait_ge(*l_act.at("ta", i))
                for n, e, r, rows in heads:
                    dst = g1[rows, 1, r * HD:(r + 1) * HD]
                    nc.tensor.matmul(dst, ktok[:, r, rows], vtok[:, r, rows], start=True, stop=False)
                    last = nc.tensor.matmul(dst, btok[:, r, rows], Un[:, n, :], start=False, stop=True)
                last.then_inc(*B.sig("dS"))
            if front:
                pe.wait_ge(*l_act.at("ta", i))
                pe.wait_ge(*f_pool.at("rkb", i))
                nc.tensor.matmul(g0[:, 1, :], con(C_HONES), flat(rkb[:]), start=True,
                                 stop=True).then_inc(*F.sig("bonus"))
                pe.wait_ge(zm_in, i * 16 + 16)
                pe.wait_ge(*m_act.at("nm", i))
                turn(m0, zm[:, MH:2 * MH, :]).then_inc(*M.sig("kT"))
                pe.wait_ge(*m_act.at("gtok", i))
                turn(m1, zm[:, 2 * MH:3 * MH, :]).then_inc(*M.sig("vT"))
                pe.wait_ge(*f_dve.at("alpha", i))
                turn(g0[:, 0, :], alpha).then_inc(*F.sig("aT"))
                pe.wait_ge(*b_dve.at("dS", j))
                pe.wait_ge(*f_dve.at("Q", i - 1))
                turn(g1[:, 1, :], zs[:, 8:12, :]).then_inc(*F.sig("vT"))
                pe.wait_ge(*f_dve.at("bv", i))
                turn(g0[:, 1, :], beta).then_inc(*F.sig("bT"))
                pe.wait_ge(*f_pool.at("kap", i))
                turn(g1[:, 0, :], kap).then_inc(*F.sig("kT"))
            if back:
                pe.wait_ge(*b_act.at("Y1", j))
                nc.tensor.matmul(g2[:, 0, :], con(C_HONES), flat(Ys[:]), start=True, stop=True).then_inc(*B.sig("mean"))
            if front:
                pe.wait_ge(*f_act.at("ktok", i))
                gram(alpha, beta, g1).then_inc(*F.sig("A"))
                pe.wait_ge(*f_pool.at("rho", i))
                gram(beta, rho, g0).then_inc(*F.sig("Mu"))
            if back:
                pe.wait_ge(*b_pool.at("ysq", j))
                nc.tensor.matmul(g2[:, 1, :], con(C_HONES), flat(ysq[:]), start=True, stop=True).then_inc(*B.sig("var"))
            if not front:
                return
            pe.wait_ge(*m_act.at("ktok", i))
            for h in range(MH):
                last = nc.tensor.matmul(m0[:, h * SEG:(h + 1) * SEG], zm[:, MH + h, :], zm[:, h, :], start=True, stop=True)
            last.then_inc(*M.sig("S"))
            stay_awake(g2[:, 0, :], 3)
            pe.wait_ge(*f_dve.at("am0", i))
            for n in range(NH):
                last = nc.tensor.matmul(flat(g1[:])[:, n * P:(n + 1) * P], AL[:, 0, n, :], idr[:, 0:P], start=True, stop=True)
            last.then_inc(*F.sig("am0T"))
            stay_awake(g2[:, 0, :], 3)
            pe.wait_ge(*f_dve.at("Mu", i))
            gram(kap, alpha, g0).then_inc(*F.sig("B"))
            for n in range(1, LEVELS):
                pe.wait_ge(*f_dve.at(f"U{n - 1}", i))
                pe.wait_ge(*f_pool.at(f"am{n}", i))
                eight(g1, AL[:, n % 2], Ur).then_inc(*F.sig(f"W{n}"))
                if n == 1:
                    stay_awake(g2[:, 0, :], 4)
                    pe.wait_ge(*f_pool.at("T0", i))
                    pe.wait_ge(*f_dve.at("B", i))
                else:
                    pe.wait_ge(*(f_dve.at("Mv", i) if n == 2 else f_act.at(f"Tc{n - 2}", i)))
                    for h in range(NH):
                        last = nc.tensor.matmul(flat(g2[:])[:, h * P:(h + 1) * P], Ur[:, h, :], idr[:, 0:P], start=True,
                                                stop=True)
                    last.then_inc(*F.sig(f"V{n - 1}"))
                if n == 3:
                    nc.tensor.matmul(m0, con(C_ONES), flat(Pb[:]), start=True, stop=False)
                    for h in range(MH):
                        last = nc.tensor.matmul(m0[:, h * SEG:(h + 1) * SEG], CN[:, 1, h, :], qe[:, h, :],
                                                start=False, stop=h == MH - 1)
                    last.then_inc(*M.sig("den"))
                if n == 4:
                    pe.wait_ge(*m_pool.at("kw", i))
                    pe.wait_ge(*m_act.at("aden", i))
                    for h in range(MH):
                        last = nc.tensor.matmul(m0[:, h * SEG:(h + 1) * SEG], kw[:, h, :], mvtok[:, h, :],
                                                start=True, stop=True)
                    last.then_inc(*M.sig("dC"))
                if n == 5:
                    pe.wait_ge(*m_dve.at("C", i))
                    nc.tensor.matmul(m0, con(C_ONES), flat(hm[:]), start=True, stop=True).then_inc(*M.sig("mean"))
                if n == 6:
                    pe.wait_ge(*m_pool.at("ysq", i))
                    nc.tensor.matmul(m1, con(C_ONES), flat(mysq[:]), start=True, stop=True).then_inc(*M.sig("var"))
                if n == 2:
                    stay_awake(g0[:, 0, :], 4)
                pe.wait_ge(*f_act.at(f"Wc{n}" if n == 1 else f"Tc{n - 1}", i))
                eight(g0, Tr, Wr).then_inc(*F.sig(f"E{n}"))
                if n == 1:
                    pe.wait_ge(*b_dve.at("ve", j))
                    gram(kap, rho, g2).then_inc(*F.sig("Mv"))
                elif n > 2:
                    stay_awake(g1[:, 0, :], 5)
                if n == 4:
                    pe.wait_ge(*m_dve.at("hm", i))
                    for h in range(MH):
                        last = nc.tensor.matmul(m1[:, h * SEG:(h + 1) * SEG], kw[:, h, :], con(C_ONES),
                                                start=True, stop=True)
                    last.then_inc(*M.sig("dN"))
                if n == 2:
                    pe.wait_ge(*m_act.at("vtok", i))
                    pe.wait_ge(*m_dve.at("qe", i))
                    for h in range(MH):
                        dst = m1[:, h * SEG:(h + 1) * SEG]
                        nc.tensor.matmul(dst, mvtok[:, h, :], Pb[:, h, :], start=True, stop=False)
                        last = nc.tensor.matmul(dst, CN[:, 0, h, :], qe[:, h, :], start=False, stop=True)
                    last.then_inc(*M.sig("num"))
            pe.wait_ge(*f_dve.at(f"U{LEVELS - 1}", i))
            eight(g1, Am, Ur[:].bitcast(F32)).then_inc(*F.sig("F"))
            pe.wait_ge(*f_act.at(f"Tc{LEVELS - 2}", i))
            for n in range(NH):
                last = nc.tensor.matmul(flat(g2[:])[:, n * P:(n + 1) * P], Ur[:, n, :], idr[:, 0:P], start=True, stop=True)
            last.then_inc(*F.sig(f"V{LEVELS - 1}"))
            stay_awake(g0[:, 0, :], 8)
            pe.wait_ge(*f_act.at(f"Tc{LEVELS - 1}", i))
            pe.wait_ge(*f_dve.at("Q", i))
            eight(g0, Tr, Qr).then_inc(*F.sig("UQ"))
            if more:
                ahead(i + 1)
            pe.wait_ge(*f_dve.at("Uf", i))
            for n, e, r, rows in heads:
                last = nc.tensor.matmul(g2[rows, 1, r * P:(r + 1) * P], atok[:, r, rows], Uf[:, n, :],
                                        start=True, stop=True)
            last.then_inc(*F.sig("Wst"))
            for n, e, r, rows in heads:
                last = nc.tensor.matmul(g0[:, 0, n * HD:(n + 1) * HD], Bm[:, n, :], vtok[:, r, rows],
                                        start=True, stop=True)
            last.then_inc(*F.sig("Z"))
            for r in range(RC):
                last = nc.tensor.matmul(g2[:, 0, r * P:(r + 1) * P], loraw[:, 1, r * P:(r + 1) * P], gsig[:],
                                        start=True, stop=True)
            last.then_inc(*F.sig("gate"))

        def merge():
            def output_chunk(t):
                pe.wait_ge(*sp_dve.at(f"l{t % 2}", t // 2))

            def body(i, first):
                for r in range(2):
                    for n in range(2):
                        if r == 0:
                            dve_bank(i * 2 + (c.dve + n))
                        else:
                            act_bank(i * 2 + (c.act + n))
                        if n == 0:
                            unit_ready(i * 2 + (c.unit + r))
                        bank = bank_dve(c.dve + n) if r == 0 else bank_act(c.act + n)
                        last = product(bank, (c.unit + r) % 2, range(n * RC, (n + 1) * RC),
                                       yhi[:, n * RC:(n + 1) * RC, :], ylo[:, n * RC:(n + 1) * RC, :],
                                       output_chunk if first and r == 0 else None)
                    last.then_inc(unit_used, 1)

            pairs(KD, True, body)
            c.advance(unit=KD, act=KD, dve=KD)

        def keys_values():
            for part in range(2):
                with pe.Fori(0, KD // 2) as i:
                    for r in range(2):
                        act_bank(i * 2 + (c.act + r))
                        unit_ready(i * 2 + (c.unit + r))
                        k = (c.unit + r) % 2
                        bank = bank_act(c.act + r)
                        if part == 0:
                            for t in range(KD):
                                last = tile3(bank[:, 0, 0:MEM], k, t, memhi[:, t, :], memlo[:, t, :], t == 0, t == KD - 1)
                        else:
                            for m in range(2):
                                rows, dst = slice(m * P, (m + 1) * P), bank[:, m, 0:P]
                                for t in range(KD):
                                    wh, wl = whi[:, k, t * P:(t + 1) * P], wlo[:, k, t * P:(t + 1) * P]
                                    nc.tensor.matmul(dst, memhi[:, t, rows], wh, start=t == 0, stop=False)
                                    nc.tensor.matmul(dst, memhi[:, t, rows], wl, start=False, stop=False)
                                    last = nc.tensor.matmul(dst, memlo[:, t, rows], wh, start=False, stop=t == KD - 1)
                        last.then_inc(unit_used, 1)
                c.advance(unit=KD, act=KD)

        def attend(i, front, back):
            g0, g1, g2, g3 = G
            j = i - 1
            if back:
                pe.wait_ge(*xp_dve.at("p", j))
                for h in range(XH):
                    for m in range(2):
                        last = nc.tensor.transpose(flat(g1[:])[:, (2 * h + m) * P:(2 * h + m + 1) * P],
                                                   px[:, h, m * P:(m + 1) * P], con(C_ID))
                last.then_inc(*xo_pe.sig("T"))
            if front:
                pe.wait_ge(*xp_act.at("e", i - 1))
                pe.wait_ge(*xp_act.at("q", i))
                for h in range(XH):
                    for n in range(2):
                        last = nc.tensor.matmul(flat(g0[:])[:, h * MEM:(h + 1) * MEM], qs[:, 2 * h + n, :],
                                                kTx[:, 2 * h + n, :], start=n == 0, stop=n == 1)
                last.then_inc(*xp_pe.sig("S"))
            if back:
                pe.wait_ge(*xo_act.at("pt", j))
                pe.wait_ge(*xo_dve.at("lo", j - 1))
                for n in range(KD):
                    for m in range(2):
                        last = nc.tensor.matmul(flat(g2[:])[:, n * P:(n + 1) * P], vx[:, m, n * P:(n + 1) * P],
                                                pxt[:, n // 2, m, :], start=m == 0, stop=m == 1)
                last.then_inc(*xo_pe.sig("O"))

        pe.wait_ge(consts_in, CONSTS * 16)
        ffn()
        norm(nt, T)
        arrive()
        gemm(RW_UNITS, "act", chunk_ready=norm_chunk)
        gemm(ML_UNITS, "act")
        gemm(1, "act")
        gemm(2 * KD, "act")
        barrier(pe, c)
        barrier(pe, c)
        pipelined(pe, iteration, ahead)
        barrier(pe, c)
        merge()
        pe.wait_ge(*mg_dve.at("l1", 3))
        barrier(pe, c)
        gemm(2, "dve")
        norm(memr[:, 2, :], MEM)
        gemm(KD - 2, "dve")
        pe.wait_ge(*nh_dve.at("l1", c.norm - 1))
        norm(nt, T)
        keys_values()
        arrive()
        gemm(KD, "act", chunk_ready=norm_chunk)
        barrier(pe, c)
        pipelined(pe, attend)
        barrier(pe, c)
        gemm(KD, "dve")
        ffn()
        norm(nt, T)

    @block.scalar
    def _(act):
        c = Count()
        act.sem_inc(act_free, credit)
        for s in (*z_out, silu_made, yr_out, ym_out):
            act.sem_inc(s, 16)
        for s in ACT_STEPS:
            act.sem_inc(s.sem, s.n)
        activation = nc.scalar.activation

        def log_exp_tables():
            nc.scalar.preload_act_table_set("natural_log_exp_and_others")

        def output_ready(u):
            act.wait_ge(unit_used, u + (credit + 1))

        def squares(src, sq, residual=False, first=0, chunks=KD):
            with loop(act, chunks // 2) as i:
                for n in range(2):
                    if residual:
                        act.wait_ge(dve_free, i * 2 + (c.dve + n + 1 + credit))
                    act.wait_ge(*nsq_dve.at(f"add{n}", i + (c.sq - 1)))
                    activation(sq[:, n, :], src[:, i * 2 + (first + n), :], ACT.Square).then_inc(*nsq_act.sig(f"sq{n}"))
            c.sq += chunks // 2
            if residual:
                c.advance(unit=chunks, dve=chunks)

        def norm_root(ms, r):
            log_exp_tables()
            act.wait_ge(norm_ms, c.norms + 1)
            activation(r, ms, ACT.Ln).then_inc(act_seq, 1)
            c.seq += 1
            act.wait_ge(act_seq, c.seq)
            activation(r, r, ACT.Exp, scale=-0.5).then_inc(norm_r, 1)
            c.advance(norms=1, dve=1)

        def norm_part(i, n, h, hi):
            act.wait_ge(*nh_dve.at(f"h{n}", i + c.norm))
            activation(hi[:, i * 2 + n, :], h[:, n, :], ACT.Copy).then_inc(*nh_act.sig(f"c{n}"))

        def norm(ms, r, h, hi):
            norm_root(ms, r)
            if hi is not None:
                with act.Fori(0, KD // 2) as i:
                    for n in range(2):
                        norm_part(i, n, h, hi)
            c.advance(norm=4)

        def norm_x(hi=hhi):
            norm(nms[:], nr[:], nh, hi)

        def ffn():
            norm_x()
            for n in FF_PARTS:
                with loop(act, n // 2) as i:
                    for r in range(2):
                        output_ready(i * 4 + (c.unit + 2 * r))
                        act.wait_ge(dve_free, i * 2 + (c.dve + r + credit))
                        act.wait_ge(*nh_dve.at("l1", c.norm - 1))
                        activation(s0[:], flat(bank_act(c.act + r)[:]), ACT.Silu).then_inc(act_free, 1)
                        act.wait_ge(dve_free, i * 2 + (c.dve + r + 1 + credit))
                        activation(ahi[:, i * 2 + r, :], s1[:], ACT.Copy).then_inc(a_hi, 1)
                c.advance(unit=2 * n, act=n, dve=n, a=n)
                if n != FF_PARTS[-1]:
                    c.advance(unit=KD, dve=KD)
            squares(xT, nsq, residual=True)

        def store_z(dst, r, turn):
            act.dma_start(dst, po[:, r, :]).then_inc(z_out[r], 16)

        def po_free(r, turn):
            act.wait_ge(z_out[r], (turn + 1) * 16)

        def project_rw():
            with act.Fori(0, RW_UNITS // 2) as i:
                for r in range(2):
                    output_ready(i * 2 + (c.unit + r))
                    act.wait_ge(*rp_dve.at(f"m{r}", i - 1))
                    activation(stg[:, r, 3:3 + T], flat(bank_act(c.act + r)[:]), ACT.Copy).then_inc(act_free, 1)
                    act.wait_ge(*rp_dve.at(f"m{r}", i))
                    store_z(zrw_d[i * 2 + r], r, 0)
            c.advance(unit=RW_UNITS, act=RW_UNITS, z=RW_UNITS // 2)

        def project_ml():
            with act.Fori(0, MH) as i:
                for r in range(2):
                    output_ready(i * 2 + (c.unit + r))
                    act.wait_ge(*cv_dve.at(f"t3{r}", i - 1))
                    activation(stg[:, r, 3:3 + T], flat(bank_act(c.act + r)[:]), ACT.Copy).then_inc(act_free, 1)
                    act.wait_ge(*cv_dve.at(f"t3{r}", i))
                    po_free(r, i + c.z)
                    activation(po[:, r, :], pd[:, r, :], ACT.Silu).then_inc(silu_made, 1)
                    act.wait_ge(silu_made, i * 2 + (r + 1 + 16))
                    store_z(zml_d[i * 2 + r], r, 0)
            c.advance(unit=2 * MH, act=2 * MH, z=MH)
            for first, func in ((2 * MH, ACT.Copy), (3 * MH, ACT.Sigmoid)):
                with act.Fori(0, MH // 2) as i:
                    for r in range(2):
                        output_ready(i * 2 + (c.unit + r))
                        po_free(r, i + c.z)
                        activation(po[:, r, :], flat(bank_act(c.act + r)[:]), func).then_inc(act_free, 1)
                        act.wait_ge(act_free, i * 2 + (c.act + r + 1 + credit))
                        store_z(zml_d[i * 2 + (first + r)], r, 0)
                c.advance(unit=MH, act=MH, z=MH // 2)
            output_ready(c.unit)
            activation(ifs[:], flat(bank_act(c.act)[:]), ACT.Copy).then_inc(act_free, 1)
            c.advance(unit=1, act=1)
            act.wait_ge(act_free, c.act + credit)
            act.dma_start(ifr[:], ifs[0:MH, :]).then_inc(x_in, 16)
            act.dma_start(grow[:], ifs[MH:2 * MH, :]).then_inc(x_in, 16)
            mlstm_rows()
            with act.Fori(0, KD) as i:
                for r, dst in enumerate((gates_d[0], gates_d[1])):
                    output_ready(i * 2 + (c.unit + r))
                    po_free(r, i + c.z)
                    activation(po[:, r, :], flat(bank_act(c.act + r)[:]), ACT.Sigmoid).then_inc(act_free, 1)
                    act.wait_ge(act_free, i * 2 + (c.act + r + 1 + credit))
                    store_z(dst[i], r, 0)
            c.advance(unit=2 * KD, act=2 * KD, z=KD)
            for r in range(2):
                act.wait_ge(z_out[r], (c.z + 1) * 16)

        def store_output(j):
            act.wait_ge(*b_pool.at("y4", j))
            act.dma_start(y_d[0:RC].rearrange("r p t -> p r t")[:, :, bass.ds(j * SEG, SEG)], yo[:]).then_inc(yr_out, 16)

        def ahead_gate(i):
            activation(gsig[:], zs[:, 13, :], ACT.Tanh, scale=0.5).then_inc(*l_act.sig("gt"))

        def ahead(i, gate=True):
            act.wait_ge(zs_in, i * 16 + 16)
            activation(lora[0:HD, :], zs[0:HD, 12, :], ACT.Tanh).then_inc(*l_act.sig("th"))
            activation(lora[HD:P, :], zs[HD:P, 12, :], ACT.Copy).then_inc(*l_act.sig("ad"))
            act.wait_ge(*l_pe.at("lora", i))
            for r in range(RC):
                last = activation(dec[:, r, 1:DEC], G[1][:, 0, r * P:(r + 1) * P], ACT.Tanh, scale=0.5,
                                  bias=hw0[:, r:r + 1])
            last.then_inc(*l_act.sig("tw"))
            for r in range(RC):
                last = activation(ga[:, r, :], G[1][:, 1, r * P:(r + 1) * P], ACT.Tanh, scale=0.5,
                                  bias=hw0[:, RC + r:RC + r + 1])
            last.then_inc(*l_act.sig("ta"))
            if gate:
                ahead_gate(i)

        def iteration(i, front, back, more=True):
            F, B, M = f_act, b_act, m_act
            j = i - 1
            g0, g1, g2, m0, m1 = G[0], G[1], G[2], G[3][:, 0, :], G[3][:, 1, :]
            if front:
                log_exp_tables()
                activation(gst[:], grow[:, bass.ds(i * SEG, SEG)], ACT.Copy).then_inc(*M.sig("gst"))
                act.wait_ge(*m_pe.at("bce", i))
                activation(flat(Eb[:]), m1, ACT.Exp).then_inc(*M.sig("E"))
                act.wait_ge(*f_dve.at("cc", i))
                activation(flat(Pp[:]), flat(dec[:]), ACT.Exp, scale=-KAPPA).then_inc(*F.sig("P"))
                activation(flat(Pi[:]), flat(dec[:]), ACT.Exp, scale=KAPPA).then_inc(*F.sig("Pi"))
                act.wait_ge(*f_dve.at("ssc", i))
                activation(flat(rinv[:]), flat(ssc[:]), ACT.Ln, scale=2.0 ** 20).then_inc(*F.sig("lnn"))
                act.wait_ge(*F.at("lnn", i))
                activation(flat(rinv[:]), flat(rinv[:]), ACT.Exp, scale=-0.5,
                           bias=cst[:, C_RSC:C_RSC + 1]).then_inc(*F.sig("rinv"))
            if back:
                act.wait_ge(*b_pe.at("U", j))
                activation(Un[:].rearrange("p (e r) v -> p e (r v)", e=2), g2[:, :, 0:RC * HD], ACT.Copy,
                           scale=-1.0).then_inc(*B.sig("Un"))
                act.wait_ge(*b_pe.at("Y", j))
                act.wait_ge(*b_pool.at("y4", j - 1))
                for e in range(2):
                    rows = slice(e * HD, (e + 1) * HD)
                    activation(flat(Ys[rows]), g2[rows, e, :], ACT.Copy).then_inc(*B.sig(f"Y{e}"))
            if front:
                act.wait_ge(*m_pe.at("bcn", i))
                act.wait_ge(*m_dve.at("y1", i - 1))
                activation(flat(nmb[:]), m0, ACT.Exp, scale=-1.0).then_inc(*M.sig("nm"))
                act.wait_ge(*m_pe.at("gT", i))
                activation(gtok[:], m1[:, 0:MH], ACT.Copy).then_inc(*M.sig("gtok"))
                for name, dst, src in (("a", atok, g0[:, 0, :]), ("v", vtok, g1[:, 1, :]), ("b", btok, g0[:, 1, :]),
                                       ("k", ktok, g1[:, 0, :])):
                    act.wait_ge(*f_pe.at(f"{name}T", i))
                    if name == "v":
                        act.wait_ge(*b_pe.at("dS", j))
                    activation(flat(dst[:]), src, ACT.Copy).then_inc(*F.sig(f"{name}tok"))
                act.wait_ge(*m_pe.at("kT", i))
                activation(flat(mktok[:]), m0, ACT.Copy).then_inc(*M.sig("ktok"))
                act.wait_ge(*m_pe.at("vT", i))
                activation(flat(mvtok[:]), m1, ACT.Copy).then_inc(*M.sig("vtok"))
                act.wait_ge(*M.at("gtok", i))
                act.wait_ge(*m_dve.at("arg", i))
                for h in range(MH):
                    last = activation(Db[:, h, :], argb[:, h, :], ACT.Exp, bias=gtok[:, h:h + 1])
                last.then_inc(*M.sig("D"))
            if back:
                act.wait_ge(*b_dve.at("ve", j))
                activation(flat(yrs[:]), flat(yve[:]), ACT.Ln).then_inc(*B.sig("lnv"))
                act.wait_ge(*B.at("lnv", j))
                activation(flat(yrs[:]), flat(yrs[:]), ACT.Exp, scale=-0.5).then_inc(*B.sig("rsv"))
            if not front:
                store_output(j)
                return
            for n in range(1, LEVELS):
                act.wait_ge(*f_pe.at(f"W{n}", i))
                activation(flat(Wr[:]), flat(g1[:]), ACT.Copy).then_inc(*F.sig(f"Wc{n}"))
                if n > 1:
                    act.wait_ge(*f_pe.at(f"V{n - 1}", i))
                    activation(flat(Tr[:]), flat(g2[:]), ACT.Copy).then_inc(*F.sig(f"Tc{n - 1}"))
                if n == 3:
                    act.wait_ge(*m_pe.at("den", i))
                    activation(flat(aden[:]), m0, ACT.Abs).then_inc(*M.sig("aden"))
            act.wait_ge(*m_dve.at("ve", i))
            activation(flat(mrs[:]), flat(mve[:]), ACT.Ln).then_inc(*M.sig("lnv"))
            act.wait_ge(*M.at("lnv", i))
            activation(flat(mrs[:]), flat(mrs[:]), ACT.Exp, scale=-0.5).then_inc(*M.sig("rsv"))
            if more:
                nc.scalar.preload_act_table(ACT.Tanh)
            act.wait_ge(*f_pe.at(f"V{LEVELS - 1}", i))
            activation(flat(Tr[:]), flat(g2[:]), ACT.Copy).then_inc(*F.sig(f"Tc{LEVELS - 1}"))
            if more:
                ahead(i + 1, gate=False)
            act.wait_ge(*f_pe.at("Wst", i))
            activation(flat(W1m[:]), g2[:, 1, :], ACT.Copy).then_inc(*F.sig("W1c"))
            act.wait_ge(*f_pe.at("Z", i))
            activation(flat(Zm[:]), g0[:, 0, :], ACT.Copy).then_inc(*F.sig("Zc"))
            act.wait_ge(*f_pe.at("gate", i))
            if back:
                store_output(j)
            activation(flat(gout[:]), g2[:, 0, :], ACT.Copy).then_inc(*F.sig("gev"))
            if more:
                ahead_gate(i + 1)

        def mlstm_rows():
            act.wait_ge(dve_seq, ROWS_SEQ + 1)
            activation(arow[:], grow[:], ACT.Abs).then_inc(act_seq, 1)
            act.wait_ge(act_seq, c.seq + 1)
            activation(nrow[:], arow[:], ACT.Exp, scale=-1.0).then_inc(act_seq, 1)
            act.wait_ge(act_seq, c.seq + 2)
            activation(nrow[:], nrow[:], ACT.Ln, bias=1.0).then_inc(act_seq, 1)
            c.seq += 3

        def split_load(src, hi):
            with act.Fori(0, KD // 2) as i:
                for r in range(2):
                    act.wait_ge(*sp_dve.at(f"l{r}", i + (c.split - 1)))
                    act.dma_start(ysg[:, r, :], src[i * 2 + r]).then_inc(sp_in[r], 16)
                for r in range(2):
                    act.wait_ge(sp_in[r], (i + (c.split + 1)) * 16)
                    activation(hi[:, i * 2 + r, :], ysg[:, r, :], ACT.Copy).then_inc(*sp_act.sig(f"c{r}"))
            c.split += 4

        def merge():
            def load_gates(i, r):
                for n in range(2):
                    act.dma_start(sg[:, r, n, :], gates_d[n, i * 2 + r]).then_inc(sg_in[r], 16)

            for r in range(2):
                load_gates(0, r)

            def chunks(i, more):
                for r in range(2):
                    act.wait_ge(*mg_dve.at(f"mo{r}", i))
                    activation(hhi[:, i * 2 + r, :], mo[:, r, :], ACT.Copy).then_inc(*mg_act.sig(f"h{r}"))
                    if more:
                        load_gates(i + 1, r)

            with act.Fori(0, KD // 2 - 1) as i:
                chunks(i, True)
            chunks(KD // 2 - 1, False)
            c.advance(unit=KD, act=KD, dve=KD)

        def keys_values():
            with act.Fori(0, KD // 2) as i:
                for r in range(2):
                    output_ready(i * 2 + (c.unit + r))
                    activation(kTx[:, i * 2 + r, :], bank_act(c.act + r)[:, 0, 0:MEM], ACT.Copy).then_inc(act_free, 1)
            c.advance(unit=KD, act=KD)
            with act.Fori(0, KD // 2) as i:
                for r in range(2):
                    output_ready(i * 2 + (c.unit + r))
                    activation(vx[:, :, bass.ds((i * 2 + r) * P, P)], bank_act(c.act + r)[:, :, 0:P],
                               ACT.Copy).then_inc(act_free, 1)
                    norm_part(i, r, nh, hhi)
            c.advance(unit=KD, act=KD, norm=4)

        def attend(i, front, back):
            g0, g1, g2, g3 = G
            j = i - 1
            if front:
                act.wait_ge(*xp_pe.at("S", i - 1))
                activation(qs[:], qT[:, :, bass.ds(i * SEG, SEG)], ACT.Copy).then_inc(*xp_act.sig("q"))
            if back:
                act.wait_ge(*xo_pe.at("T", j))
                activation(pxt[:].rearrange("p h m t -> p (h m t)"), flat(g1[:]), ACT.Copy).then_inc(*xo_act.sig("pt"))
            if front:
                act.wait_ge(*xp_dve.at("nmx", i))
                for h in range(XH):
                    last = activation(sx[:, h, :], flat(g0[:])[:, h * MEM:(h + 1) * MEM], ACT.Exp, scale=XA_SCALE,
                                      bias=mx[:, XH + h:XH + h + 1], accum_out=mx[:, 2 * XH + h:2 * XH + h + 1])
                last.then_inc(*xp_act.sig("e"))
            if back:
                act.wait_ge(*xo_pe.at("O", j))
                activation(hhi[:, :, bass.ds(j * SEG, SEG)], flat(g2[:]).rearrange("p (k t) -> p k t", k=KD),
                           ACT.Copy).then_inc(*xo_act.sig("hi"))

        for n in range(KD // 2):
            act.dma_start(xT[:, 2 * n:2 * n + 2, :], a["x"][:, 2 * n:2 * n + 2, :]).then_inc(xc_in[n], 16)
        for dst, src in const_loads:
            act.dma_start(dst, src).then_inc(consts_in, 16)
        for k in range(KD):
            act.wait_ge(xc_in[k // 2], 16)
            act.wait_ge(*nsq_dve.at(f"add{k % 2}", k // 2 - 1))
            activation(nsq[:, k % 2, :], xT[:, k, :], ACT.Square).then_inc(*nsq_act.sig(f"sq{k % 2}"))
        c.sq += 4
        act.wait_ge(consts_in, CONSTS * 16)
        ffn()
        act.wait_ge(dve_free, c.dve + credit)
        act.dma_start(x_park, xT[:]).then_inc(store, 16)
        norm_x()
        act.wait_ge(store, 16)
        barrier(act, c)
        project_rw()
        project_ml()
        barrier(act, c)
        act.dma_start(loraw[:, 0, :], a["lora_wa"]).then_inc(x_in, 16)
        act.dma_start(loraw[:, 1, :], a["lora_g"]).then_inc(x_in, 16)
        act.wait_ge(x_in, 4 * 16)
        barrier(act, c)
        pipelined(act, iteration, ahead)
        act.wait_ge(yr_out, (NSEG + 1) * 16)
        act.wait_ge(ym_out, (NSEG + 1) * 16)
        barrier(act, c)
        split_load(y_d, yhi)
        merge()
        barrier(act, c)
        act.dma_start(memx[:], a["mem"]).then_inc(x_in, 16)
        act.dma_start(xT[:], x_park).then_inc(x_in, 16)
        act.wait_ge(x_in, 6 * 16)
        squares(memx, memq)
        squares(xT, nsq, residual=True, chunks=2)
        norm(memr[:, 0, :], memr[:, 1, :], memh, memhi)
        squares(xT, nsq, residual=True, first=2, chunks=KD - 2)
        norm_root(nms[:], nr[:])
        keys_values()
        barrier(act, c)
        with act.Fori(0, KD // 2) as i:
            for r in range(2):
                output_ready(i * 2 + (c.unit + r))
                activation(qT[:, i * 2 + r, :], flat(bank_act(c.act + r)[:]), ACT.Copy).then_inc(act_free, 1)
        c.advance(unit=KD, act=KD)
        barrier(act, c)
        pipelined(act, attend)
        barrier(act, c)
        squares(xT, nsq, residual=True)
        ffn()
        norm_x(None)
        for k in range(KD):
            act.wait_ge(dve_seq, FINAL_SEQ + k + 1)
            act.dma_start(out[k], xT[:, k, :]).then_inc(store, 16)
        act.wait_ge(store, (1 + KD) * 16)

    @block.vector
    def _(dve):
        c = Count()
        dve.sem_inc(dve_free, credit)
        dve.sem_inc(a_lo, 1)
        for s in DVE_STEPS:
            dve.sem_inc(s.sem, s.n)
        tt, ts, stt = nc.vector.tensor_tensor, nc.vector.tensor_scalar, nc.vector.scalar_tensor_tensor

        def step(ins):
            c.seq += 1
            ins.then_inc(dve_seq, 1)
            dve.wait_ge(dve_seq, c.seq)

        def output_ready(u):
            dve.wait_ge(unit_used, u + (credit + 1))

        def add_squares(i, n, sq, t):
            dve.wait_ge(*nsq_act.at(f"sq{n}", i + c.sq))
            dve.wait_ge(*(nsq_dve.at("add0", i + c.sq) if n else nsq_dve.at("add1", i + (c.sq - 1))))
            tt(t, t, sq[:, n, :], ALU.add).then_inc(*nsq_dve.sig(f"add{n}"))

        def squares(sq, t):
            step(nc.vector.memset(t, 0.0))
            with dve.Fori(0, KD // 2) as i:
                for n in range(2):
                    add_squares(i, n, sq, t)
            c.sq += 4

        def norm(gain, src, width, ms, r, t, h, hi, lo):
            dve.wait_ge(norm_sum, c.norms + 1)
            src_ps = bank_dve(c.dve)
            src_ps = flat(src_ps[:]) if width == T else src_ps[:, 0, 0:width]
            ts(ms, src_ps, 1.0 / D, EPS, ALU.mult, ALU.add).then_inc(norm_ms, 1)
            dve.wait_ge(norm_r, c.norms + 1)
            step(stt(t, r, -0.5, r, ALU.mult, ALU.mult))
            step(tt(t, t, ms, ALU.mult))
            step(stt(r, t, 1.5, r, ALU.add, ALU.mult))
            dve.sem_inc(dve_free, 1)
            if hi is not None:
                with dve.Fori(0, KD // 2) as i:
                    for n in range(2):
                        dve.wait_ge(*nh_dve.at(f"l{n}", i + (c.norm - 1)))
                        col = VCOL[gain] + n
                        stt(h[:, n, :], src[:, i * 2 + n, :], vec[:, bass.ds(i * 2 + col, 1)], r, ALU.mult,
                            ALU.mult).then_inc(*nh_dve.sig(f"h{n}"))
                    for n in range(2):
                        dve.wait_ge(*nh_act.at(f"c{n}", i + c.norm))
                        tt(lo[:, i * 2 + n, :], h[:, n, :], hi[:, i * 2 + n, :].bitcast(F32),
                           ALU.subtract).then_inc(*nh_dve.sig(f"l{n}"))
            c.advance(norm=4, norms=1, dve=1)

        def norm_x(gain, hi=hhi):
            norm(gain, xT, T, nms[:], nr[:], nt[:], nh, hi, hlo)

        def residual(scale, last=True, first=0, chunks=KD):
            if last and first == 0:
                step(nc.vector.memset(nt[:], 0.0))
            with loop(dve, chunks // 2) as i:
                for r in range(2):
                    output_ready(i * 2 + (c.unit + r))
                    x_ = xT[:, i * 2 + (first + r), :]
                    stt(x_, flat(bank_dve(c.dve + r)[:]), scale, x_, ALU.mult, ALU.add).then_inc(dve_free, 1)
                    if last:
                        add_squares(i, r, nsq, nt[:])
            c.advance(unit=chunks, dve=chunks)
            c.sq += chunks // 2 if last else 0

        def ffn(gain):
            norm_x(gain)
            for n in FF_PARTS:
                with loop(dve, n // 2) as i:
                    for r in range(2):
                        dve.wait_ge(act_free, i * 2 + (c.act + r + 1 + credit))
                        output_ready(i * 4 + (c.unit + 2 * r + 1))
                        dve.wait_ge(a_lo, i * 2 + (c.a + r + 1))
                        tt(s1[:], s0[:], flat(bank_dve(c.dve + r)[:]), ALU.mult).then_inc(dve_free, 1)
                        dve.wait_ge(a_hi, i * 2 + (c.a + r + 1))
                        tt(alo[:, i * 2 + r, :], s1[:], ahi[:, i * 2 + r, :].bitcast(F32),
                           ALU.subtract).then_inc(a_lo, 1)
                c.advance(unit=2 * n, act=n, dve=n, a=n)
                residual(0.5, last=n == FF_PARTS[-1])

        def project_rw():
            with dve.Fori(0, RW_UNITS // 2) as i:
                for r in range(2):
                    dve.wait_ge(act_free, i * 2 + (c.act + r + 1 + credit))
                    tt(pd[:, r, :], stg[:, r, 2:2 + T], stg[:, r, 3:3 + T], ALU.subtract).then_inc(*rp_dve.sig(f"d{r}"))
                    dve.wait_ge(*rp_dve.at(f"d{r}", i))
                    dve.wait_ge(z_out[r], (i + 1) * 16)
                    stt(po[:, r, :], pd[:, r, :], vec[:, bass.ds(i * 2 + (VCOL["rw_mu"] + r), 1)], stg[:, r, 3:3 + T],
                        ALU.mult, ALU.add).then_inc(*rp_dve.sig(f"m{r}"))
            c.advance(unit=RW_UNITS, act=RW_UNITS)

        def project_ml():
            with dve.Fori(0, MH) as i:
                for r in range(2):
                    dve.wait_ge(act_free, i * 2 + (c.act + r + 1 + credit))

                    def w(name):
                        return vec[:, bass.ds(i * 2 + (VCOL[name] + r), 1)]

                    dve.wait_ge(silu_made, i * 2 + 16)
                    ts(pd[:, r, :], stg[:, r, 3:3 + T], w("conv_w0"), w("conv_b"), ALU.mult,
                       ALU.add).then_inc(*cv_dve.sig(f"t0{r}"))
                    for j in range(1, 4):
                        dve.wait_ge(*cv_dve.at(f"t{j - 1}{r}", i))
                        stt(pd[:, r, :], stg[:, r, 3 - j:3 - j + T], w(f"conv_w{j}"), pd[:, r, :], ALU.mult,
                            ALU.add).then_inc(*cv_dve.sig(f"t{j}{r}"))
            c.advance(unit=ML_UNITS + 1, act=ML_UNITS + 1)

        def newton(S, names, r, v, w, i):
            stt(flat(w[:]), flat(r[:]), -0.5, flat(r[:]), ALU.mult, ALU.mult).then_inc(*S.sig(names[0]))
            dve.wait_ge(*S.at(names[0], i))
            tt(flat(w[:]), flat(w[:]), flat(v[:]), ALU.mult).then_inc(*S.sig(names[1]))
            dve.wait_ge(*S.at(names[1], i))
            stt(flat(r[:]), flat(w[:]), 1.5, flat(r[:]), ALU.add, ALU.mult).then_inc(*S.sig(names[2]))
            dve.wait_ge(*S.at(names[2], i))

        def iteration(i, front, back):
            F, B, M = f_dve, b_dve, m_dve
            j = i - 1
            g0, g1, g2, m0, m1 = G[0], G[1], G[2], G[3][:, 0, :], G[3][:, 1, :]

            def copies(col, n=NH):
                return con(col).unsqueeze(1).to_broadcast([P, n, P])

            def three(ap):
                return ap.rearrange("p (n t) -> p n t", t=SEG)

            def gram(name, dst, src, mask):
                nc.vector.copy_predicated(dst[:], copies(mask).bitcast(U32), three(flat(src[:]))).then_inc(*F.sig(name))

            def output_variance():
                dve.wait_ge(*b_pe.at("var", j))
                ts(flat(yve[:]), g2[:, 1, :], 1.0 / HD, GN_EPS, ALU.mult, ALU.add).then_inc(*B.sig("ve"))

            def output_norm():
                dve.wait_ge(*b_act.at("rsv", j))
                newton(B, ("g1", "g2", "g3"), yrs, yve, ynw, j)
                tt(Ys[:], Ys[:], yrs[:], ALU.mult).then_inc(*B.sig("y1"))

            if front:
                dve.wait_ge(*l_act.at("tw", i))
                ts(dec[:, :, 1:DEC], dec[:, :, 1:DEC], 1.0, None, ALU.add).then_inc(*F.sig("dec"))
                dve.wait_ge(*F.at("dec", i))
                nc.vector.tensor_tensor_scan(flat(cum[:]), con(C_RST, RC * DEC), flat(dec[:]), 0.0, ALU.mult,
                                             ALU.add).then_inc(*F.sig("scan"))
                dve.wait_ge(*F.at("scan", i))
                ts(hend[:], cum[:, :, DEC - 1:DEC], 0.5, None, ALU.mult).then_inc(*F.sig("hend"))
                dve.wait_ge(*F.at("hend", i))
                tt(dec[:], cum[:], hend[:].to_broadcast([P, RC, DEC]), ALU.subtract).then_inc(*F.sig("cc"))
                dve.wait_ge(*m_pe.at("bca", i))
                dve.wait_ge(*m_pool.at("y3", i - 1))
                tt(argb[:], three(m0), copies(C_ADD, MH), ALU.add).then_inc(*M.sig("arg"))
                dve.wait_ge(*l_act.at("gt", i))
                ts(gsig[:], gsig[:], 0.5, 0.5, ALU.mult, ALU.add).then_inc(*F.sig("gs"))
                dve.wait_ge(*l_act.at("ta", i))
                ts(ga[:], ga[:], 0.5, 0.5, ALU.mult, ALU.add).then_inc(*F.sig("av"))
                dve.wait_ge(*F.at("av", i))
                stt(gu[:], ga[:], -1.0, vbc("rw_k_a", SEG), ALU.add, ALU.mult).then_inc(*F.sig("gu"))
                dve.wait_ge(*F.at("gu", i))
                stt(flat(kmod[:]), flat(gu[:]), 1.0, zs[:, 4:8, :].rearrange("p r t -> p (r t)"), ALU.add,
                    ALU.mult).then_inc(*F.sig("kmod"))
                dve.wait_ge(*f_pe.at("ss", i))
                ts(flat(ssc[:]), g0[:, 0, :], 1e-24, None, ALU.max).then_inc(*F.sig("ssc"))
            if front:
                dve.wait_ge(*f_act.at("rinv", i))
                newton(F, ("n1", "n2", "rin"), rinv, ssc, nw, i)
                tt(kk[:], kk[:], rinv[:], ALU.mult).then_inc(*F.sig("kk"))
                dve.wait_ge(*F.at("kk", i))
                tt(kka[:], kk[:], ga[:], ALU.mult).then_inc(*F.sig("kka"))
                dve.wait_ge(*f_act.at("Pi", i))
                tt(alpha[:], kk[:], Pp[:, :, 0:SEG], ALU.mult).then_inc(*F.sig("alpha"))
                dve.wait_ge(*F.at("kka", i))
                tt(beta[:], kka[:], Pi[:, :, 1:DEC], ALU.mult).then_inc(*F.sig("beta"))
            if back:
                dve.wait_ge(*b_pe.at("dS", j))
                tt(St[:], S0s[:], g1[:, 1, 0:RC * HD].rearrange("p (r v) -> p r v", r=RC), ALU.add).then_inc(*B.sig("dS"))
                dve.wait_ge(*B.at("dS", j))
                tt(St[:], St[:], pend[:].to_broadcast([P, RC, HD]), ALU.mult).then_inc(*B.sig("S"))
            if front:
                dve.wait_ge(*f_pe.at("bonus", i))
                dve.wait_ge(*b_pool.at("bvb", j))
                tt(bv[:], three(g0[:, 1, :]), zs[:, 8:12, :], ALU.mult).then_inc(*F.sig("bv"))
            if back:
                dve.wait_ge(*b_pe.at("mean", j))
                stt(flat(Ys[:]), g2[:, 0, :], -1.0 / HD, flat(Ys[:]), ALU.mult, ALU.add).then_inc(*B.sig("yc"))
            if not front:
                output_variance()
                output_norm()
                return
            dve.wait_ge(*f_pe.at("A", i))
            tt(pend[:], Pp[:, :, DEC - 1:DEC], con(C_ONES, 1).unsqueeze(1).to_broadcast([P, RC, 1]),
               ALU.mult).then_inc(*F.sig("pend"))
            gram("A", Am, g1, C_LOW)
            dve.wait_ge(*F.at("A", i))
            tt(AL[:, 0], Am[:], copies(C_LEV), ALU.mult).then_inc(*F.sig("am0"))
            if back:
                output_variance()
            dve.wait_ge(*m_act.at("D", i))
            dve.wait_ge(*m_pe.at("S", i))
            stt(flat(Pb[:]), m0, ML_SCALE, flat(Db[:]), ALU.mult, ALU.mult).then_inc(*M.sig("P"))
            gram("Mu", Mu, g0, C_UPEQ)
            dve.wait_ge(*f_pe.at("am0T", i))
            tt(Ur[:], copies(C_ID), three(flat(g1[:])), ALU.subtract).then_inc(*F.sig("U0"))
            dve.wait_ge(*f_pe.at("B", i))
            stt(flat(qe[:]), zm[:, 0:MH, :].rearrange("p h t -> p (h t)"), ML_SCALE, flat(Eb[:]), ALU.mult,
                ALU.mult).then_inc(*M.sig("qe"))
            gram("B", Bm, g0, C_UP)
            for n in range(1, LEVELS):
                if n == 4:
                    dve.wait_ge(*m_act.at("aden", i))
                    tt(aden[:], aden[:], nmb[:], ALU.max).then_inc(*M.sig("dmax"))
                    dve.wait_ge(*M.at("dmax", i))
                    nc.vector.reciprocal(flat(aden[:]), flat(aden[:])).then_inc(*M.sig("rec"))
                    dve.wait_ge(*M.at("rec", i))
                    tt(flat(hm[:]), m1, flat(aden[:]), ALU.mult).then_inc(*M.sig("hm"))
                dve.wait_ge(*f_pe.at(f"E{n}", i))
                tt(flat(Ur[:]), flat(Ur[:]).bitcast(F32), flat(g0[:]), ALU.subtract).then_inc(*F.sig(f"U{n}"))
                if n == 1:
                    dve.wait_ge(*b_dve.at("S", j))
                    dve.wait_ge(*f_pe.at("Mv", i))
                    tt(S0s[:], St[:], Pi[:, :, 0:1].to_broadcast([P, RC, HD]), ALU.mult).then_inc(*F.sig("S0s"))
                    gram("Mv", Mv, g2, C_UPEQ)
                    if back:
                        output_norm()
                if n == 4:
                    dve.wait_ge(*m_pool.at("dec", i))
                    dve.wait_ge(*m_pe.at("dN", i))
                    tt(CN[:].rearrange("p a h t -> p (a h t)"), CN[:].rearrange("p a h t -> p (a h t)"), flat(G[3][:]),
                       ALU.add).then_inc(*M.sig("C"))
                if n == 5:
                    dve.wait_ge(*m_pe.at("mean", i))
                    stt(flat(hm[:]), m0, -1.0 / P, flat(hm[:]), ALU.mult, ALU.add).then_inc(*M.sig("yc"))
            dve.wait_ge(*m_pe.at("var", i))
            ts(flat(mve[:]), m1, 1.0 / P, ML_EPS, ALU.mult, ALU.add).then_inc(*M.sig("ve"))
            dve.wait_ge(*f_pool.at("IU", i))
            dve.wait_ge(*f_pe.at("F", i))
            tt(flat(Qr[:]), flat(Uf[:]), flat(g1[:]), ALU.subtract).then_inc(*F.sig("Q"))
            dve.wait_ge(*f_pe.at("UQ", i))
            tt(flat(Uf[:]), flat(Ur[:]).bitcast(F32), flat(g0[:]), ALU.add).then_inc(*F.sig("Uf"))
            dve.wait_ge(*m_act.at("rsv", i))
            newton(M, ("g1", "g2", "g3"), mrs, mve, mnw, i)
            tt(hm[:], hm[:], mrs[:], ALU.mult).then_inc(*M.sig("y1"))

        def mlstm_rows():
            assert c.seq == ROWS_SEQ, c.seq
            dve.wait_ge(x_in, 2 * 16)
            step(ts(grow[:], grow[:], gbias[:, 1:2], None, ALU.add))
            step(ts(ifr[:], ifr[:], gbias[:, 0:1], None, ALU.add))
            step(ts(brow[:], grow[:], 0.0, None, ALU.min))
            dve.wait_ge(act_seq, ROWS_ACT + 3)
            step(tt(brow[:], brow[:], nrow[:], ALU.subtract))
            step(nc.vector.tensor_tensor_scan(mrow[:], brow[:], ifr[:], 0.0, ALU.add, ALU.max))
            for n in range(NSEG):
                cols = slice(n * SEG, (n + 1) * SEG)
                step(nc.vector.tensor_tensor_scan(arow[:, cols], con(C_ONES, P, MH), brow[:, cols], 0.0, ALU.mult,
                                                  ALU.add))
            step(tt(grow[:], ifr[:], arow[:], ALU.subtract))
            step(tt(arow[:], arow[:], mrow[:], ALU.subtract))
            step(nc.vector.tensor_copy(erow[:, 0:SEG], arow[:, 0:SEG]))
            before = mrow[:].rearrange("p (n t) -> p n t", n=NSEG)[:, 0:NSEG - 1, SEG - 1:SEG]
            step(tt(erow[:, SEG:T].rearrange("p (n t) -> p n t", n=NSEG - 1),
                    arow[:, SEG:T].rearrange("p (n t) -> p n t", n=NSEG - 1),
                    before.to_broadcast([MH, NSEG - 1, SEG]), ALU.add))

        def split_load(hi, lo):
            with dve.Fori(0, KD // 2) as i:
                for r in range(2):
                    dve.wait_ge(*sp_act.at(f"c{r}", i + c.split))
                    tt(lo[:, i * 2 + r, :], ysg[:, r, :], hi[:, i * 2 + r, :].bitcast(F32),
                       ALU.subtract).then_inc(*sp_dve.sig(f"l{r}"))
            c.split += 4

        def merge():
            S = mg_dve
            with dve.Fori(0, KD // 2) as i:
                for r in range(2):
                    output_ready(i * 2 + (c.unit + r))
                    dve.wait_ge(sg_in[r], i * 32 + 32)
                    dve.wait_ge(*S.at(f"l{r}", i - 1))
                    banks = [bank_act(c.act + n) if r else bank_dve(c.dve + n) for n in range(2)]
                    tt(mo[:, r, :], sg[:, r, 0, :], flat(banks[0][:]), ALU.mult).then_inc(*S.sig(f"p{r}"))
                    tt(sg[:, r, 1, :], sg[:, r, 1, :], flat(banks[1][:]), ALU.mult).then_inc(*S.sig(f"q{r}"))
                    dve.wait_ge(*S.at(f"q{r}", i))
                    dve.sem_inc(act_free if r else dve_free, 2)
                    tt(mo[:, r, :], mo[:, r, :], sg[:, r, 1, :], ALU.add).then_inc(*S.sig(f"mo{r}"))
                    dve.wait_ge(*mg_act.at(f"h{r}", i))
                    tt(hlo[:, i * 2 + r, :], mo[:, r, :], hhi[:, i * 2 + r, :].bitcast(F32),
                       ALU.subtract).then_inc(*S.sig(f"l{r}"))
            c.advance(unit=KD, act=KD, dve=KD)

        def attend(i, front, back):
            S, (g0, g1, g2, g3) = xp_dve, G
            j = i - 1
            if front:
                dve.wait_ge(*xp_pe.at("S", i))
                nc.vector.reduce_max(mx[:, 0:XH], flat(g0[:]).rearrange("p (h m) -> p h m", h=XH),
                                     AX_X).then_inc(*S.sig("mx"))
                dve.wait_ge(*S.at("mx", i))
                ts(mx[:, XH:2 * XH], mx[:, 0:XH], -XA_SCALE, None, ALU.mult).then_inc(*S.sig("nmx"))
                dve.wait_ge(*xp_act.at("e", i))
                nc.vector.reciprocal(mx[:, 3 * XH:4 * XH], mx[:, 2 * XH:3 * XH]).then_inc(*S.sig("r"))
                dve.wait_ge(*S.at("r", i))
                dve.wait_ge(*xo_pe.at("T", j))
                tt(px[:], sx[:], mx[:, 3 * XH:4 * XH].unsqueeze(2).to_broadcast([P, XH, MEM]),
                   ALU.mult).then_inc(*S.sig("p"))
            if back:
                dve.wait_ge(*xo_act.at("hi", j))
                cols = bass.ds(j * SEG, SEG)
                tt(hlo[:, :, cols], flat(g2[:]).rearrange("p (k t) -> p k t", k=KD), hhi[:, :, cols].bitcast(F32),
                   ALU.subtract).then_inc(*xo_dve.sig("lo"))

        squares(nsq, nt[:])
        dve.wait_ge(consts_in, CONSTS * 16)
        for done in xc_in:
            dve.wait_ge(done, 16)
        step(ts(hw0[:], vec[:, VCOL["rw_w0"]:VCOL["rw_w0"] + 2 * RC], 0.5, None, ALU.mult))
        ffn("ffn1_norm")
        dve.wait_ge(dve_free, c.dve + credit)
        norm_x("mix_norm")
        barrier(dve, c)
        for r in range(2):
            step(nc.vector.memset(stg[:, r, 0:3], 0.0))
        project_rw()
        c.z = RW_UNITS // 2 + MH + MH // 2 * 2
        project_ml()
        mlstm_rows()
        c.advance(unit=2 * KD, act=2 * KD)
        barrier(dve, c)
        step(nc.vector.tensor_copy(idr[:].rearrange("p (n t) -> p n t", n=RC),
                                   con(C_ID).unsqueeze(1).to_broadcast([P, RC, P])))
        for m in (Am, Bm, Mv, Mu, St, dec, CN):
            step(nc.vector.memset(m[:], 0.0))
        barrier(dve, c)
        pipelined(dve, iteration)
        barrier(dve, c)
        split_load(yhi, ylo)
        merge()
        barrier(dve, c)
        dve.wait_ge(x_in, 6 * 16)
        squares(memq, memr[:, 2, :])
        residual(1.0, chunks=2)
        norm("mem_norm", memx, MEM, memr[:, 0, :], memr[:, 1, :], memr[:, 2, :], memh, memhi, memlo)
        residual(1.0, first=2, chunks=KD - 2)
        c.advance(unit=2 * KD, act=2 * KD)
        norm_x("xa_norm")
        barrier(dve, c)
        c.advance(unit=KD, act=KD)
        barrier(dve, c)
        pipelined(dve, attend)
        barrier(dve, c)
        residual(1.0)
        ffn("ffn2_norm")
        dve.wait_ge(dve_free, c.dve + credit)
        norm_x("final_norm", None)
        assert c.seq == FINAL_SEQ, c.seq
        for k in range(KD):
            x_ = xT[:, k, :]
            stt(x_, x_, v1("final_norm", k), nr[:], ALU.mult, ALU.mult).then_inc(dve_seq, 1)

    ctx.close()


def constants():
    c = np.zeros((P, NCONST), np.float32)
    p, f = np.arange(P)[:, None], np.arange(P)[None, :]
    c[:, C_ID:C_ID + P] = p == f
    c[:, C_ONES:C_ONES + P] = 1
    c[:, C_HONES:C_HONES + P] = p // HD == f // HD
    c[:, C_LOW:C_LOW + P] = f < p
    c[:, C_UP:C_UP + P] = p < f
    c[:, C_UPEQ:C_UPEQ + P] = p <= f
    for n in range(LEVELS):
        b = 1 << n
        c[:, C_LEV + n * P:C_LEV + (n + 1) * P] = (p // (2 * b) == f // (2 * b)) & (p // b % 2 == 1) & (f // b % 2 == 0)
    c[:, C_ADD:C_ADD + P] = np.where(p <= f, 0.0, -1e30)
    c[:, C_RST:C_RST + RC * DEC] = np.arange(RC * DEC) % DEC != 0
    for h in range(MH):
        c[h, C_SEL + h * P:C_SEL + (h + 1) * P] = 1
    c[:, C_RSC] = 10 * np.log(2.0)
    return c


def kernel(**inputs):
    import concourse.bacc as bacc
    from concourse.bass_utils import run_bass_kernel_spmd

    g = {k: np.asarray(v) for k, v in inputs.items()}

    def units(w):
        k, n = w.shape[0] // P, w.shape[1] // P
        return np.ascontiguousarray(w.reshape(k, P, n, P).transpose(2, 1, 0, 3).reshape(n, P, k * P))

    def cols(v):
        return v.reshape(-1, P).T

    arrays = {}
    for f in ("ffn1", "ffn2"):
        n = f[-1]
        arrays[f"wg{n}"] = units(g[f"{f}_w_gate"][0])
        arrays[f"wu{n}"] = units(g[f"{f}_w_up"][0])
        at = 0
        for part, c in enumerate(FF_PARTS):
            arrays[f"wd{n}_{part}"] = units(g[f"{f}_w_down"][0][at * P:(at + c) * P])
            at += c
    w_in = g["w_in"][0]
    rw, mlc = RW_UNITS * P, ML_UNITS * P
    arrays["rw_in"] = units(w_in[:, :rw])
    arrays["ml_in"] = units(w_in[:, rw:rw + mlc])
    wif = np.zeros((D, P), np.float32)
    wif[:, :2 * MH] = w_in[:, rw + mlc:rw + mlc + 2 * MH]
    arrays["if_in"] = units(wif)
    gates = rw + mlc + 2 * MH
    arrays["ga_in"] = units(w_in[:, gates:gates + D])
    arrays["gb_in"] = units(w_in[:, gates + D:])
    arrays["up"] = units(np.concatenate([g["w_up_rw"][0], g["w_up_ml"][0]], axis=0))
    arrays["w_out"] = units(g["w_out"][0])
    arrays["wq"] = units(g["xa_wq"][0])
    arrays["wkv"] = units(g["xa_wkv"][0])
    arrays["wo"] = units(g["xa_wo"][0])
    arrays["lora_wa"] = np.concatenate([g["rw_w2"][0], g["rw_a2"][0]], axis=0)
    arrays["lora_g"] = np.ascontiguousarray(g["rw_g2"][0])
    arrays["x"] = np.ascontiguousarray(g["x"][0].T.reshape(KD, P, T).transpose(1, 0, 2))
    arrays["mem"] = np.ascontiguousarray(g["mem"][0].T.reshape(KD, P, MEM).transpose(1, 0, 2))
    vecs = {n: g[n] if n == "final_norm" else g[n][0] for n, _ in VECS if n in g}
    for j in range(4):
        vecs[f"conv_w{j}"] = g["ml_conv_w"][0, j]
    vecs["conv_b"] = g["ml_conv_b"][0]
    arrays["vecs"] = np.ascontiguousarray(np.concatenate([cols(vecs[n].reshape(-1)) for n, _ in VECS], axis=1))
    arrays["gate_b"] = np.ascontiguousarray(np.stack([g["ml_i_b"][0], g["ml_f_b"][0]], axis=1))
    arrays["consts"] = constants()

    nc = bacc.Bacc("TRN2", target_bir_lowering=False, num_devices=1)
    aps = {n: nc.dram_tensor(f"in_{n}", v.shape, F32, kind="ExternalInput").ap() for n, v in arrays.items()}
    out = nc.dram_tensor("out", [KD, P, T], F32, kind="ExternalOutput").ap()
    layer_kernel(nc, aps, out)
    res = run_bass_kernel_spmd(nc, [{f"in_{n}": v for n, v in arrays.items()}], core_ids=[0])
    return res.results[0]["out"].reshape(D, T).T.reshape(1, T, D)
```
